# Optimizing a Trainium2 kernel written in Bass

```python
import math
import jax, jax.numpy as jnp
from jax import lax
import numpy as np

D_MODEL = 1024
BATCH = 1
SEQ = 256
DEPTH = 2

N_MIXERS = 2
N_HEADS = 8
HEAD_DIM = D_MODEL // N_HEADS
DIFF_HALF = HEAD_DIM // 2
MOBA_BLOCK = 256
MOBA_TOPK = 3
Q_BLOCK = 128
D_FF = -(-8 * D_MODEL // (3 * 256)) * 256
N_BUCKETS = 32
MAX_EXACT = N_BUCKETS // 2
MAX_DISTANCE = 2048
N_MOBA_LAYERS = (DEPTH + 1) // 2
N_DIFF_LAYERS = DEPTH // 2
RMS_EPS = 1e-6
NEG_INF = -1e30


def rms_norm(x, g):
    x32 = x.astype(jnp.float32)
    y = x32 * lax.rsqrt(jnp.mean(x32 * x32, axis=-1, keepdims=True) + RMS_EPS)
    return (y * g.astype(jnp.float32)).astype(x.dtype)

def t5_bucket(rel):
    n = jnp.maximum(rel, 0)
    nf = jnp.maximum(n, 1).astype(jnp.float32)
    large = MAX_EXACT + (jnp.log(nf / MAX_EXACT) / math.log(MAX_DISTANCE / MAX_EXACT)
                         * (N_BUCKETS - MAX_EXACT)).astype(jnp.int32)
    large = jnp.minimum(large, N_BUCKETS - 1)
    return jnp.where(n < MAX_EXACT, n, large)

def moba_attention(h, w_qkv, w_o, rel_table):
    B, S, _ = h.shape
    pad = (-S) % MOBA_BLOCK
    s_pad = S + pad
    nb = s_pad // MOBA_BLOCK
    nq = s_pad // Q_BLOCK
    k_sel_n = min(MOBA_TOPK, nb)
    q, k, v = jnp.split(h @ w_qkv, 3, axis=-1)

    def heads(t):
        t = t.reshape(B, S, N_HEADS, HEAD_DIM).transpose(0, 2, 1, 3)
        return jnp.pad(t, ((0, 0), (0, 0), (0, pad), (0, 0)))

    q = heads(q) * (HEAD_DIM ** -0.5)
    k, v = heads(k), heads(v)
    k_blk = k.reshape(B, N_HEADS, nb, MOBA_BLOCK, HEAD_DIM)
    v_blk = v.reshape(B, N_HEADS, nb, MOBA_BLOCK, HEAD_DIM)
    k_mean = jnp.mean(k_blk, axis=3)
    q_blocks = q.reshape(B, N_HEADS, nq, Q_BLOCK, HEAD_DIM).transpose(2, 0, 1, 3, 4)
    b_idx = jnp.arange(B)[:, None, None, None]
    h_idx = jnp.arange(N_HEADS)[None, :, None, None]
    table_t = rel_table.T

    def one_block(args):
        qb, qi = args
        q_pos = qi * Q_BLOCK + jnp.arange(Q_BLOCK)
        own = qi // (MOBA_BLOCK // Q_BLOCK)
        gate = jnp.einsum('bhqd,bhnd->bhqn', qb, k_mean).astype(jnp.float32)
        gate = jnp.where(jnp.arange(nb) < own, gate, NEG_INF)
        _, sel = lax.top_k(gate, k_sel_n)
        slot_valid = jnp.repeat(jnp.arange(k_sel_n) < own, MOBA_BLOCK)
        k_sel = k_blk[b_idx, h_idx, sel].reshape(B, N_HEADS, Q_BLOCK, k_sel_n * MOBA_BLOCK, HEAD_DIM)
        v_sel = v_blk[b_idx, h_idx, sel].reshape(B, N_HEADS, Q_BLOCK, k_sel_n * MOBA_BLOCK, HEAD_DIM)
        k_pos_sel = (sel[..., None] * MOBA_BLOCK + jnp.arange(MOBA_BLOCK)).reshape(
            B, N_HEADS, Q_BLOCK, k_sel_n * MOBA_BLOCK)
        bias_sel = table_t[h_idx, t5_bucket(q_pos[None, None, :, None] - k_pos_sel)]
        s_sel = jnp.einsum('bhqd,bhqkd->bhqk', qb, k_sel).astype(jnp.float32) + bias_sel.astype(jnp.float32)
        s_sel = jnp.where(slot_valid, s_sel, NEG_INF)
        k_own = lax.dynamic_slice_in_dim(k, own * MOBA_BLOCK, MOBA_BLOCK, axis=2)
        v_own = lax.dynamic_slice_in_dim(v, own * MOBA_BLOCK, MOBA_BLOCK, axis=2)
        k_pos_own = own * MOBA_BLOCK + jnp.arange(MOBA_BLOCK)
        rel_own = q_pos[:, None] - k_pos_own[None, :]
        bias_own = jnp.moveaxis(rel_table[t5_bucket(rel_own)], -1, 0)
        s_own = jnp.einsum('bhqd,bhkd->bhqk', qb, k_own).astype(jnp.float32) + bias_own[None].astype(jnp.float32)
        s_own = jnp.where(rel_own >= 0, s_own, NEG_INF)
        p = jax.nn.softmax(jnp.concatenate([s_sel, s_own], axis=-1), axis=-1).astype(v.dtype)
        n_sel = k_sel_n * MOBA_BLOCK
        return (jnp.einsum('bhqk,bhqkd->bhqd', p[..., :n_sel], v_sel)
                + jnp.einsum('bhqk,bhkd->bhqd', p[..., n_sel:], v_own))

    o = lax.map(one_block, (q_blocks, jnp.arange(nq)))
    o = o.transpose(1, 0, 3, 2, 4).reshape(B, s_pad, D_MODEL)[:, :S]
    return o @ w_o

def diff_attention(h, w_qkv, w_o, lam, subln_g, rel_table, layer_idx):
    B, S, _ = h.shape
    nq = S // Q_BLOCK
    lambda_init = 0.8 - 0.6 * math.exp(-0.3 * layer_idx)
    q, k, v = jnp.split(h @ w_qkv, 3, axis=-1)
    q = q.reshape(B, S, N_HEADS, 2, DIFF_HALF).transpose(0, 2, 3, 1, 4) * (DIFF_HALF ** -0.5)
    k = k.reshape(B, S, N_HEADS, 2, DIFF_HALF).transpose(0, 2, 3, 1, 4)
    v = v.reshape(B, S, N_HEADS, HEAD_DIM).transpose(0, 2, 1, 3)
    lam32 = lam.astype(jnp.float32)
    lam_full = (jnp.exp(jnp.sum(lam32[0] * lam32[1])) - jnp.exp(jnp.sum(lam32[2] * lam32[3]))
                + lambda_init)
    q_blocks = q.reshape(B, N_HEADS, 2, nq, Q_BLOCK, DIFF_HALF).transpose(3, 0, 1, 2, 4, 5)
    k_pos = jnp.arange(S)

    def one_block(args):
        qb, qi = args
        q_pos = qi * Q_BLOCK + jnp.arange(Q_BLOCK)
        rel = q_pos[:, None] - k_pos[None, :]
        bias = jnp.moveaxis(rel_table[t5_bucket(rel)], -1, 0)
        s = jnp.einsum('bhcqd,bhckd->bhcqk', qb, k).astype(jnp.float32) + bias[None, :, None].astype(jnp.float32)
        s = jnp.where(rel >= 0, s, NEG_INF)
        p = jax.nn.softmax(s, axis=-1)
        a = p[:, :, 0] - lam_full * p[:, :, 1]
        return jnp.einsum('bhqk,bhkd->bhqd', a.astype(v.dtype), v)

    o = lax.map(one_block, (q_blocks, jnp.arange(nq)))
    o = o.transpose(1, 2, 0, 3, 4).reshape(B, N_HEADS, S, HEAD_DIM)
    o = rms_norm(o, subln_g) * (1.0 - lambda_init)
    o = o.transpose(0, 2, 1, 3).reshape(B, S, D_MODEL)
    return o @ w_o

def swiglu(h, w_in, w_out):
    g, u = jnp.split(h @ w_in, 2, axis=-1)
    return (jax.nn.silu(g) * u) @ w_out

def first_inputs(seed: int = 0) -> dict:
    key = jax.random.key(seed)
    ks = jax.random.split(key, 16)
    f32 = jnp.float32
    D = D_MODEL
    return {
        "x": jax.random.normal(ks[0], (BATCH, SEQ, D), f32),
        "c": jax.random.normal(ks[1], (BATCH, D), f32),
        "rel_bias": 0.5 * jax.random.normal(ks[2], (N_BUCKETS, N_HEADS), f32),
        "ada_w": jax.random.normal(ks[3], (DEPTH, D, 6 * D), f32) * D ** -0.5,
        "ada_b": 0.01 * jax.random.normal(ks[4], (DEPTH, 6 * D), f32),
        "norm_g": 1.0 + 0.1 * jax.random.normal(ks[5], (DEPTH, 4, D), f32),
        "moba_w_qkv": jax.random.normal(ks[6], (N_MOBA_LAYERS, D, 3 * D), f32) * D ** -0.5,
        "moba_w_o": jax.random.normal(ks[7], (N_MOBA_LAYERS, D, D), f32) * D ** -0.5,
        "diff_w_qkv": jax.random.normal(ks[8], (N_DIFF_LAYERS, D, 3 * D), f32) * D ** -0.5,
        "diff_w_o": jax.random.normal(ks[9], (N_DIFF_LAYERS, D, D), f32) * D ** -0.5,
        "diff_lambda": 0.1 * jax.random.normal(ks[10], (N_DIFF_LAYERS, 4, DIFF_HALF), f32),
        "diff_subln_g": 1.0 + 0.1 * jax.random.normal(ks[11], (N_DIFF_LAYERS, HEAD_DIM), f32),
        "ffn_w_in": jax.random.normal(ks[12], (DEPTH, D, 2 * D_FF), f32) * D ** -0.5,
        "ffn_w_out": jax.random.normal(ks[13], (DEPTH, D_FF, D), f32) * D_FF ** -0.5,
    }

def first_block(x, c, rel_bias, ada_w, ada_b, norm_g, moba_w_qkv, moba_w_o, diff_w_qkv, diff_w_o,
              diff_lambda, diff_subln_g, ffn_w_in, ffn_w_out):
    c_act = jax.nn.silu(c)
    for i in range(DEPTH):
        mod = (c_act @ ada_w[i] + ada_b[i])[:, None, :]
        sh_a, sc_a, g_a, sh_f, sc_f, g_f = jnp.split(mod, 6, axis=-1)
        h = rms_norm(x, norm_g[i, 0]) * (1.0 + sc_a) + sh_a
        if i % N_MIXERS == 0:
            y = moba_attention(h, moba_w_qkv[i // 2], moba_w_o[i // 2], rel_bias)
        else:
            y = diff_attention(h, diff_w_qkv[i // 2], diff_w_o[i // 2], diff_lambda[i // 2],
                               diff_subln_g[i // 2], rel_bias, i)
        x = x + g_a * rms_norm(y, norm_g[i, 1])
        h = rms_norm(x, norm_g[i, 2]) * (1.0 + sc_f) + sh_f
        x = x + g_f * rms_norm(swiglu(h, ffn_w_in[i], ffn_w_out[i]), norm_g[i, 3])
    return x


DEPTH_2 = 1

N_MIXERS_2 = 3
CONF_CONV_WIDTH = 31
POOL_WINDOWS = (2, 4, 8, 16)
POOL_GROUPS = len(POOL_WINDOWS)
POOL_GROUP_DIM = D_MODEL // POOL_GROUPS
SHORT_CONV_WIDTH = 3
FFN_CONV_WIDTH = 3
D_FF_2 = 2816
LN_EPS = 1e-5
N_A = (DEPTH_2 + N_MIXERS_2 - 1) // N_MIXERS_2
N_B = (DEPTH_2 + N_MIXERS_2 - 2) // N_MIXERS_2
N_C = (DEPTH_2 + N_MIXERS_2 - 3) // N_MIXERS_2


def rmsnorm(x, g):
    x32 = x.astype(jnp.float32)
    y = x32 * lax.rsqrt(jnp.mean(x32 * x32, axis=-1, keepdims=True) + RMS_EPS)
    return y.astype(x.dtype) * g

def layernorm(x, g, b):
    x32 = x.astype(jnp.float32)
    mu = jnp.mean(x32, axis=-1, keepdims=True)
    var = jnp.mean(jnp.square(x32 - mu), axis=-1, keepdims=True)
    y = (x32 - mu) * lax.rsqrt(var + LN_EPS)
    return y.astype(x.dtype) * g + b

def causal_dwconv(x, w):
    k, ch = w.shape
    return lax.conv_general_dilated(
        x, w[:, None, :].astype(x.dtype), window_strides=(1,), padding=[(k - 1, 0)],
        dimension_numbers=("NWC", "WIO", "NWC"), feature_group_count=ch)

def conformer_conv_module(h, w1, b1, dw_w, dw_b, ln_g, ln_b, w2, b2):
    u = h @ w1 + b1
    a, gt = jnp.split(u, 2, axis=-1)
    u = a * jax.nn.sigmoid(gt)
    u = causal_dwconv(u, dw_w) + dw_b
    u = jax.nn.silu(layernorm(u, ln_g, ln_b))
    return u @ w2 + b2

def pooling_mixer(h, group_w, group_b, ch_scale):
    bsz, t_len, d = h.shape
    h32 = h.astype(jnp.float32)
    cs = jnp.cumsum(h32, axis=1)
    pos = jnp.arange(1, t_len + 1, dtype=jnp.float32)[None, :, None]
    means = []
    for g, w in enumerate(POOL_WINDOWS):
        csg = cs[..., g * POOL_GROUP_DIM:(g + 1) * POOL_GROUP_DIM]
        prev = jnp.pad(csg, ((0, 0), (w, 0), (0, 0)))[:, :t_len]
        means.append((csg - prev) / jnp.minimum(pos, float(w)))
    pooled = (jnp.concatenate(means, axis=-1) - h32).astype(h.dtype)
    pooled = pooled.reshape(bsz, t_len, POOL_GROUPS, POOL_GROUP_DIM)
    mixed = jnp.einsum("btgc,gcd->btgd", pooled, group_w).reshape(bsz, t_len, d)
    return (mixed + group_b) * ch_scale

def short_conv_mixer(h, w_in, w_conv, w_out):
    bcx = h @ w_in
    gb, gc, v = jnp.split(bcx, 3, axis=-1)
    return (gb * causal_dwconv(gc * v, w_conv)) @ w_out

def conv_ffn(h, w_up, dw_w, dw_b, w_down):
    u = causal_dwconv(h @ w_up, dw_w) + dw_b
    gt, v = jnp.split(u, 2, axis=-1)
    return (jax.nn.silu(gt) * v) @ w_down

def second_inputs(seed: int = 0) -> dict:
    key = jax.random.key(seed)
    ks = iter(jax.random.split(key, 40))
    d, f = D_MODEL, D_FF_2

    def nrm(shape, scale):
        return scale * jax.random.normal(next(ks), shape, jnp.float32)

    def gain(shape):
        return 1.0 + nrm(shape, 0.05)

    return {
        "x": nrm((BATCH, SEQ, d), 1.0),
        "c": nrm((BATCH, d), 1.0),
        "mod_w": nrm((DEPTH_2, d, 6 * d), 0.5 * d ** -0.5),
        "mod_b": nrm((DEPTH_2, 6 * d), 0.02),
        "norm_pre_mix": gain((DEPTH_2, d)),
        "norm_post_mix": gain((DEPTH_2, d)),
        "norm_pre_ffn": gain((DEPTH_2, d)),
        "norm_post_ffn": gain((DEPTH_2, d)),
        "a_pw1_w": nrm((N_A, d, 2 * d), d ** -0.5),
        "a_pw1_b": nrm((N_A, 2 * d), 0.02),
        "a_dw_w": nrm((N_A, CONF_CONV_WIDTH, d), CONF_CONV_WIDTH ** -0.5),
        "a_dw_b": nrm((N_A, d), 0.02),
        "a_ln_g": gain((N_A, d)),
        "a_ln_b": nrm((N_A, d), 0.02),
        "a_pw2_w": nrm((N_A, d, d), d ** -0.5),
        "a_pw2_b": nrm((N_A, d), 0.02),
        "b_group_w": nrm((N_B, POOL_GROUPS, POOL_GROUP_DIM, POOL_GROUP_DIM), POOL_GROUP_DIM ** -0.5),
        "b_group_b": nrm((N_B, d), 0.02),
        "b_scale": gain((N_B, d)),
        "c_in_w": nrm((N_C, d, 3 * d), d ** -0.5),
        "c_conv_w": nrm((N_C, SHORT_CONV_WIDTH, d), SHORT_CONV_WIDTH ** -0.5),
        "c_out_w": nrm((N_C, d, d), d ** -0.5),
        "f_up_w": nrm((DEPTH_2, d, 2 * f), d ** -0.5),
        "f_dw_w": nrm((DEPTH_2, FFN_CONV_WIDTH, 2 * f), FFN_CONV_WIDTH ** -0.5),
        "f_dw_b": nrm((DEPTH_2, 2 * f), 0.02),
        "f_down_w": nrm((DEPTH_2, f, d), f ** -0.5),
    }

def second_block(x, c, mod_w, mod_b, norm_pre_mix, norm_post_mix, norm_pre_ffn, norm_post_ffn,
              a_pw1_w, a_pw1_b, a_dw_w, a_dw_b, a_ln_g, a_ln_b, a_pw2_w, a_pw2_b,
              b_group_w, b_group_b, b_scale,
              c_in_w, c_conv_w, c_out_w,
              f_up_w, f_dw_w, f_dw_b, f_down_w):
    c_act = jax.nn.silu(c)
    for i in range(DEPTH_2):
        mod = c_act @ mod_w[i] + mod_b[i]
        sh_m, sc_m, gt_m, sh_f, sc_f, gt_f = [m[:, None, :] for m in jnp.split(mod, 6, axis=-1)]

        h = rmsnorm(x, norm_pre_mix[i]) * (1.0 + sc_m) + sh_m
        kind, slot = i % N_MIXERS_2, i // N_MIXERS_2
        if kind == 0:
            y = conformer_conv_module(h, a_pw1_w[slot], a_pw1_b[slot], a_dw_w[slot], a_dw_b[slot],
                                      a_ln_g[slot], a_ln_b[slot], a_pw2_w[slot], a_pw2_b[slot])
        elif kind == 1:
            y = pooling_mixer(h, b_group_w[slot], b_group_b[slot], b_scale[slot])
        else:
            y = short_conv_mixer(h, c_in_w[slot], c_conv_w[slot], c_out_w[slot])
        x = x + gt_m * rmsnorm(y, norm_post_mix[i])

        h = rmsnorm(x, norm_pre_ffn[i]) * (1.0 + sc_f) + sh_f
        y = conv_ffn(h, f_up_w[i], f_dw_w[i], f_dw_b[i], f_down_w[i])
        x = x + gt_f * rmsnorm(y, norm_post_ffn[i])
    return x


def setup_inputs(seed=0):
    out = dict(first_inputs(seed))
    for name, value in second_inputs(seed + 1).items():
        if name != "x":
            out[name + "_2"] = value
    return out


def reference(
    x, c, rel_bias, ada_w, ada_b, norm_g, moba_w_qkv, moba_w_o, diff_w_qkv, diff_w_o,
    diff_lambda, diff_subln_g, ffn_w_in, ffn_w_out, c_2, mod_w_2, mod_b_2, norm_pre_mix_2,
    norm_post_mix_2, norm_pre_ffn_2, norm_post_ffn_2, a_pw1_w_2, a_pw1_b_2, a_dw_w_2, a_dw_b_2,
    a_ln_g_2, a_ln_b_2, a_pw2_w_2, a_pw2_b_2, b_group_w_2, b_group_b_2, b_scale_2, c_in_w_2,
    c_conv_w_2, c_out_w_2, f_up_w_2, f_dw_w_2, f_dw_b_2, f_down_w_2,
):
    x = first_block(
        x, c, rel_bias, ada_w, ada_b, norm_g, moba_w_qkv, moba_w_o, diff_w_qkv, diff_w_o,
        diff_lambda, diff_subln_g, ffn_w_in, ffn_w_out,
    )
    return second_block(
        x, c_2, mod_w_2, mod_b_2, norm_pre_mix_2, norm_post_mix_2, norm_pre_ffn_2,
        norm_post_ffn_2, a_pw1_w_2, a_pw1_b_2, a_dw_w_2, a_dw_b_2, a_ln_g_2, a_ln_b_2,
        a_pw2_w_2, a_pw2_b_2, b_group_w_2, b_group_b_2, b_scale_2, c_in_w_2, c_conv_w_2,
        c_out_w_2, f_up_w_2, f_dw_w_2, f_dw_b_2, f_down_w_2,
    )


_drawn_inputs = setup_inputs


def setup_inputs(seed=0):
    import zlib

    import numpy as np

    out = dict(_drawn_inputs(seed))
    spreads = {}
    factors = {'mod_b_2': 2.814,
     'norm_pre_mix_2': 5.671,
     'norm_post_mix_2': 6.04,
     'norm_pre_ffn_2': 4.676,
     'norm_post_ffn_2': 6.213,
     'a_pw1_b_2': 8.0,
     'a_dw_b_2': 7.641,
     'a_ln_g_2': 5.156,
     'a_ln_b_2': 8.0,
     'a_pw2_b_2': 8.0,
     'f_dw_b_2': 8.0}
    for name, (base, spread) in spreads.items():
        noise = np.random.default_rng([zlib.crc32(name.encode()), seed]).standard_normal(out[name].shape)
        drawn = base * np.exp(spread * noise) if base else spread * noise
        out[name] = __import__('jax').numpy.asarray(drawn.astype(out[name].dtype))
    for name, factor in factors.items():
        out[name] = (out[name] * factor).astype(out[name].dtype)
    return out
```

```python
from contextlib import ExitStack

import concourse.bass as bass
from concourse import mybir

F32 = mybir.dt.float32
F32R = mybir.dt.float32r
ALU = mybir.AluOpType
ACT = mybir.ActivationFunctionType
AX = mybir.AxisListType

P = 128
S = 256
D = 1024
H = 8
KT = D // P
TT = S // P
FT = 22
FF = FT * P
CONV = 31
EPS, LN_EPS = 1e-6, 1e-5
LAMBDA_INIT = 0.8 - 0.6 * 0.7408182206817179
REL = 384
BLK = 512
NBLK = 6 * D // BLK
PADW = S + CONV - 1
LAST = 5

NORM, PW1B, DWB, LNG, LNB, SUB = 0, 48, 64, 72, 80, 88
FDW, ADW = 89, 89 + 8 * FT
COLS = ADW + CONV * KT
PAR_ROWS = (16, 89, 4 * FT, 4 * FT, 16 * KT, 15 * KT)

USE = {0: (0, 0, 0, 0), 1: (4, 4, 4, 4), 2: (15, 15, 15, 4), 3: (19, 19, 19, 8),
       4: (30, 30, 30, 8), 5: (34, 34, 32, 10)}
ROWS = {0: 0, 1: 8, 2: 30, 3: 38, 5: 60}
STEPS = {1: 0, 3: 22, 4: 44, 5: 52}
HEADS = {0: 0, 2: 8}
NI_A, NI_F, NI_C = H // 2, FT // 2, KT // 2


def build(nc, x, c, rel_bias, ada_w, ada_b, norm_g, moba_w_qkv, moba_w_o, diff_w_qkv, diff_w_o,
          diff_lambda, diff_subln_g, ffn_w_in, ffn_w_out, c_2, mod_w_2, mod_b_2, norm_pre_mix_2,
          norm_post_mix_2, norm_pre_ffn_2, norm_post_ffn_2, a_pw1_w_2, a_pw1_b_2, a_dw_w_2, a_dw_b_2,
          a_ln_g_2, a_ln_b_2, a_pw2_w_2, a_pw2_b_2, f_up_w_2, f_dw_w_2, f_dw_b_2, f_down_w_2,
          bucket_onehot, causal_fill, out):
    with ExitStack() as ctx:
        def sb(name, shape, dt=F32):
            return ctx.enter_context(nc.sbuf_tensor(name, shape, dt))

        def sem(name):
            return ctx.enter_context(nc.semaphore(name))

        rel_rows = nc.dram_tensor("rel_rows", (H, P, REL), F32, kind="Internal").ap()

        raw = sb("raw", [P, 8, D])
        whi = sb("whi", [P, 8, D], F32R)
        wlo = sb("wlo", [P, 8, D], F32R)
        ada_raw = sb("ada_raw", [P, 2, 4, BLK])
        acc = sb("acc", [P, 6 * D])
        xt = sb("xt", [P, TT, D])
        xs = sb("xs", [P, TT, D])
        h_hi = sb("h_hi", [P, KT, S], F32R)
        h_lo = sb("h_lo", [P, KT, S], F32R)
        head_bias = sb("head_bias", [P, H, REL])
        Ga = sb("Ga", [P, D])
        Gf = sb("Gf", [P, D])
        a_hi = sb("a_hi", [P, 2, S], F32R)
        a_lo = sb("a_lo", [P, 2, S], F32R)
        mix = sb("mix", [P, 2688])
        cols = sb("cols", [P, COLS])
        csil = sb("csil", [P, 16])
        colA = sb("colA", [P, KT])
        colB = sb("colB", [P, KT])
        taps = sb("taps", [P, 2, 36])
        ident = sb("ident", [P, P])
        ones = sb("ones", [P, P])
        small = sb("small", [P, 96])
        relt = sb("relt", [32, H])
        Y = ctx.enter_context(nc.psum_tensor("Y", [P, 4, 512], F32))
        work = ctx.enter_context(nc.psum_tensor("work", [P, 4, 512], F32))

        qk = mix[:, 0:512]
        vv = mix[:, 512:1024].rearrange("p (t n) -> p t n", t=TT)
        pr = mix[:, 1024:1792].rearrange("p (c n) -> p c n", c=2)
        pT = mix[:, 1792:2176]
        oraw = mix[:, 2176:2432]
        osc = mix[:, 2432:2688]
        lam_in, lam_pr = oraw, osc[:, 0:128]
        gate_of = {n: mix[:, at:at + 2 * S].rearrange("p (j n) -> p j n", j=2)
                   for n, at in ((1, 0), (3, 0), (5, 0), (4, 2176))}
        act32 = mix[:, 512:512 + 2 * S].rearrange("p (j n) -> p j n", j=2)
        upad = mix[:, 0:2 * PADW].rearrange("p (j n) -> p j n", j=2)
        cacc = mix[:, 576:576 + 2 * S].rearrange("p (j n) -> p j n", j=2)
        b2row = mix[:, 1152:1152 + D]
        convT = head_bias[:, :, 0:S]
        prow = xs[:, 0, 0:6 * P].rearrange("p (g n) -> p g n", g=6)
        onehot = xs[0:32, 1, 0:REL]
        relrow = xs[0:H, 1, REL:2 * REL]
        par_bank = [Y[:, 3, :], work[:, 0, :], work[:, 1, :], work[:, 2, :], Y[:, 1, :], Y[:, 2, :]]
        ssx, msx, rsx = small[:, 0:2], small[:, 2:4], small[:, 4:6]
        ssy, msy, rsy = small[:, 6:8], small[:, 8:10], small[:, 10:12]
        mhalf, eps2 = small[:, 12:13], small[:, 13:14]
        mmax, mneg = small[:, 14:18], small[:, 18:22]
        msum, mrec = small[:, 22:26], small[:, 26:30]
        lrec = small[:, 30:32]
        sso, mso, rso = small[:, 32:34], small[:, 34:36], small[:, 36:38]
        subg = small[:, 38:39]
        lamv, lame, lamf = small[:, 40:42], small[:, 42:44], small[:, 44:46]
        bnst, bnag = small[:, 48:72], small[:, 72:76]
        lnm, lnr = small[:, 76:78], small[:, 78:80]

        ld = [sem(f"unit_loaded{u}") for u in range(8)]
        hi = [sem(f"unit_hi{u}") for u in range(8)]
        lo = [sem(f"unit_lo{u}") for u in range(8)]
        used = [sem(f"unit_multiplied{u}") for u in range(8)]
        ada_ld = [sem(f"ada_loaded{k}") for k in range(2)]
        gemv = sem("gemv_steps")
        acc_zero, acc_bias = sem("acc_zero"), sem("acc_bias")
        c_loaded, par_loaded, x_loaded = sem("c_loaded"), sem("par_loaded"), sem("x_loaded")
        rel_loaded, rel_mm, rel_row = sem("rel_loaded"), sem("rel_mm"), sem("rel_row")
        rel_stored, bias_loaded = sem("rel_stored"), sem("bias_loaded")
        lam_loaded, lam_seq, lam_exp = sem("lam_loaded"), sem("lam_seq"), sem("lam_exp")
        b2_loaded, gain_loaded = sem("b2_loaded"), sem("gain_loaded")
        id_zero, consts = sem("id_zero"), sem("consts")
        par_T, cols_ready, csil_ready = sem("par_T"), sem("cols_ready"), sem("csil_ready")
        ssx_done, msx_done, rsx_done = sem("ssx_done"), sem("msx_done"), sem("rsx_done")
        ssy_done, msy_done, rsy_done = sem("ssy_done"), sem("msy_done"), sem("rsy_done")
        xs0, xs1 = sem("xs0_ready"), sem("xs1_ready")
        hT, h32v, h32a, hhi, hlo = sem("hT"), sem("h32v"), sem("h32a"), sem("h_hi_done"), sem("h_lo_done")
        x_ready, y0_done, y_tmp, yb = sem("x_ready"), sem("y0_done"), sem("y_tmp"), sem("y_biased")
        mod_cols, mod_cols_used = sem("mod_cols"), sem("mod_cols_used")
        mod_ga, mod_gf = sem("mod_ga"), sem("mod_gf")
        mod_ga_used, mod_gf_used = sem("mod_ga_used"), sem("mod_gf_used")
        gate_done, act_done = sem("gate_done"), sem("act_done")
        ahi, alo = sem("a_hi_done"), sem("a_lo_done")
        taps_ready = sem("taps_ready")
        cv_g0, cv_g, cv_u, cv_seq = sem("cv_g0"), sem("cv_g"), sem("cv_u"), sem("cv_seq")
        qk_ev, s_mm, sb_done, mx_done = sem("qk_ev"), sem("s_mm"), sem("sb_done"), sem("mx_done")
        ng_done, ex_done, rc_done = sem("ng_done"), sem("ex_done"), sem("rc_done")
        p_done, pT_mm, pT_ev = sem("p_done"), sem("pT_mm"), sem("pT_ev")
        pv_mm, v_ev = sem("pv_mm"), sem("v_ev")
        ocp, oss, oms, ors = sem("ocp"), sem("oss"), sem("oms"), sem("ors")
        osn, oT_mm, dif_seq = sem("osn"), sem("oT_mm"), sem("dif_seq")
        pad_zero, tap_seq, conv_done = sem("pad_zero"), sem("tap_seq"), sem("conv_done")
        cT_mm, bn_done, ag_done = sem("cT_mm"), sem("bn_done"), sem("ag_done")
        lv_done, lr_done, z_done = sem("lv_done"), sem("lr_done"), sem("z_done")
        zT_mm, ln_act, p_hi, p_lo = sem("zT_mm"), sem("ln_act"), sem("p_hi"), sem("p_lo")
        stored = sem("stored")

        block = ctx.enter_context(nc.Block())

        def need(eng, s, v):
            if not (isinstance(v, int) and v <= 0):
                eng.wait_ge(s, v)

        def sweep(eng, peel, n, s, body):
            for i in range(peel):
                body(i, True)
            end = n - 1 if s == LAST else n
            if end - peel > 1:
                with eng.Fori(peel, end) as i:
                    body(i, True)
            elif end > peel:
                body(peel, True)
            if s == LAST:
                body(n - 1, False)

        qkv_w = {0: moba_w_qkv, 2: diff_w_qkv}
        o_w = {0: moba_w_o, 2: diff_w_o}
        in_w = {1: ffn_w_in[0], 3: ffn_w_in[1], 5: f_up_w_2[0]}
        out_w = {1: ffn_w_out[0], 3: ffn_w_out[1], 5: f_down_w_2[0]}
        ada = [ada_w[0], ada_w[1], mod_w_2[0]]
        scale_of = {0: P ** -0.5, 2: (P // 2) ** -0.5}

        @block.sync
        def _(sp):
            def load(u, n, src):
                need(sp, hi[u], n)
                need(sp, lo[u], n)
                dst = raw[:, u, :]
                if len(src.shape) == 3:
                    dst = dst.rearrange("p (k n) -> p k n", k=KT)
                sp.dma_start(dst, src).then_inc(ld[u], 16)

            def col_unit(w, at):
                return w[:, bass.ds(at, P)].rearrange("(k p) n -> p k n", p=P)

            def row_unit(w, at):
                return w[bass.ds(at, P), :]

            def pair(s, p, i):
                for j in range(2):
                    at = i * (2 * P) + j * P
                    if s in (0, 2):
                        src = col_unit(qkv_w[s][0], at + p * D) if p < 3 else row_unit(o_w[s][0], at)
                    elif s == 4:
                        src = col_unit(a_pw1_w_2[0], at + p * D)
                    else:
                        src = col_unit(in_w[s], at + p * FF) if p < 2 else row_unit(out_w[s], at)
                    load(2 * p + j, i + USE[s][p], src)

            def pw2_pair(r, p, n):
                for j in range(2):
                    load(2 * p + j, n, row_unit(a_pw2_w_2[0], (2 * r + j) * P))

            def ada_block(layer, b):
                m8 = (b + NBLK * layer) * 8
                for k in range(2):
                    need(sp, gemv, m8 + (4 * k - 4))
                    sp.dma_start(ada_raw[:, k, :, :],
                                 ada[layer][k * 4 * P:(k + 1) * 4 * P, bass.ds(b * BLK, BLK)]
                                 .rearrange("(k p) n -> p k n", p=P)).then_inc(ada_ld[k], 16)

            def attention_loads(s, i):
                for p in range(3):
                    pair(s, p, i)
                pair(s, 3, i - 1)
                if s == 0:
                    ada_block(0, i * 2 + 2)
                    ada_block(0, i * 2 + 3)

            def ffn_loads(s, i, first=False):
                pair(s, 0, i)
                pair(s, 1, i)
                if not first:
                    pair(s, 2, i - 1)
                if s < 5:
                    ada_block(s // 2 + 1, i - 1)

            def pw1_loads(i):
                pair(4, 0, i)
                pair(4, 1, i)

            for b in range(3):
                ada_block(0, b)
                pair(0, b, 0)
            ada_block(0, 3)
            for s in range(LAST + 1):
                more = s < LAST
                if s in (0, 2):
                    with sp.Fori(1, NI_A) as i:
                        attention_loads(s, i)
                    if more:
                        for p in range(3):
                            pair(s + 1, p, 0)
                    pair(s, 3, NI_A - 1)
                    if s == 0:
                        ada_block(0, NBLK - 2)
                        ada_block(0, NBLK - 1)
                elif s == 4:
                    with sp.Fori(1, NI_C) as i:
                        pw1_loads(i)
                    if more:
                        pair(5, 0, 0)
                        pair(5, 1, 0)
                    pw2_pair(2, 2, USE[4][2] + 1)
                    pw2_pair(3, 3, USE[4][3] + 1)
                    if more:
                        pair(5, 2, 0)
                else:
                    ffn_loads(s, 1, True)
                    with sp.Fori(2, NI_F) as i:
                        ffn_loads(s, i)
                    if more:
                        pair(s + 1, 0, 0)
                        pair(s + 1, 1, 0)
                    pair(s, 2, NI_F - 1)
                    if s < 5:
                        ada_block(s // 2 + 1, NI_F - 1)
                    if more:
                        if s == 1:
                            pair(2, 2, 0)
                        else:
                            pw2_pair(0, 2, USE[4][2])
                            pw2_pair(1, 3, USE[4][3])
                        ada_block(s // 2 + 1, NBLK - 1)
            for t in range(TT):
                sp.wait_ge(x_ready, 2 * LAST + t + 1)
                sp.dma_start(out[0, t * P:(t + 1) * P, :], xt[:, t, :]).then_inc(stored, 16)
            sp.wait_ge(stored, 16 * TT)

        @block.gpsimd
        def _(pool):
            pool.memset(ident[:], 0.0).then_inc(id_zero, 1)
            pool.wait_ge(id_zero, 1)
            pool.affine_select(out=ident[:], in_=ident[:], compare_op=ALU.not_equal, fill=1.0, base=0,
                               pattern=[[-1, P]], channel_multiplier=1).then_inc(consts, 1)
            pool.memset(ones[:], 1.0).then_inc(consts, 1)
            pool.memset(mhalf, -0.5).then_inc(consts, 1)
            pool.memset(eps2, 2 * EPS).then_inc(consts, 1)

            def row(src):
                return bass.AP(src.tensor, src.offset, [[0, P], [1, D]])

            def acc_init(layer):
                if layer:
                    pool.wait_ge(mod_gf, 2 * layer)
                pool.memset(acc[:], 0.0).then_inc(acc_zero, 1)
                pool.wait_ge(acc_zero, layer + 1)
                bias = ada_b[layer:layer + 1, :] if layer < 2 else mod_b_2[0:1, :]
                pool.dma_start(acc[0:1, :], bias).then_inc(acc_bias, 16)

            def gains(layer):
                need(pool, x_ready, 4 * layer)
                post = ((norm_g[layer, 1], norm_g[layer, 3]) if layer < 2
                        else (norm_post_mix_2[0], norm_post_ffn_2[0]))
                for g, src in zip((Ga, Gf), post):
                    pool.dma_start(g[:], row(src)).then_inc(gain_loaded, 16)
                if layer == 2:
                    pool.dma_start(b2row, row(a_pw2_b_2[0])).then_inc(b2_loaded, 16)

            def rstd(ss, ms, rs, ss_done, ms_done, rs_done, at, t):
                pool.wait_ge(ss_done, at + 1)
                pool.tensor_scalar(ms[:, t:t + 1], ss[:, t:t + 1], EPS, None, ALU.add).then_inc(ms_done, 1)
                pool.wait_ge(ms_done, at + 1)
                pool.tensor_tensor(rs[:, t:t + 1], ms[:, t:t + 1], mhalf, ALU.pow).then_inc(rs_done, 1)

            acc_init(0)
            pool.wait_ge(consts, 4)
            for s in range(LAST + 1):
                for t in range(TT):
                    rstd(ssx, msx, rsx, ssx_done, msx_done, rsx_done, 2 * s + t, t)
                if s % 2 == 0:
                    gains(s // 2)
                elif s < 5:
                    acc_init(s // 2 + 1)
                if s == 2:
                    def head_rstd(i):
                        for at in range(2 * TT):
                            t = at % TT
                            pool.wait_ge(oss, i * 4 + at + 1)
                            pool.tensor_tensor(mso[:, t:t + 1], sso[:, t:t + 1], eps2, ALU.add).then_inc(oms, 1)
                            pool.wait_ge(oms, i * 4 + at + 1)
                            pool.tensor_tensor(rso[:, t:t + 1], mso[:, t:t + 1], mhalf, ALU.pow)\
                                .then_inc(ors, 1)
                    with pool.Fori(0, NI_A) as i:
                        head_rstd(i)
                if s == 4:
                    for t in range(TT):
                        pool.wait_ge(ag_done, t + 1)
                        pool.tensor_scalar(lnm[:, t:t + 1], bnag[:, 2 * t + 1:2 * t + 2], LN_EPS, None,
                                           ALU.add).then_inc(lv_done, 1)
                        pool.wait_ge(lv_done, t + 1)
                        pool.tensor_tensor(lnr[:, t:t + 1], lnm[:, t:t + 1], mhalf, ALU.pow)\
                            .then_inc(lr_done, 1)
                for t in range(TT):
                    rstd(ssy, msy, rsy, ssy_done, msy_done, rsy_done, 2 * s + t, t)

        @block.tensor
        def _(pe):
            def col_product(dst, u, n, early=None):
                pe.wait_ge(lo[u], n + 1)
                for k in range(KT):
                    if early is not None and k % 2 == 0:
                        pe.wait_ge(hlo, 4 * early + k // 2 + 1)
                    ws = slice(k * P, (k + 1) * P)
                    for m, (w, h) in enumerate(((whi, h_hi), (whi, h_lo), (wlo, h_hi))):
                        mm = pe.matmul(dst, w[:, u, ws], h[:, k, :], start=(k == 0 and m == 0),
                                       stop=(k == KT - 1 and m == 2))
                mm.then_inc(used[u], 1)

            def row_product(a_h, a_l, u, n, first=False, end=False):
                pe.wait_ge(lo[u], n + 1)
                for t in range(TT):
                    ts = slice(t * P, (t + 1) * P)
                    for m, (a, w) in enumerate(((a_h, whi), (a_h, wlo), (a_l, whi))):
                        for f in range(2):
                            mm = pe.matmul(Y[:, 2 * t + f, :], a[:, ts], w[:, u, f * 512:(f + 1) * 512],
                                           start=(first and m == 0), stop=(end and m == 2))
                    if t == 0 and end:
                        mm.then_inc(y0_done, 1)
                mm.then_inc(used[u], 1)

            def mod_columns(base):
                for m in range(2 * KT):
                    mm = pe.matmul(work[:, 3, m:m + 1], acc[:, base + m * P:base + (m + 1) * P],
                                   ones[:, 0:1], start=True, stop=True)
                mm.then_inc(mod_cols, 1)

            def mod_first(layer):
                pe.wait_ge(gemv, 8 * (NBLK * layer + 4))
                mod_columns(0)

            def mod_rest(layer):
                pe.wait_ge(gemv, 8 * NBLK * (layer + 1))
                for f in range(2):
                    mm = pe.matmul(work[:, f, :], ones[:], acc[:, 2 * D + f * 512:2 * D + (f + 1) * 512],
                                   start=True, stop=True)
                mm.then_inc(mod_ga, 1)
                mod_columns(3 * D)
                pe.matmul(work[:, 2, :], ones[:], acc[:, 5 * D:5 * D + 512],
                          start=True, stop=True).then_inc(mod_gf, 1)
                pe.wait_ge(mod_cols_used, 2 * layer + 2)
                pe.matmul(work[:, 3, :], ones[:], acc[:, 5 * D + 512:6 * D],
                          start=True, stop=True).then_inc(mod_gf, 1)

            def pre_norm(s):
                pe.wait_ge(mod_cols_used, s + 1)
                if s % 2:
                    pe.wait_ge(mod_ga_used, s // 2 + 1)
                    pe.wait_ge(mod_gf_used, s // 2 + 1)
                for t in range(TT):
                    pe.wait_ge((xs0, xs1)[t], s + 1)
                    for k in range(KT):
                        at = (k % 2) * S + t * P
                        mm = pe.transpose(work[:, k // 2, at:at + P], xs[:, t, k * P:(k + 1) * P], ident[:])
                        if t == TT - 1 and k % 2:
                            mm.then_inc(hT, 1)

            pe.wait_ge(consts, 4)
            for g, rows in enumerate(PAR_ROWS):
                if g == 0:
                    pe.wait_ge(c_loaded, 32)
                elif g == 1:
                    pe.wait_ge(par_loaded, 16 * 16)
                pe.transpose(par_bank[g][:, 0:rows], prow[0:rows, g, :],
                             ident[0:rows, 0:rows]).then_inc(par_T, 1)
            pe.wait_ge(rel_loaded, 48)
            pe.matmul(Y[0:H, 0, 0:REL], relt[:], onehot, start=True, stop=True).then_inc(rel_mm, 1)

            def attention(s):
                hb, rb, nb, nb3 = HEADS[s], ROWS[s], USE[s][0], USE[s][3]

                def head_out_T(T, end=False):
                    pe.wait_ge(osn, (T - hb) * 2 + 2)
                    if not end:
                        pe.wait_ge(sb_done, (T - hb) * 2 + (4 + HEADS[2]))
                    for t in range(TT):
                        mm = pe.transpose(work[:, 2, t * P:(t + 1) * P], osc[:, t * P:(t + 1) * P], ident[:])
                    mm.then_inc(oT_mm, 1)

                def probs_T(T):
                    pe.wait_ge(p_done, T * 2 + 2)
                    for m in range(3):
                        mm = pe.transpose(work[:, 3, m * P:(m + 1) * P], pr[:, 0, m * P:(m + 1) * P], ident[:])
                    mm.then_inc(pT_mm, 1)

                def head_values(i, j):
                    pe.wait_ge(pT_ev, i * 2 + (hb + j + 1))
                    pe.wait_ge(v_ev, i + (hb // 2 + 1))
                    v0, v1 = (vv[:, t, j * P:(j + 1) * P] for t in range(TT))
                    if s == 0:
                        pe.matmul(work[:, 1, 0:P], v0, pT[:, 0:P], start=True, stop=True)
                        pe.matmul(work[:, 1, P:S], v0, pT[:, P:S], start=True, stop=False)
                        mm = pe.matmul(work[:, 1, P:S], v1, pT[:, S:3 * P], start=False, stop=True)
                    else:
                        pe.matmul(work[:, 1, 0:P], pT[:, 0:P], v0, start=True, stop=True)
                        pe.matmul(work[:, 1, P:S], pT[:, P:S], v0, start=True, stop=False)
                        mm = pe.matmul(work[:, 1, P:S], pT[:, S:3 * P], v1, start=False, stop=True)
                    mm.then_inc(pv_mm, 1)

                def scores(T):
                    pe.wait_ge(qk_ev, T + 1)
                    if s == 0:
                        need(pe, sb_done, T)
                        pe.matmul(work[:, 2, 0:P], qk[:, 0:P], qk[:, S:S + P], start=True, stop=True)
                        mm = pe.matmul(work[:, 2, P:3 * P], qk[:, P:S], qk[:, S:2 * S], start=True, stop=True)
                    else:
                        need(pe, alo, T - hb + (rb - 1))
                        for g in range(2):
                            half = slice(g * 64, (g + 1) * 64)
                            pe.matmul(work[:, 2 + g, 0:P], qk[half, 0:P], qk[half, S:S + P],
                                      start=True, stop=True)
                            mm = pe.matmul(work[:, 2 + g, P:3 * P], qk[half, P:S], qk[half, S:2 * S],
                                           start=True, stop=True)
                    mm.then_inc(s_mm, 1)

                def values(T, n):
                    pe.wait_ge(lo[4], n + 1)
                    pe.wait_ge(lo[5], n + 1)
                    if s == 0:
                        need(pe, alo, T - hb + rb)
                    else:
                        need(pe, ocp, T - hb)
                    for t, units in ((0, (4, 6)), (1, (4, 5)), (1, (5, 6))):
                        ts = slice(t * P, (t + 1) * P)
                        u0, u1 = units
                        dst = work[:, 1, t * S + (u0 - 4) * P:t * S + (u1 - 4) * P]
                        for k in range(KT):
                            ws = slice(k * P, (k + 1) * P)
                            for m, (h, w) in enumerate(((h_hi, whi), (h_lo, whi), (h_hi, wlo))):
                                mm = pe.matmul(dst, h[:, k, ts], w[:, u0:u1, ws],
                                               start=(k == 0 and m == 0), stop=(k == KT - 1 and m == 2))
                        if t:
                            mm.then_inc(used[u0], 1)

                def w_o(i, j, first=False, end=False):
                    pe.wait_ge(alo, i * 2 + (rb + j + 1))
                    row_product(a_hi[:, j, :], a_lo[:, j, :], 6 + j, i + nb3, first, end)

                def step(i, j):
                    T = i * 2 + (hb + j)
                    start = isinstance(i, int) and i == 0
                    if s == 2 and not start:
                        head_out_T(T - 2)
                    need(pe, qk_ev, T)
                    col_product(work[:, 0, 0:S], j, i + nb, s if start and j == 0 else None)
                    col_product(work[:, 0, S:2 * S], 2 + j, i + nb)
                    if not (start and j == 0):
                        probs_T(T - 1)
                    if not start:
                        w_o(i - 1, j, first=isinstance(i, int) and i == 1 and j == 0)
                    if j:
                        head_values(i, 0)
                    elif not start:
                        head_values(i - 1, 1)
                    scores(T)
                    if j == 0:
                        values(T, i + nb)

                for i in range(2):
                    step(i, 0)
                    step(i, 1)
                with pe.Fori(2, NI_A) as i:
                    step(i, 0)
                    step(i, 1)
                T = hb + H
                if s == 2:
                    head_out_T(T - 2)
                probs_T(T - 1)
                w_o(NI_A - 1, 0)
                head_values(NI_A - 1, 1)
                if s == 2:
                    head_out_T(T - 1, end=True)
                w_o(NI_A - 1, 1, end=True)

            def gated(s):
                rb, fb, nb, nb2 = ROWS[s], STEPS[s], USE[s][0], USE[s][2]

                def down(i, j, first=False, end=False):
                    pe.wait_ge(alo, i * 2 + (rb + j + 1))
                    row_product(a_hi[:, j, :], a_lo[:, j, :], 4 + j, i + nb2, first, end)

                def step(i, j):
                    start = isinstance(i, int) and i == 0
                    before = i * 2 + j - 1
                    if not start:
                        if s == 5:
                            pe.wait_ge(cv_g, before)
                        else:
                            pe.wait_ge(gate_done, before + fb)
                    col_product(work[:, 2 * j, 0:S], j, i + nb, s if start and j == 0 else None)
                    if not start:
                        if s == 5:
                            pe.wait_ge(cv_u, before)
                        else:
                            pe.wait_ge(act_done, before + fb)
                    col_product(work[:, 2 * j + 1, 0:S], 2 + j, i + nb)
                    if j == 1:
                        down(i, 0, first=start)
                    elif not start:
                        down(i - 1, 1)

                def both(i, more):
                    step(i, 0)
                    step(i, 1)

                sweep(pe, 1, NI_F, s, both)
                down(NI_F - 1, 1, end=True)

            def conformer():
                nb, fb = USE[4][0], STEPS[4]

                def step(i, j):
                    start = isinstance(i, int) and i == 0
                    before = i * 2 + (j - 1 + fb)
                    if not start:
                        pe.wait_ge(act_done, before)
                    col_product(work[:, 2 * j, 0:S], j, i + nb, 4 if start and j == 0 else None)
                    if not start:
                        pe.wait_ge(gate_done, before)
                    col_product(work[:, 2 * j + 1, 0:S], 2 + j, i + nb)

                def both(i, more):
                    step(i, 0)
                    step(i, 1)

                sweep(pe, 1, NI_C, 4, both)
                pe.wait_ge(conv_done, KT)
                for t in range(TT):
                    for k in range(KT):
                        mm = pe.transpose(work[:, 2 * t + k // 4, (k % 4) * P:(k % 4 + 1) * P],
                                          convT[:, k, t * P:(t + 1) * P], ident[:])
                        if k % 4 == 3:
                            mm.then_inc(cT_mm, 1)
                pe.wait_ge(z_done, TT)
                for t in range(TT):
                    for k in range(KT):
                        at = (k % 2) * S + t * P
                        mm = pe.transpose(work[:, k // 2, at:at + P], xs[:, t, k * P:(k + 1) * P], ident[:])
                        if t == TT - 1 and k % 2:
                            mm.then_inc(zT_mm, 1)
                for k in range(KT):
                    r, j = k // 2, k % 2
                    pe.wait_ge(p_lo, r + 1)
                    row_product(h_hi[:, k, :], h_lo[:, k, :], 4 + 2 * (r % 2) + j,
                                USE[4][2 + r % 2] + r // 2, first=(k == 0), end=(k == KT - 1))

            mod_first(0)
            for s in range(LAST + 1):
                pre_norm(s)
                pe.wait_ge(x_ready, 2 * s) if s else pe.wait_ge(rel_row, 1)
                if s in (0, 2):
                    attention(s)
                elif s == 4:
                    conformer()
                else:
                    gated(s)
                if s % 2 == 0:
                    mod_rest(s // 2)
                elif s < LAST:
                    mod_first(s // 2 + 1)

        @block.scalar
        def _(act):
            def prep(u, n):
                act.wait_ge(ld[u], n * 16 + 16)
                need(act, used[u], n)
                act.activation(whi[:, u, :], raw[:, u, :], ACT.Copy).then_inc(hi[u], 1)

            def params(dst, src, s):
                act.dma_start(dst, src).then_inc(s, 16)

            def rows(src):
                return src.rearrange("a (r p) -> (a r) p", p=P)

            params(prow[0:8, 0, :], rows(c), c_loaded)
            params(prow[8:16, 0, :], rows(c_2), c_loaded)
            for t in range(TT):
                params(xt[:, t, :], x[0, t * P:(t + 1) * P, :], x_loaded)
            pre = [norm_g[0, 0:1], norm_g[0, 2:3], norm_g[1, 0:1], norm_g[1, 2:3], norm_pre_mix_2,
                   norm_pre_ffn_2, a_pw1_b_2, a_dw_b_2, a_ln_g_2, a_ln_b_2, diff_subln_g]
            at = 0
            for src in pre:
                r = src.shape[1] // P
                params(prow[at:at + r, 1, :], rows(src), par_loaded)
                at += r
            params(prow[0:4 * FT, 2, :], rows(f_dw_w_2[0, 0:2]), par_loaded)
            params(prow[0:2 * FT, 3, :], rows(f_dw_w_2[0, 2:3]), par_loaded)
            params(prow[2 * FT:4 * FT, 3, :], rows(f_dw_b_2), par_loaded)
            params(prow[0:16 * KT, 4, :], rows(a_dw_w_2[0, 0:16]), par_loaded)
            params(prow[0:15 * KT, 5, :], rows(a_dw_w_2[0, 16:CONV]), par_loaded)
            params(relt[:], rel_bias, rel_loaded)
            params(onehot, bucket_onehot, rel_loaded)
            params(relrow, causal_fill, rel_loaded)
            params(lam_in, bass.AP(diff_lambda.tensor, diff_lambda.offset, [[0, P], [1, 256]]), lam_loaded)

            act.wait_ge(par_T, 1)
            act.activation(csil[:], par_bank[0][:, 0:16], ACT.Silu).then_inc(csil_ready, 1)
            for u in range(4):
                prep(u, 0)
            act.wait_ge(rel_row, 1)
            act.dma_start(rel_rows, relrow.unsqueeze(1).broadcast_to([H, P, REL])).then_inc(rel_stored, 16)
            for u in range(4, 6):
                prep(u, 0)
            act.wait_ge(rel_stored, 16)
            for off, lo_c, hi_c in ((255, 0, P), (127, P, 3 * P)):
                src = bass.AP(rel_rows.tensor, rel_rows.offset + off, [[REL - 1, P], [P * REL, H], [1, hi_c - lo_c]])
                act.dma_start(head_bias[:, :, lo_c:hi_c], src).then_inc(bias_loaded, 16)

            def pre_norm(s):
                for t in range(TT):
                    if s == 0:
                        act.wait_ge(x_loaded, 32)
                        act.wait_ge(par_T, len(PAR_ROWS))
                    else:
                        act.wait_ge(x_ready, 2 * (s - 1) + t + 1)
                    act.activation(xs[:, t, :], xt[:, t, :], ACT.Square, scale=D ** -0.5,
                                   accum_out=ssx[:, t:t + 1]).then_inc(ssx_done, 1)
                act.wait_ge(rsx_done, 2 * s + 2)
                act.activation(xs[:, 1, :], xt[:, 1, :], ACT.Copy, scale=rsx[:, 1:2]).then_inc(xs1, 1)
                act.wait_ge(mod_cols_used, s + 1)
                def scaled(b):
                    act.wait_ge(hT, 4 * s + b + 1)
                    for k in (2 * b, 2 * b + 1):
                        bank = work[:, b, (k % 2) * S:(k % 2 + 1) * S]
                        a = act.activation(bank, bank, ACT.Identity, scale=colA[:, k:k + 1],
                                           bias=colB[:, k:k + 1])
                    a.then_inc(h32a, 1)
                def high(b):
                    act.wait_ge((h32v, h32a)[b % 2], 2 * s + b // 2 + 1)
                    act.activation(h_hi[:, 2 * b:2 * b + 2, :].rearrange("p k n -> p (k n)"), work[:, b, :],
                                   ACT.Copy).then_inc(hhi, 1)
                scaled(1)
                high(0)
                high(1)
                scaled(3)
                high(2)
                high(3)

            def post_norm(s, u, n):
                for t in range(TT):
                    if s == 4:
                        act.wait_ge(yb, t + 1)
                    elif t == 0:
                        act.wait_ge(y0_done, s + 1)
                    else:
                        act.wait_ge(used[u], n + 1)
                    act.activation(xs[:, t, :], Y[:, 2 * t:2 * t + 2, :].rearrange("p a b -> p (a b)"),
                                   ACT.Square, scale=D ** -0.5,
                                   accum_out=ssy[:, t:t + 1]).then_inc(ssy_done, 1)

            def attention(s):
                hb, rb, nb, nb3 = HEADS[s], ROWS[s], USE[s][0], USE[s][3]
                ne = 2 if s == 0 else 4

                def probs_T(T):
                    act.wait_ge(pT_mm, T + 1)
                    need(act, pv_mm, T)
                    act.activation(pT, work[:, 3, 0:3 * P], ACT.Copy).then_inc(pT_ev, 1)

                def out_hi(i, j):
                    if s == 0:
                        act.wait_ge(pv_mm, i * 2 + (hb + j + 1))
                        src, by = work[:, 1, 0:S], 1.0
                    else:
                        act.wait_ge(oT_mm, i * 2 + (j + 1))
                        src, by = work[:, 2, 0:S], subg
                    need(act, used[6 + j], i + nb3)
                    act.activation(a_hi[:, j, :], src, ACT.Copy, scale=by).then_inc(ahi, 1)

                def squares(T):
                    act.wait_ge(ocp, T - hb + 1)
                    for t in range(TT):
                        need(act, oT_mm, T - hb)
                        act.activation(osc[:, t * P:(t + 1) * P], oraw[:, t * P:(t + 1) * P], ACT.Square,
                                       scale=0.125, accum_out=sso[:, t:t + 1]).then_inc(oss, 1)

                def step(i, j, more):
                    T = i * 2 + (hb + j)
                    start = isinstance(i, int) and i == 0
                    first = start and j == 0
                    if s == 2 and not start:
                        out_hi(i - 1, j)
                    act.wait_ge(used[2 + j], i + (nb + 1))
                    need(act, s_mm, T)
                    act.activation(qk, work[:, 0, :], ACT.Copy).then_inc(qk_ev, 1)
                    if not first:
                        probs_T(T - 1)
                    if more:
                        prep(j, i + (nb + 1))
                        prep(2 + j, i + (nb + 1))
                    prep(6 + j, i + nb3)
                    if not first:
                        if s == 2:
                            squares(T - 1)
                        elif j:
                            out_hi(i, 0)
                        else:
                            out_hi(i - 1, 1)
                    act.wait_ge(ng_done, T + 1)
                    for q, (a, b) in enumerate(((0, P), (P, 3 * P))):
                        for g in range(ne // 2):
                            m = q * (ne // 2) + g
                            act.activation(pr[:, g, a:b], pr[:, g, a:b], ACT.Exp, bias=mneg[:, m:m + 1],
                                           accum_out=msum[:, m:m + 1]).then_inc(ex_done, 1)
                    if j == 0:
                        act.wait_ge(used[5], i + (nb + 1))
                        need(act, pv_mm, T)
                        act.activation(mix[:, 512:1024], work[:, 1, :], ACT.Copy).then_inc(v_ev, 1)
                    if more:
                        prep(4 + j, i + (nb + 1))

                def both(i, more):
                    step(i, 0, more)
                    step(i, 1, more)

                if s == 2:
                    act.wait_ge(lam_seq, 2)
                    act.activation(lame, lamv, ACT.Exp).then_inc(lam_exp, 1)
                    act.wait_ge(lam_seq, 5)
                sweep(act, 1, NI_A, s, both)
                T = hb + H
                if s == 2:
                    out_hi(NI_A - 1, 0)
                probs_T(T - 1)
                if s == 2:
                    squares(T - 1)
                out_hi(NI_A - 1, 1)

            def gated(s):
                rb, fb, nb, nb2 = ROWS[s], STEPS[s], USE[s][0], USE[s][2]
                gate = gate_of[s]

                def step(i, j, more):
                    start = isinstance(i, int) and i == 0
                    F = i * 2 + (fb + j)
                    if not start:
                        prep(4 + j, i + nb2)
                    act.wait_ge(used[j], i + (nb + 1))
                    if not start:
                        act.wait_ge(act_done, F - 1)
                    if s == 5:
                        act.wait_ge(taps_ready, i * 2 + (2 * KT + j + 1))
                        act.activation(gate[:, j, :], work[:, 2 * j, 0:S], ACT.Identity, scale=taps[:, j, 4:5],
                                       bias=taps[:, j, 6:7]).then_inc(cv_g0, 1)
                        if more:
                            prep(j, i + (nb + 1))
                        act.wait_ge(cv_g, i * 2 + (j + 1))
                        act.activation(gate[:, j, :], gate[:, j, :], ACT.Silu).then_inc(gate_done, 1)
                    else:
                        act.activation(gate[:, j, :], work[:, 2 * j, 0:S], ACT.Silu).then_inc(gate_done, 1)
                        if more:
                            prep(j, i + (nb + 1))
                    if more:
                        prep(2 + j, i + (nb + 1))
                    act.wait_ge(act_done, F + 1)
                    need(act, used[4 + j], i + nb2)
                    act.activation(a_hi[:, j, :], act32[:, j, :], ACT.Copy).then_inc(ahi, 1)

                def both(i, more):
                    step(i, 0, more)
                    step(i, 1, more)

                sweep(act, 1, NI_F, s, both)

            def conformer():
                nb, fb = USE[4][0], STEPS[4]
                gate = gate_of[4]

                def step(i, j, more):
                    start = isinstance(i, int) and i == 0
                    F = i * 2 + (fb + j)
                    if more:
                        prep(j, i + (nb + 1))
                    act.wait_ge(used[2 + j], i + (nb + 1))
                    act.wait_ge(taps_ready, i * 4 + (2 * j + 2))
                    if not start:
                        act.wait_ge(act_done, F - 1)
                    act.activation(gate[:, j, :], work[:, 2 * j + 1, 0:S], ACT.Sigmoid,
                                   bias=taps[:, j, 32:33]).then_inc(gate_done, 1)
                    if more:
                        prep(2 + j, i + (nb + 1))

                def both(i, more):
                    step(i, 0, more)
                    step(i, 1, more)

                sweep(act, 1, NI_C, 4, both)
                for b in range(4):
                    act.wait_ge(zT_mm, b + 1)
                    for k in (2 * b, 2 * b + 1):
                        bank = work[:, b, (k % 2) * S:(k % 2 + 1) * S]
                        a = act.activation(bank, bank, ACT.Silu, scale=cols[:, LNG + k:LNG + k + 1],
                                           bias=cols[:, LNB + k:LNB + k + 1])
                    a.then_inc(ln_act, 1)
                for p in (2, 3):
                    for j in range(2):
                        prep(2 * p + j, USE[4][p] + 1)

            for s in range(LAST + 1):
                pre_norm(s)
                if s in (2, 4, 5):
                    for j in range(2):
                        prep(4 + j, USE[s][2])
                if s == 4:
                    for j in range(2):
                        prep(6 + j, USE[4][3])
                if s in (0, 2):
                    attention(s)
                    post_norm(s, 7, USE[s][3] + NI_A - 1)
                elif s == 4:
                    conformer()
                    post_norm(s, 7, USE[4][3] + 1)
                else:
                    gated(s)
                    post_norm(s, 5, USE[s][2] + NI_F - 1)

        @block.vector
        def _(dve):
            def prep(u, n):
                dve.wait_ge(hi[u], n + 1)
                dve.tensor_tensor(wlo[:, u, :], raw[:, u, :], whi[:, u, :].bitcast(F32),
                                  ALU.subtract).then_inc(lo[u], 1)

            def gemv_step(layer, b, q):
                k, m = q // 4, b + NBLK * layer
                if q % 4 == 0:
                    dve.wait_ge(ada_ld[k], m * 16 + 16)
                if q:
                    dve.wait_ge(gemv, m * 8 + q)
                at = acc[:, bass.ds(b * BLK, BLK)]
                ccol = (8 if layer == 2 else 0) + q
                dve.scalar_tensor_tensor(at, ada_raw[:, k, q % 4, :], csil[:, ccol:ccol + 1], at,
                                         ALU.mult, ALU.add).then_inc(gemv, 1)

            def gemv_start(layer):
                dve.wait_ge(acc_bias, 16 * (layer + 1))
                if layer == 0:
                    dve.wait_ge(csil_ready, 1)

            gemv_start(0)
            for b in range(4):
                for q in range(KT):
                    gemv_step(0, b, q)
                if b < 3:
                    prep(2 * b, 0)
                    prep(2 * b + 1, 0)
                if b == 1:
                    at = 0
                    for g, rows in enumerate(PAR_ROWS):
                        if g:
                            dve.wait_ge(par_T, g + 1)
                            dve.tensor_copy(cols[:, at:at + rows],
                                            par_bank[g][:, 0:rows]).then_inc(cols_ready, 1)
                            at += rows
                    dve.wait_ge(rel_mm, 1)
                    dve.tensor_tensor(relrow, Y[0:H, 0, 0:REL], relrow, ALU.add).then_inc(rel_row, 1)

            def columns(s):
                dve.wait_ge(mod_cols, s + 1)
                dve.wait_ge(cols_ready, len(PAR_ROWS) - 1)
                dve.scalar_tensor_tensor(colA[:], work[:, 3, KT:2 * KT], 1.0,
                                         cols[:, NORM + KT * s:NORM + KT * (s + 1)], ALU.add, ALU.mult)
                dve.tensor_copy(colB[:], work[:, 3, 0:KT]).then_inc(mod_cols_used, 1)

            def pre_norm(s):
                dve.wait_ge(rsx_done, 2 * s + 1)
                if s == 0:
                    dve.wait_ge(rel_stored, 16)
                dve.tensor_scalar(xs[:, 0, :], xt[:, 0, :], rsx[:, 0:1], None, ALU.mult).then_inc(xs0, 1)
                dve.wait_ge(mod_cols_used, s + 1)
                for b in (0, 2):
                    dve.wait_ge(hT, 4 * s + b + 1)
                    for k in (2 * b, 2 * b + 1):
                        bank = work[:, b, (k % 2) * S:(k % 2 + 1) * S]
                        v = dve.tensor_scalar(bank, bank, colA[:, k:k + 1], colB[:, k:k + 1], ALU.mult, ALU.add)
                    v.then_inc(h32v, 1)
                for b in range(4):
                    dve.wait_ge(hhi, 4 * s + b + 1)
                    hs = slice(2 * b, 2 * b + 2)
                    dve.tensor_tensor(h_lo[:, hs, :].rearrange("p k n -> p (k n)"), work[:, b, :],
                                      h_hi[:, hs, :].rearrange("p k n -> p (k n)").bitcast(F32),
                                      ALU.subtract).then_inc(hlo, 1)

            def post_norm(s, u, n):
                L = s // 2
                G, G_used = (Ga, mod_ga_used) if s % 2 == 0 else (Gf, mod_gf_used)
                if s % 2 == 0:
                    dve.wait_ge(mod_ga, L + 1)
                    dve.wait_ge(gain_loaded, 32 * (L + 1))
                    dve.tensor_tensor(Ga[:], work[:, 0:2, :].rearrange("p a b -> p (a b)"), Ga[:],
                                      ALU.mult).then_inc(mod_ga_used, 1)
                    columns(s + 1)
                dve.wait_ge(G_used, L + 1)
                for t in range(TT):
                    yt = Y[:, 2 * t:2 * t + 2, :].rearrange("p a b -> p (a b)")
                    dve.wait_ge(rsy_done, 2 * s + t + 1)
                    dve.scalar_tensor_tensor(xs[:, t, :], yt, rsy[:, t:t + 1], G[:], ALU.mult,
                                             ALU.mult).then_inc(y_tmp, 1)
                    dve.wait_ge(y_tmp, 2 * s + t + 1)
                    if s == 0:
                        dve.wait_ge(x_loaded, 32)
                    dve.tensor_tensor(xt[:, t, :], xt[:, t, :], xs[:, t, :], ALU.add).then_inc(x_ready, 1)
                if s % 2 == 0:
                    dve.wait_ge(mod_gf, 2 * L + 2)
                    dve.tensor_tensor(Gf[:], work[:, 2:4, :].rearrange("p a b -> p (a b)"), Gf[:],
                                      ALU.mult).then_inc(mod_gf_used, 1)

            def attention(s):
                hb, rb, nb, nb3 = HEADS[s], ROWS[s], USE[s][0], USE[s][3]

                def out_lo(i, j):
                    R = i * 2 + (rb + j)
                    dve.wait_ge(ahi, R + 1)
                    high = a_hi[:, j, :].bitcast(F32)
                    if s == 0:
                        dve.tensor_tensor(a_lo[:, j, :], work[:, 1, 0:S], high, ALU.subtract).then_inc(alo, 1)
                    else:
                        dve.scalar_tensor_tensor(a_lo[:, j, :], work[:, 2, 0:S], subg, high, ALU.mult,
                                                 ALU.subtract).then_inc(alo, 1)

                def copy_out(T):
                    dve.wait_ge(pv_mm, T + 1)
                    dve.tensor_copy(oraw, work[:, 1, 0:S]).then_inc(ocp, 1)

                def norm_out(T):
                    for t in range(TT):
                        dve.wait_ge(ors, (T - hb) * 2 + (t + 1))
                        dve.wait_ge(ocp, T - hb + 1)
                        dve.tensor_scalar(osc[:, t * P:(t + 1) * P], oraw[:, t * P:(t + 1) * P],
                                          rso[:, t:t + 1], None, ALU.mult).then_inc(osn, 1)

                def softmax(T, h, between):
                    ng = 1 if s == 0 else 2
                    n1 = (T - hb) * ng + (0 if s == 0 else HEADS[2])
                    dve.wait_ge(s_mm, T + 1)
                    need(dve, pT_mm, T)
                    for g in range(ng):
                        dve.scalar_tensor_tensor(pr[:, g, :], work[:, 2 + g, 0:3 * P], scale_of[s],
                                                 head_bias[:, bass.ds(h, 1), :].rearrange("p a n -> p (a n)"),
                                                 ALU.mult, ALU.add).then_inc(sb_done, 1)
                    dve.wait_ge(sb_done, n1 + ng)
                    for q, (a, b) in enumerate(((0, P), (P, 3 * P))):
                        dve.tensor_reduce(mmax[:, q * ng:(q + 1) * ng], pr[:, 0:ng, a:b], AX.X,
                                          ALU.max).then_inc(mx_done, 1)
                    dve.wait_ge(mx_done, T * 2 + 2)
                    dve.tensor_scalar(mneg[:, 0:2 * ng], mmax[:, 0:2 * ng], -1.0, None,
                                      ALU.mult).then_inc(ng_done, 1)
                    between()
                    n2 = (T - hb) * (2 * ng) + (0 if s == 0 else 2 * HEADS[2])
                    dve.wait_ge(ex_done, n2 + 2 * ng)
                    dve.reciprocal(mrec[:, 0:2 * ng], msum[:, 0:2 * ng]).then_inc(rc_done, 1)
                    dve.wait_ge(rc_done, T + 1)
                    if s == 0:
                        for q, (a, b) in enumerate(((0, P), (P, 3 * P))):
                            dve.tensor_scalar(pr[:, 0, a:b], pr[:, 0, a:b], mrec[:, q:q + 1], None,
                                              ALU.mult).then_inc(p_done, 1)
                        return
                    n3 = (T - hb) * 3
                    dve.tensor_scalar(lrec, mrec.rearrange("p (q g) -> p q g", g=2)[:, :, 1], lamf[:, 0:1], None,
                                      ALU.mult).then_inc(dif_seq, 1)
                    dve.wait_ge(dif_seq, n3 + 1)
                    for q, (a, b) in enumerate(((0, P), (P, 3 * P))):
                        dve.tensor_scalar(pr[:, 1, a:b], pr[:, 1, a:b], lrec[:, q:q + 1], None,
                                          ALU.mult).then_inc(dif_seq, 1)
                    for q, (a, b) in enumerate(((0, P), (P, 3 * P))):
                        dve.wait_ge(dif_seq, n3 + 2 + q)
                        dve.scalar_tensor_tensor(pr[:, 0, a:b], pr[:, 0, a:b], mrec[:, 2 * q:2 * q + 1],
                                                 pr[:, 1, a:b], ALU.mult, ALU.subtract).then_inc(p_done, 1)

                def step(i, j, more):
                    T = i * 2 + (hb + j)
                    start = isinstance(i, int) and i == 0
                    first = start and j == 0

                    def sums(q0):
                        if s == 0:
                            for q in range(q0, q0 + 2):
                                gemv_step(0, i * 2 + (4 + j), q)

                    if s == 2 and not start:
                        out_lo(i - 1, j)
                    sums(0)
                    if more:
                        prep(j, i + (nb + 1))
                        prep(2 + j, i + (nb + 1))
                    sums(2)
                    prep(6 + j, i + nb3)
                    if not first:
                        if s == 2:
                            copy_out(T - 1)
                        elif j:
                            out_lo(i, 0)
                        else:
                            out_lo(i - 1, 1)
                    sums(4)

                    def between():
                        if s == 2 and not first:
                            norm_out(T - 1)
                        sums(6)

                    softmax(T, i * 2 + j, between)
                    if more:
                        prep(4 + j, i + (nb + 1))

                def both(i, more):
                    step(i, 0, more)
                    step(i, 1, more)

                sweep(dve, 1, NI_A, s, both)
                T = hb + H
                if s == 2:
                    out_lo(NI_A - 1, 0)
                    copy_out(T - 1)
                    norm_out(T - 1)
                out_lo(NI_A - 1, 1)

            def lam_and_gain():
                dve.wait_ge(lam_loaded, 16)
                lam = lam_in.rearrange("p (a b n) -> p a b n", a=2, b=2)
                dve.tensor_tensor(lam_pr.rearrange("p (a n) -> p a n", a=2), lam[:, :, 0, :], lam[:, :, 1, :],
                                  ALU.mult).then_inc(lam_seq, 1)
                dve.wait_ge(lam_seq, 1)
                dve.tensor_reduce(lamv, lam_pr.rearrange("p (a n) -> p a n", a=2), AX.X, ALU.add).then_inc(lam_seq, 1)
                dve.wait_ge(lam_exp, 1)
                dve.tensor_tensor(lamf[:, 1:2], lame[:, 0:1], lame[:, 1:2], ALU.subtract).then_inc(lam_seq, 1)
                dve.wait_ge(lam_seq, 3)
                dve.tensor_scalar(lamf[:, 0:1], lamf[:, 1:2], LAMBDA_INIT, None, ALU.add).then_inc(lam_seq, 1)
                dve.tensor_scalar(subg, cols[:, SUB:SUB + 1], (1.0 - LAMBDA_INIT) * 2 ** 0.5, None, ALU.mult).then_inc(lam_seq, 1)
                dve.wait_ge(lam_seq, 5)

            def gated(s):
                rb, fb, nb, nb2 = ROWS[s], STEPS[s], USE[s][0], USE[s][2]
                gate = gate_of[s]
                fdw = cols[:, FDW:FDW + 8 * FT].rearrange("p (a g t) -> p a g t", a=4, g=2)

                def step(i, j, more):
                    start = isinstance(i, int) and i == 0
                    t1 = i * 2 + (j + 1)
                    F = i * 2 + (fb + j)

                    def sums(q):
                        if s < 5:
                            gemv_step(s // 2 + 1, i, 4 * j + q)

                    if s == 5:
                        dve.tensor_scalar(taps[:, j, 0:8].rearrange("p (a g t) -> p a g t", a=4, g=2),
                                          fdw[:, :, :, bass.ds(i * 2 + j, 1)], 1.0, None,
                                          ALU.mult).then_inc(taps_ready, 1)
                    sums(0)
                    if not start:
                        prep(4 + j, i + nb2)
                    sums(1)
                    if s == 5:
                        g, u = work[:, 2 * j, :], work[:, 2 * j + 1, :]
                        gt, ut = gate[:, j, :], act32[:, j, :]
                        dve.wait_ge(taps_ready, t1 + 2 * KT)
                        dve.wait_ge(cv_g0, t1)
                        dve.scalar_tensor_tensor(gt[:, 1:S], g[:, 0:S - 1], taps[:, j, 2:3], gt[:, 1:S],
                                                 ALU.mult, ALU.add).then_inc(cv_seq, 1)
                        if more:
                            prep(j, i + (nb + 1))
                        n = i * 6 + 3 * j
                        dve.wait_ge(cv_seq, n + 1)
                        dve.scalar_tensor_tensor(gt[:, 2:S], g[:, 0:S - 2], taps[:, j, 0:1], gt[:, 2:S],
                                                 ALU.mult, ALU.add).then_inc(cv_g, 1)
                        dve.wait_ge(used[2 + j], i + (nb + 1))
                        dve.tensor_scalar(ut, u[:, 0:S], taps[:, j, 5:6], taps[:, j, 7:8], ALU.mult,
                                          ALU.add).then_inc(cv_seq, 1)
                        dve.wait_ge(cv_seq, n + 2)
                        dve.scalar_tensor_tensor(ut[:, 1:S], u[:, 0:S - 1], taps[:, j, 3:4], ut[:, 1:S],
                                                 ALU.mult, ALU.add).then_inc(cv_seq, 1)
                        dve.wait_ge(cv_seq, n + 3)
                        dve.scalar_tensor_tensor(ut[:, 2:S], u[:, 0:S - 2], taps[:, j, 1:2], ut[:, 2:S],
                                                 ALU.mult, ALU.add).then_inc(cv_u, 1)
                        dve.wait_ge(cv_u, t1)
                        dve.wait_ge(gate_done, F + 1)
                        dve.tensor_tensor(ut, ut, gt, ALU.mult).then_inc(act_done, 1)
                        if more:
                            prep(2 + j, i + (nb + 1))
                    else:
                        if more:
                            prep(j, i + (nb + 1))
                        sums(2)
                        dve.wait_ge(used[2 + j], i + (nb + 1))
                        dve.wait_ge(gate_done, F + 1)
                        dve.tensor_tensor(act32[:, j, :], work[:, 2 * j + 1, 0:S], gate[:, j, :],
                                          ALU.mult).then_inc(act_done, 1)
                        if more:
                            prep(2 + j, i + (nb + 1))
                        sums(3)
                    dve.wait_ge(ahi, i * 2 + (rb + j + 1))
                    dve.wait_ge(act_done, F + 1)
                    dve.tensor_tensor(a_lo[:, j, :], act32[:, j, :], a_hi[:, j, :].bitcast(F32),
                                      ALU.subtract).then_inc(alo, 1)

                def both(i, more):
                    step(i, 0, more)
                    step(i, 1, more)

                if s < 5:
                    gemv_start(s // 2 + 1)
                sweep(dve, 1, NI_F, s, both)

            def conformer():
                nb, fb = USE[4][0], STEPS[4]
                gate = gate_of[4]
                adw = cols[:, ADW:ADW + CONV * KT].rearrange("p (c t) -> p c t", t=KT)
                bias = cols[:, PW1B:PW1B + 3 * KT].rearrange("p (c t) -> p c t", t=KT)
                dve.memset(upad[:, :, 0:CONV - 1], 0.0).then_inc(pad_zero, 1)
                dve.wait_ge(pad_zero, 1)

                def step(i, j, more):
                    t = i * 2 + j
                    F = i * 2 + (fb + j)
                    dve.tensor_scalar(taps[:, j, 0:CONV].rearrange("p (c t) -> p c t", t=1),
                                      adw[:, :, bass.ds(t, 1)], 1.0, None, ALU.mult).then_inc(taps_ready, 1)
                    dve.tensor_scalar(taps[:, j, CONV:CONV + 3].rearrange("p (c t) -> p c t", t=1),
                                      bias[:, :, bass.ds(t, 1)], 1.0, None, ALU.mult).then_inc(taps_ready, 1)
                    if more:
                        prep(j, i + (nb + 1))
                    dve.wait_ge(taps_ready, i * 4 + (2 * j + 2))
                    dve.wait_ge(gate_done, F + 1)
                    u = upad[:, j, :]
                    dve.scalar_tensor_tensor(u[:, CONV - 1:PADW], work[:, 2 * j, 0:S], taps[:, j, 31:32],
                                             gate[:, j, :], ALU.add, ALU.mult).then_inc(act_done, 1)
                    if more:
                        prep(2 + j, i + (nb + 1))
                    dve.wait_ge(act_done, F + 1)
                    n = i * (2 * CONV) + CONV * j
                    for m in range(CONV):
                        w = taps[:, j, m:m + 1]
                        sums = cacc[:, m % 2, :]
                        if m == 0:
                            v = dve.tensor_scalar(sums, u[:, 0:S], w, taps[:, j, 33:34], ALU.mult, ALU.add)
                        elif m == 1:
                            v = dve.tensor_scalar(sums, u[:, 1:1 + S], w, None, ALU.mult)
                        else:
                            dve.wait_ge(tap_seq, n + (m - 1))
                            v = dve.scalar_tensor_tensor(sums, u[:, m:m + S], w, sums, ALU.mult, ALU.add)
                        v.then_inc(tap_seq, 1)
                    dve.wait_ge(tap_seq, n + CONV)
                    dve.tensor_tensor(convT[:, bass.ds(t, 1), :].rearrange("p a n -> p (a n)"),
                                      cacc[:, 0, :], cacc[:, 1, :], ALU.add).then_inc(conv_done, 1)

                def both(i, more):
                    step(i, 0, more)
                    step(i, 1, more)

                sweep(dve, 1, NI_C, 4, both)
                for t in range(TT):
                    for f in range(2):
                        dve.wait_ge(cT_mm, 2 * t + f + 1)
                        at = (2 * t + f) * 6
                        dve.bn_stats(bnst[:, at:at + 6], work[:, 2 * t + f, :]).then_inc(bn_done, 1)
                    dve.wait_ge(bn_done, 2 * t + 2)
                    dve.bn_aggr(bnag[:, 2 * t:2 * t + 2], bnst[:, 12 * t:12 * t + 12]).then_inc(ag_done, 1)
                for t in range(TT):
                    dve.wait_ge(lr_done, t + 1)
                    dve.tensor_scalar(xs[:, t, :], work[:, 2 * t:2 * t + 2, :].rearrange("p a b -> p (a b)"),
                                      bnag[:, 2 * t:2 * t + 1], lnr[:, t:t + 1], ALU.subtract,
                                      ALU.mult).then_inc(z_done, 1)
                for b in range(4):
                    hs = slice(2 * b, 2 * b + 2)
                    dve.wait_ge(ln_act, b + 1)
                    high = h_hi[:, hs, :].rearrange("p k n -> p (k n)")
                    dve.tensor_copy(high, work[:, b, :]).then_inc(p_hi, 1)
                    dve.wait_ge(p_hi, b + 1)
                    dve.tensor_tensor(h_lo[:, hs, :].rearrange("p k n -> p (k n)"), work[:, b, :],
                                      high.bitcast(F32), ALU.subtract).then_inc(p_lo, 1)
                for p in (2, 3):
                    for j in range(2):
                        prep(2 * p + j, USE[4][p] + 1)
                dve.wait_ge(b2_loaded, 16)
                for t in range(TT):
                    for f in range(2):
                        if t == 0:
                            dve.wait_ge(y0_done, 5)
                        else:
                            dve.wait_ge(used[7], USE[4][3] + 2)
                        yt = Y[:, 2 * t + f, :]
                        v = dve.tensor_tensor(yt, yt, b2row[:, f * 512:(f + 1) * 512], ALU.add)
                    v.then_inc(yb, 1)

            columns(0)
            for s in range(LAST + 1):
                if s and s % 2 == 0:
                    columns(s)
                pre_norm(s)
                if s in (2, 4, 5):
                    for j in range(2):
                        prep(4 + j, USE[s][2])
                if s == 4:
                    for j in range(2):
                        prep(6 + j, USE[4][3])
                if s in (2, 4):
                    for q in range(KT):
                        gemv_step(s // 2, NBLK - 1, q)
                if s in (0, 2):
                    if s == 0:
                        dve.wait_ge(bias_loaded, 32)
                    else:
                        lam_and_gain()
                    attention(s)
                    post_norm(s, 7, USE[s][3] + NI_A - 1)
                elif s == 4:
                    conformer()
                    post_norm(s, 7, USE[4][3] + 1)
                else:
                    gated(s)
                    post_norm(s, 5, USE[s][2] + NI_F - 1)


def relative_constants():
    import math

    import numpy as np

    buckets, exact, far = 32, 16, 2048
    rel = (S - 1) - np.arange(REL)
    n = np.maximum(rel, 0)
    nf = np.maximum(n, 1).astype(np.float32)
    large = exact + (np.log(nf / np.float32(exact)) / np.float32(math.log(far / exact))
                     * np.float32(buckets - exact)).astype(np.int32)
    bucket = np.where(n < exact, n, np.minimum(large, buckets - 1))
    onehot = ((np.arange(buckets)[:, None] == bucket[None, :]) & (rel >= 0)).astype(np.float32)
    fill = np.broadcast_to(np.where(rel >= 0, 0.0, -1e30).astype(np.float32), (H, REL))
    return np.ascontiguousarray(onehot), np.ascontiguousarray(fill)


_INS = ["x", "c", "rel_bias", "ada_w", "ada_b", "norm_g", "moba_w_qkv", "moba_w_o", "diff_w_qkv",
        "diff_w_o", "diff_lambda", "diff_subln_g", "ffn_w_in", "ffn_w_out", "c_2", "mod_w_2", "mod_b_2",
        "norm_pre_mix_2", "norm_post_mix_2", "norm_pre_ffn_2", "norm_post_ffn_2", "a_pw1_w_2",
        "a_pw1_b_2", "a_dw_w_2", "a_dw_b_2", "a_ln_g_2", "a_ln_b_2", "a_pw2_w_2", "a_pw2_b_2",
        "f_up_w_2", "f_dw_w_2", "f_dw_b_2", "f_down_w_2"]


def kernel(**inputs):
    import numpy as np
    import concourse.bacc as bacc
    from concourse.bass_utils import run_bass_kernel_spmd

    nc = bacc.Bacc("TRN2", target_bir_lowering=False, num_devices=1)
    arrays, args = {}, []
    given = {name: np.ascontiguousarray(inputs[name]) for name in _INS}
    given["bucket_onehot"], given["causal_fill"] = relative_constants()
    for name, a in given.items():
        arrays[f"in_{name}"] = a
        args.append(nc.dram_tensor(f"in_{name}", a.shape, mybir.dt.from_np(a.dtype), kind="ExternalInput").ap())
    out = nc.dram_tensor("out", (1, S, D), F32, kind="ExternalOutput").ap()
    build(nc, *args, out)
    r = run_bass_kernel_spmd(nc, [arrays], core_ids=[0])
    return r.results[0]["out"]
```

```python
from contextlib import ExitStack

import concourse.bass as bass
from concourse import mybir

F32 = mybir.dt.float32
F32R = mybir.dt.float32r
ALU = mybir.AluOpType
ACT = mybir.ActivationFunctionType
AX = mybir.AxisListType

P = 128
S = 256
D = 1024
H = 8
KT = D // P
TT = S // P
FT = 22
FF = FT * P
CONV = 31
NP = 13
EPS, LN_EPS = 1e-6, 1e-5
LAMBDA_INIT = 0.8 - 0.6 * 0.7408182206817179
REL = 384
BLK = 512
NBLK = 6 * D // BLK
PADW = S + CONV - 1
LAST = 5

NORM, PW1B, DWB, LNG, LNB, SUB = 0, 48, 64, 72, 80, 88
FDW, ADW = 89, 89 + 8 * FT
COLS = ADW + CONV * KT
PAR_ROWS = (16, 89, 4 * FT, 4 * FT, 16 * KT, 15 * KT)

USE = {0: (0, 0, 0, 0), 1: (4, 4, 4, 4), 2: (15, 15, 15, 4), 3: (19, 19, 19, 8),
       4: (30, 30, 30, 8), 5: (34, 34, 32, 10)}
ROWS = {0: 0, 1: 8, 2: 30, 3: 38, 5: 60}
STEPS = {1: 0, 3: 22, 4: 44, 5: 52}
HEADS = {0: 0, 2: 8}
NI_A, NI_F, NI_C = H // 2, FT // 2, KT // 2


def build(nc, x, c, rel_bias, ada_w, ada_b, norm_g, moba_w_qkv, moba_w_o, diff_w_qkv, diff_w_o,
          diff_lambda, diff_subln_g, ffn_w_in, ffn_w_out, c_2, mod_w_2, mod_b_2, norm_pre_mix_2,
          norm_post_mix_2, norm_pre_ffn_2, norm_post_ffn_2, a_pw1_w_2, a_pw1_b_2, a_dw_w_2, a_dw_b_2,
          a_ln_g_2, a_ln_b_2, a_pw2_w_2, a_pw2_b_2, f_up_w_2, f_dw_w_2, f_dw_b_2, f_down_w_2,
          bucket_onehot, causal_fill, out):
    with ExitStack() as ctx:
        def sb(name, shape, dt=F32):
            return ctx.enter_context(nc.sbuf_tensor(name, shape, dt))

        def sem(name):
            return ctx.enter_context(nc.semaphore(name))

        rel_rows = nc.dram_tensor("rel_rows", (H, P, REL), F32, kind="Internal").ap()

        raw = sb("raw", [P, 8, D])
        whi = sb("whi", [P, 8, D], F32R)
        wlo = sb("wlo", [P, 8, D], F32R)
        ada_raw = sb("ada_raw", [P, 4, 2, BLK])
        acc = sb("acc", [P, 6 * D])
        xt = sb("xt", [P, TT, D])
        xs = sb("xs", [P, TT, D])
        h_hi = sb("h_hi", [P, KT, S], F32R)
        h_lo = sb("h_lo", [P, KT, S], F32R)
        head_bias = sb("head_bias", [P, H, REL])
        Ga = sb("Ga", [P, D])
        Gf = sb("Gf", [P, D])
        ab_hi = sb("ab_hi", [P, 2, PADW], F32R)
        ab_lo = sb("ab_lo", [P, 2, PADW], F32R)
        mix = sb("mix", [P, 2688])
        cols = sb("cols", [P, COLS])
        csil = sb("csil", [P, 16])
        colA = sb("colA", [P, KT])
        colB = sb("colB", [P, KT])
        taps = sb("taps", [P, 2, 72])
        ident = sb("ident", [P, P])
        ones = sb("ones", [P, P])
        small = sb("small", [P, 96])
        relt = sb("relt", [32, H])
        Y = ctx.enter_context(nc.psum_tensor("Y", [P, 4, 512], F32))
        work = ctx.enter_context(nc.psum_tensor("work", [P, 4, 512], F32))

        a_hi, a_lo = ab_hi[:, :, 0:S], ab_lo[:, :, 0:S]
        u_hi, u_lo = ab_hi, ab_lo
        qk = mix[:, 0:512]
        vv = mix[:, 512:1024].rearrange("p (t n) -> p t n", t=TT)
        pr = mix[:, 1024:1792].rearrange("p (c n) -> p c n", c=2)
        pT = mix[:, 1792:2176]
        oraw = mix[:, 2176:2432]
        osc = mix[:, 2432:2688]
        lam_in, lam_pr = oraw, osc[:, 0:128]
        gate_of = {n: mix[:, at:at + 2 * S].rearrange("p (j n) -> p j n", j=2)
                   for n, at in ((1, 0), (3, 0), (5, 0), (4, 2176))}
        act32 = mix[:, 512:512 + 2 * S].rearrange("p (j n) -> p j n", j=2)
        upad = mix[:, 0:2 * PADW].rearrange("p (j n) -> p j n", j=2)
        cacc = mix[:, 576:576 + 2 * S].rearrange("p (j n) -> p j n", j=2)
        b2row = mix[0:1, 1152:1152 + D]
        ln_mean = mix[:, 0:S]
        ln_diag = mix[:, 576:576 + S].rearrange("p (t n) -> p t n", t=TT)
        convT = head_bias[:, :, 0:S]
        tap_hi = head_bias[:, :, S:S + CONV]
        tap_lo = head_bias[:, :, S + 32:S + 32 + CONV]
        tap_parts = head_bias[:, :, S:S + 64].rearrange("p t (w c) -> p t w c", w=2)[:, :, :, 0:NP]
        part = xs[:, :, 576:576 + S]
        diag = [w[:, 6:8, :].rearrange("p u (m n) -> p (u m) n", n=P) for w in (whi, wlo)]
        prow = xs[:, 0, 0:6 * P].rearrange("p (g n) -> p g n", g=6)
        onehot = xs[0:32, 1, 0:REL]
        relrow = xs[0:H, 1, REL:2 * REL]
        par_bank = [Y[:, 3, :], work[:, 0, :], work[:, 1, :], work[:, 2, :], Y[:, 1, :], Y[:, 2, :]]
        ssx, msx, rsx = small[:, 0:2], small[:, 2:4], small[:, 4:6]
        ssy, msy, rsy = small[:, 6:8], small[:, 8:10], small[:, 10:12]
        mhalf, eps2 = small[:, 12:13], small[:, 13:14]
        mmax, mneg = small[:, 14:18], small[:, 18:22]
        msum, mrec = small[:, 22:26], small[:, 26:30]
        lrec = small[:, 30:32]
        sso, mso, rso = small[:, 32:34], small[:, 34:36], small[:, 36:38]
        subg = small[:, 38:39]
        lamv, lame, lamf = small[:, 40:42], small[:, 42:44], small[:, 44:46]
        lneps, ln_ms, ln_rs = small[:, 48:49], small[:, 50:52], small[:, 52:54]

        ld = [sem(f"unit_loaded{u}") for u in range(8)]
        hi = [sem(f"unit_hi{u}") for u in range(8)]
        lo = [sem(f"unit_lo{u}") for u in range(8)]
        used = [sem(f"unit_multiplied{u}") for u in range(8)]
        ada_ld = [sem(f"ada_loaded{k}") for k in range(4)]
        gemv = sem("gemv_steps")
        acc_zero, acc_bias = sem("acc_zero"), sem("acc_bias")
        c_loaded, par_loaded, x_loaded = sem("c_loaded"), sem("par_loaded"), sem("x_loaded")
        rel_loaded, rel_mm, rel_row = sem("rel_loaded"), sem("rel_mm"), sem("rel_row")
        rel_stored, bias_loaded = sem("rel_stored"), sem("bias_loaded")
        lam_loaded, lam_seq, lam_exp = sem("lam_loaded"), sem("lam_seq"), sem("lam_exp")
        b2_loaded, gain_loaded = sem("b2_loaded"), sem("gain_loaded")
        id_zero, consts = sem("id_zero"), sem("consts")
        par_T, cols_ready, csil_ready = sem("par_T"), sem("cols_ready"), sem("csil_ready")
        ssx_done, msx_done, rsx_done = sem("ssx_done"), sem("msx_done"), sem("rsx_done")
        ssy_done, msy_done, rsy_done = sem("ssy_done"), sem("msy_done"), sem("rsy_done")
        xs0, xs1 = sem("xs0_ready"), sem("xs1_ready")
        hT, h32v, h32a, hhi, hlo = sem("hT"), sem("h32v"), sem("h32a"), sem("h_hi_done"), sem("h_lo_done")
        x_ready, y0_done, y_tmp = sem("x_ready"), sem("y0_done"), sem("y_tmp")
        mod_cols, mod_cols_used = sem("mod_cols"), sem("mod_cols_used")
        mod_ga, mod_gf = sem("mod_ga"), sem("mod_gf")
        mod_ga_used, mod_gf_used = sem("mod_ga_used"), sem("mod_gf_used")
        gate_done, act_done = sem("gate_done"), sem("act_done")
        ahi, alo = sem("a_hi_done"), sem("a_lo_done")
        taps_ready = sem("taps_ready")
        cv_g0, cv_g, cv_u, cv_seq = sem("cv_g0"), sem("cv_g"), sem("cv_u"), sem("cv_seq")
        qk_ev, s_mm, sb_done, mx_done = sem("qk_ev"), sem("s_mm"), sem("sb_done"), sem("mx_done")
        ng_done, ex_done, rc_done = sem("ng_done"), sem("ex_done"), sem("rc_done")
        p_done, pT_mm, pT_ev = sem("p_done"), sem("pT_mm"), sem("pT_ev")
        pv_mm, v_ev = sem("pv_mm"), sem("v_ev")
        ocp, oss, oms, ors = sem("ocp"), sem("oss"), sem("oms"), sem("ors")
        osn, oT_mm, dif_seq = sem("osn"), sem("oT_mm"), sem("dif_seq")
        pad_zero, tap_seq, conv_done = sem("pad_zero"), sem("tap_seq"), sem("conv_done")
        thi, tlo = sem("taps_hi_done"), sem("taps_lo_done")
        uhi, ulo = sem("u_hi_done"), sem("u_lo_done")
        diag_done, diag_used, part_done = sem("diag_done"), sem("diag_multiplied"), sem("part_done")
        mean_mm, mean_done, d_done = sem("mean_mm"), sem("mean_done"), sem("d_done")
        sq_done, var_mm, lms_done, lrs_done = sem("sq_done"), sem("var_mm"), sem("lms_done"), sem("lrs_done")
        ln_dg, lrs_mm = sem("ln_diag_done"), sem("lrs_mm")
        z_done, ln_act, p_hi, p_lo = sem("z_done"), sem("ln_act"), sem("p_hi"), sem("p_lo")
        stored = sem("stored")

        block = ctx.enter_context(nc.Block())

        def need(eng, s, v):
            if not (isinstance(v, int) and v <= 0):
                eng.wait_ge(s, v)

        def sweep(eng, peel, n, s, body):
            for i in range(peel):
                body(i, True)
            end = n - 1 if s == LAST else n
            if end - peel > 1:
                with eng.Fori(peel, end) as i:
                    body(i, True)
            elif end > peel:
                body(peel, True)
            if s == LAST:
                body(n - 1, False)

        qkv_w = {0: moba_w_qkv, 2: diff_w_qkv}
        o_w = {0: moba_w_o, 2: diff_w_o}
        in_w = {1: ffn_w_in[0], 3: ffn_w_in[1], 5: f_up_w_2[0]}
        out_w = {1: ffn_w_out[0], 3: ffn_w_out[1], 5: f_down_w_2[0]}
        ada = [ada_w[0], ada_w[1], mod_w_2[0]]
        scale_of = {0: P ** -0.5, 2: (P // 2) ** -0.5}

        @block.sync
        def _(sp):
            def load(u, n, src):
                need(sp, hi[u], n)
                need(sp, lo[u], n)
                dst = raw[:, u, :]
                if len(src.shape) == 3:
                    dst = dst.rearrange("p (k n) -> p k n", k=KT)
                sp.dma_start(dst, src).then_inc(ld[u], 16)

            def col_unit(w, at):
                return w[:, bass.ds(at, P)].rearrange("(k p) n -> p k n", p=P)

            def row_unit(w, at):
                return w[bass.ds(at, P), :]

            def unit(s, p, i, j):
                at = i * (2 * P) + j * P
                if s in (0, 2):
                    src = col_unit(qkv_w[s][0], at + p * D) if p < 3 else row_unit(o_w[s][0], at)
                elif s == 4:
                    src = col_unit(a_pw1_w_2[0], at + p * D)
                else:
                    src = col_unit(in_w[s], at + p * FF) if p < 2 else row_unit(out_w[s], at)
                load(2 * p + j, i + USE[s][p], src)

            def pw2_pair(r, p, n):
                for j in range(2):
                    load(2 * p + j, n, row_unit(a_pw2_w_2[0], (2 * r + j) * P))

            def ada_quarters(layer, b, ks):
                m8 = (b + NBLK * layer) * 8
                for k in ks:
                    need(sp, gemv, m8 + (2 * k - 6))
                    sp.dma_start(ada_raw[:, k, :, :],
                                 ada[layer][k * 2 * P:(k + 1) * 2 * P, bass.ds(b * BLK, BLK)]
                                 .rearrange("(k p) n -> p k n", p=P)).then_inc(ada_ld[k], 16)

            def ada_block(layer, b):
                ada_quarters(layer, b, range(4))

            def units(s, slots, i, j):
                for p in slots:
                    unit(s, p, i, j)

            ada_block(0, 0)
            for p in range(3):
                ada_block(0, p + 1)
                units(0, (p,), 0, 0)
                units(0, (p,), 0, 1)
            for s in range(LAST + 1):
                more = s < LAST
                if s in (0, 2):
                    def attention_loads(i, j):
                        if isinstance(i, int) and i == NI_A:
                            if more:
                                units(s + 1, (0, 1), 0, j)
                            unit(s, 3, i - 1, j)
                            if more:
                                unit(s + 1, 2, 0, j)
                        else:
                            units(s, (0, 1), i, j)
                            unit(s, 3, i - 1, j)
                            unit(s, 2, i, j)
                        if s == 0:
                            ada_block(0, i * 2 + (j + 2))

                    with sp.Fori(1, NI_A) as i:
                        attention_loads(i, 0)
                        attention_loads(i, 1)
                    attention_loads(NI_A, 0)
                    attention_loads(NI_A, 1)
                elif s == 4:
                    with sp.Fori(1, NI_C) as i:
                        units(4, (0, 1), i, 0)
                        units(4, (0, 1), i, 1)
                    if more:
                        units(5, (0, 1), 0, 0)
                        units(5, (0, 1), 0, 1)
                    pw2_pair(2, 2, USE[4][2] + 1)
                    pw2_pair(3, 3, USE[4][3] + 1)
                    if more:
                        units(5, (2,), 0, 0)
                        units(5, (2,), 0, 1)
                else:
                    def ffn_loads(i, j):
                        if s < 5:
                            ada_quarters(s // 2 + 1, i - 1, (2 * j, 2 * j + 1))
                        if not (isinstance(i, int) and i == 1):
                            unit(s, 2, i - 1, j)
                        if not (isinstance(i, int) and i == NI_F):
                            units(s, (0, 1), i, j)
                        elif more:
                            units(s + 1, (0, 1), 0, j)

                    ffn_loads(1, 0)
                    ffn_loads(1, 1)
                    with sp.Fori(2, NI_F) as i:
                        ffn_loads(i, 0)
                        ffn_loads(i, 1)
                    ffn_loads(NI_F, 0)
                    ffn_loads(NI_F, 1)
                    if more:
                        if s == 1:
                            units(2, (2,), 0, 0)
                            units(2, (2,), 0, 1)
                        else:
                            pw2_pair(0, 2, USE[4][2])
                            pw2_pair(1, 3, USE[4][3])
                        ada_block(s // 2 + 1, NBLK - 1)
            for t in range(TT):
                sp.wait_ge(x_ready, 2 * LAST + t + 1)
                sp.dma_start(out[0, t * P:(t + 1) * P, :], xt[:, t, :]).then_inc(stored, 16)
            sp.wait_ge(stored, 16 * TT)

        @block.gpsimd
        def _(pool):
            pool.memset(ident[:], 0.0).then_inc(id_zero, 1)
            pool.wait_ge(id_zero, 1)
            pool.affine_select(out=ident[:], in_=ident[:], compare_op=ALU.not_equal, fill=1.0, base=0,
                               pattern=[[-1, P]], channel_multiplier=1).then_inc(consts, 1)
            pool.memset(ones[:], 1.0).then_inc(consts, 1)
            pool.memset(mhalf, -0.5).then_inc(consts, 1)
            pool.memset(eps2, 2 * EPS).then_inc(consts, 1)
            pool.memset(lneps, LN_EPS).then_inc(consts, 1)

            def row(src):
                return bass.AP(src.tensor, src.offset, [[0, P], [1, D]])

            def acc_init(layer):
                if layer:
                    pool.wait_ge(mod_gf, 2 * layer)
                pool.memset(acc[:], 0.0).then_inc(acc_zero, 1)
                pool.wait_ge(acc_zero, layer + 1)
                bias = ada_b[layer:layer + 1, :] if layer < 2 else mod_b_2[0:1, :]
                pool.dma_start(acc[0:1, :], bias).then_inc(acc_bias, 16)

            def gains(layer):
                need(pool, x_ready, 4 * layer)
                post = ((norm_g[layer, 1], norm_g[layer, 3]) if layer < 2
                        else (norm_post_mix_2[0], norm_post_ffn_2[0]))
                for g, src in zip((Ga, Gf), post):
                    pool.dma_start(g[:], row(src)).then_inc(gain_loaded, 16)
                if layer == 2:
                    pool.dma_start(b2row, a_pw2_b_2[0:1, :]).then_inc(b2_loaded, 16)

            def rstd(ss, ms, rs, ss_done, ms_done, rs_done, at, t):
                pool.wait_ge(ss_done, at + 1)
                pool.tensor_scalar(ms[:, t:t + 1], ss[:, t:t + 1], EPS, None, ALU.add).then_inc(ms_done, 1)
                pool.wait_ge(ms_done, at + 1)
                pool.tensor_tensor(rs[:, t:t + 1], ms[:, t:t + 1], mhalf, ALU.pow).then_inc(rs_done, 1)

            acc_init(0)
            pool.wait_ge(consts, 5)
            for s in range(LAST + 1):
                for t in range(TT):
                    rstd(ssx, msx, rsx, ssx_done, msx_done, rsx_done, 2 * s + t, t)
                if s % 2 == 0:
                    gains(s // 2)
                elif s < 5:
                    acc_init(s // 2 + 1)
                if s == 2:
                    def head_rstd(i):
                        for at in range(2 * TT):
                            t = at % TT
                            pool.wait_ge(oss, i * 4 + at + 1)
                            pool.tensor_tensor(mso[:, t:t + 1], sso[:, t:t + 1], eps2, ALU.add).then_inc(oms, 1)
                            pool.wait_ge(oms, i * 4 + at + 1)
                            pool.tensor_tensor(rso[:, t:t + 1], mso[:, t:t + 1], mhalf, ALU.pow)\
                                .then_inc(ors, 1)
                    with pool.Fori(0, NI_A) as i:
                        head_rstd(i)
                if s == 4:
                    pool.wait_ge(lms_done, 1)
                    pool.tensor_tensor(ln_rs, ln_ms, mhalf.broadcast_to([P, TT]), ALU.pow).then_inc(lrs_done, 1)
                for t in range(TT):
                    rstd(ssy, msy, rsy, ssy_done, msy_done, rsy_done, 2 * s + t, t)

        @block.tensor
        def _(pe):
            def col_product(dst, u, n, early=None):
                pe.wait_ge(lo[u], n + 1)
                for k in range(KT):
                    if early is not None and k % 2 == 0:
                        pe.wait_ge(hlo, 4 * early + k // 2 + 1)
                    ws = slice(k * P, (k + 1) * P)
                    for m, (w, h) in enumerate(((whi, h_hi), (whi, h_lo), (wlo, h_hi))):
                        mm = pe.matmul(dst, w[:, u, ws], h[:, k, :], start=(k == 0 and m == 0),
                                       stop=(k == KT - 1 and m == 2))
                mm.then_inc(used[u], 1)

            def row_product(a_h, a_l, u, n, first=False, end=False):
                pe.wait_ge(lo[u], n + 1)
                for t in range(TT):
                    ts = slice(t * P, (t + 1) * P)
                    for m, (a, w) in enumerate(((a_h, whi), (a_h, wlo), (a_l, whi))):
                        for f in range(2):
                            mm = pe.matmul(Y[:, 2 * t + f, :], a[:, ts], w[:, u, f * 512:(f + 1) * 512],
                                           start=(first and m == 0), stop=(end and m == 2))
                    if t == 0 and end:
                        mm.then_inc(y0_done, 1)
                mm.then_inc(used[u], 1)

            def mod_columns(base):
                for m in range(2 * KT):
                    mm = pe.matmul(work[:, 3, m:m + 1], acc[:, base + m * P:base + (m + 1) * P],
                                   ones[:, 0:1], start=True, stop=True)
                mm.then_inc(mod_cols, 1)

            def mod_first(layer):
                pe.wait_ge(gemv, 8 * (NBLK * layer + 4))
                mod_columns(0)

            def mod_rest(layer):
                pe.wait_ge(gemv, 8 * NBLK * (layer + 1))
                for f in range(2):
                    mm = pe.matmul(work[:, f, :], ones[:], acc[:, 2 * D + f * 512:2 * D + (f + 1) * 512],
                                   start=True, stop=True)
                mm.then_inc(mod_ga, 1)
                mod_columns(3 * D)
                pe.matmul(work[:, 2, :], ones[:], acc[:, 5 * D:5 * D + 512],
                          start=True, stop=True).then_inc(mod_gf, 1)
                pe.wait_ge(mod_cols_used, 2 * layer + 2)
                pe.matmul(work[:, 3, :], ones[:], acc[:, 5 * D + 512:6 * D],
                          start=True, stop=True).then_inc(mod_gf, 1)

            def pre_norm(s):
                pe.wait_ge(mod_cols_used, s + 1)
                if s % 2:
                    pe.wait_ge(mod_ga_used, s // 2 + 1)
                    pe.wait_ge(mod_gf_used, s // 2 + 1)
                for t in range(TT):
                    pe.wait_ge((xs0, xs1)[t], s + 1)
                    for k in range(KT):
                        at = (k % 2) * S + t * P
                        mm = pe.transpose(work[:, k // 2, at:at + P], xs[:, t, k * P:(k + 1) * P], ident[:])
                        if t == TT - 1 and k % 2:
                            mm.then_inc(hT, 1)

            pe.wait_ge(consts, 5)
            for g, rows in enumerate(PAR_ROWS):
                if g == 0:
                    pe.wait_ge(c_loaded, 32)
                elif g == 1:
                    pe.wait_ge(par_loaded, 16 * 16)
                pe.transpose(par_bank[g][:, 0:rows], prow[0:rows, g, :],
                             ident[0:rows, 0:rows]).then_inc(par_T, 1)
            pe.wait_ge(rel_loaded, 48)
            pe.matmul(Y[0:H, 0, 0:REL], relt[:], onehot, start=True, stop=True).then_inc(rel_mm, 1)

            def attention(s):
                hb, rb, nb, nb3 = HEADS[s], ROWS[s], USE[s][0], USE[s][3]

                def head_out_T(T, end=False):
                    pe.wait_ge(osn, (T - hb) * 2 + 2)
                    if not end:
                        pe.wait_ge(sb_done, (T - hb) * 2 + (4 + HEADS[2]))
                    for t in range(TT):
                        mm = pe.transpose(work[:, 2, t * P:(t + 1) * P], osc[:, t * P:(t + 1) * P], ident[:])
                    mm.then_inc(oT_mm, 1)

                def probs_T(T):
                    pe.wait_ge(p_done, T * 2 + 2)
                    for m in range(3):
                        mm = pe.transpose(work[:, 3, m * P:(m + 1) * P], pr[:, 0, m * P:(m + 1) * P], ident[:])
                    mm.then_inc(pT_mm, 1)

                def head_values(i, j):
                    pe.wait_ge(pT_ev, i * 2 + (hb + j + 1))
                    pe.wait_ge(v_ev, i + (hb // 2 + 1))
                    v0, v1 = (vv[:, t, j * P:(j + 1) * P] for t in range(TT))
                    if s == 0:
                        pe.matmul(work[:, 1, 0:P], v0, pT[:, 0:P], start=True, stop=True)
                        pe.matmul(work[:, 1, P:S], v0, pT[:, P:S], start=True, stop=False)
                        mm = pe.matmul(work[:, 1, P:S], v1, pT[:, S:3 * P], start=False, stop=True)
                    else:
                        pe.matmul(work[:, 1, 0:P], pT[:, 0:P], v0, start=True, stop=True)
                        pe.matmul(work[:, 1, P:S], pT[:, P:S], v0, start=True, stop=False)
                        mm = pe.matmul(work[:, 1, P:S], pT[:, S:3 * P], v1, start=False, stop=True)
                    mm.then_inc(pv_mm, 1)

                def scores(T):
                    pe.wait_ge(qk_ev, T + 1)
                    if s == 0:
                        need(pe, sb_done, T)
                        pe.matmul(work[:, 2, 0:P], qk[:, 0:P], qk[:, S:S + P], start=True, stop=True)
                        mm = pe.matmul(work[:, 2, P:3 * P], qk[:, P:S], qk[:, S:2 * S], start=True, stop=True)
                    else:
                        need(pe, alo, T - hb + (rb - 1))
                        for g in range(2):
                            half = slice(g * 64, (g + 1) * 64)
                            pe.matmul(work[:, 2 + g, 0:P], qk[half, 0:P], qk[half, S:S + P],
                                      start=True, stop=True)
                            mm = pe.matmul(work[:, 2 + g, P:3 * P], qk[half, P:S], qk[half, S:2 * S],
                                           start=True, stop=True)
                    mm.then_inc(s_mm, 1)

                def values(T, n):
                    pe.wait_ge(lo[4], n + 1)
                    pe.wait_ge(lo[5], n + 1)
                    if s == 0:
                        need(pe, alo, T - hb + rb)
                    else:
                        need(pe, ocp, T - hb)
                    for t, units in ((0, (4, 6)), (1, (4, 5)), (1, (5, 6))):
                        ts = slice(t * P, (t + 1) * P)
                        u0, u1 = units
                        dst = work[:, 1, t * S + (u0 - 4) * P:t * S + (u1 - 4) * P]
                        for k in range(KT):
                            ws = slice(k * P, (k + 1) * P)
                            for m, (h, w) in enumerate(((h_hi, whi), (h_lo, whi), (h_hi, wlo))):
                                mm = pe.matmul(dst, h[:, k, ts], w[:, u0:u1, ws],
                                               start=(k == 0 and m == 0), stop=(k == KT - 1 and m == 2))
                        if t:
                            mm.then_inc(used[u0], 1)

                def w_o(i, j, first=False, end=False):
                    pe.wait_ge(alo, i * 2 + (rb + j + 1))
                    row_product(a_hi[:, j, :], a_lo[:, j, :], 6 + j, i + nb3, first, end)

                def step(i, j):
                    T = i * 2 + (hb + j)
                    start = isinstance(i, int) and i == 0
                    if s == 2 and not start:
                        head_out_T(T - 2)
                    need(pe, qk_ev, T)
                    col_product(work[:, 0, 0:S], j, i + nb, s if start and j == 0 else None)
                    col_product(work[:, 0, S:2 * S], 2 + j, i + nb)
                    if not (start and j == 0):
                        probs_T(T - 1)
                    if not start:
                        w_o(i - 1, j, first=isinstance(i, int) and i == 1 and j == 0)
                    if j:
                        head_values(i, 0)
                    elif not start:
                        head_values(i - 1, 1)
                    scores(T)
                    if j == 0:
                        values(T, i + nb)

                for i in range(2):
                    step(i, 0)
                    step(i, 1)
                with pe.Fori(2, NI_A) as i:
                    step(i, 0)
                    step(i, 1)
                T = hb + H
                if s == 2:
                    head_out_T(T - 2)
                probs_T(T - 1)
                w_o(NI_A - 1, 0)
                head_values(NI_A - 1, 1)
                if s == 2:
                    head_out_T(T - 1, end=True)
                w_o(NI_A - 1, 1, end=True)

            def gated(s):
                rb, fb, nb, nb2 = ROWS[s], STEPS[s], USE[s][0], USE[s][2]

                def down(i, j, first=False, end=False):
                    pe.wait_ge(alo, i * 2 + (rb + j + 1))
                    row_product(a_hi[:, j, :], a_lo[:, j, :], 4 + j, i + nb2, first, end)

                def step(i, j):
                    start = isinstance(i, int) and i == 0
                    before = i * 2 + j - 1
                    if not start:
                        if s == 5:
                            pe.wait_ge(cv_g, before)
                        else:
                            pe.wait_ge(gate_done, before + fb)
                    col_product(work[:, 2 * j, 0:S], j, i + nb, s if start and j == 0 else None)
                    if not start:
                        if s == 5:
                            pe.wait_ge(cv_u, before)
                        else:
                            pe.wait_ge(act_done, before + fb)
                    col_product(work[:, 2 * j + 1, 0:S], 2 + j, i + nb)
                    if j == 1:
                        down(i, 0, first=start)
                    elif not start:
                        down(i - 1, 1)

                def both(i, more):
                    step(i, 0)
                    step(i, 1)

                sweep(pe, 1, NI_F, s, both)
                down(NI_F - 1, 1, end=True)

            def conformer():
                nb, fb = USE[4][0], STEPS[4]

                def conv(i, j):
                    T = i * 2 + j
                    pe.wait_ge(ulo, T + 1)
                    need(pe, conv_done, T - 1)
                    for m in range(NP):
                        pe.wait_ge(diag_done, T * NP + (m + 1))
                        for n, (w, u) in enumerate(((0, u_hi), (0, u_lo), (1, u_hi))):
                            mm = pe.matmul(Y[:, j, 0:S], diag[w][:, m, :], u[:, j, m:m + S],
                                           start=(m == 0 and n == 0), stop=(m == NP - 1 and n == 2))
                        mm.then_inc(diag_used, 1)

                def mean_sum(t, first=False, end=False):
                    pe.wait_ge(conv_done, t + 1)
                    mm = pe.matmul(Y[:, 2, 0:S], ones[:], convT[:, bass.ds(t, 1), :].rearrange("p a n -> p (a n)"),
                                   start=first, stop=end)
                    if end:
                        mm.then_inc(mean_mm, 1)

                def step(i, j):
                    start = isinstance(i, int) and i == 0
                    before = i * 2 + (j - 1 + fb)
                    if not start:
                        pe.wait_ge(act_done, before)
                    col_product(work[:, 2 * j, 0:S], j, i + nb, 4 if start and j == 0 else None)
                    if not start:
                        pe.wait_ge(gate_done, before)
                    col_product(work[:, 2 * j + 1, 0:S], 2 + j, i + nb)
                    if not start:
                        mean_sum(i * 2 + (j - 2), first=isinstance(i, int) and i == 1 and j == 0)
                    if j:
                        conv(i, 0)
                    elif not start:
                        conv(i - 1, 1)

                def both(i, more):
                    step(i, 0)
                    step(i, 1)

                sweep(pe, 2, NI_C, 4, both)
                conv(NI_C - 1, 1)
                mean_sum(KT - 2)
                mean_sum(KT - 1, end=True)
                for h in range(2):
                    pe.wait_ge(sq_done, h + 1)
                    for t in range(TT):
                        for k in range(4):
                            at = k * S + t * P
                            mm = pe.matmul(Y[:, 2 * t + 1, 0:1], xs[:, h, at:at + P], ones[:, 0:1],
                                           start=(h == 0 and k == 0), stop=(h == 1 and k == 3))
                mm.then_inc(var_mm, 1)
                pe.wait_ge(ln_dg, TT)
                for t in range(TT):
                    mm = pe.matmul(work[:, 0, t * P:(t + 1) * P], ones[:], ln_diag[:, t, :], start=True, stop=True)
                mm.then_inc(lrs_mm, 1)
                pe.wait_ge(b2_loaded, 16)
                pe.wait_ge(lms_done, 1)
                for t in range(TT):
                    for f in range(2):
                        pe.matmul(Y[:, 2 * t + f, :], ones[0:1, :], b2row[:, f * 512:(f + 1) * 512],
                                  start=True, stop=False)
                for k in range(KT):
                    r, j = k // 2, k % 2
                    pe.wait_ge(p_lo, r + 1)
                    row_product(h_hi[:, k, :], h_lo[:, k, :], 4 + 2 * (r % 2) + j,
                                USE[4][2 + r % 2] + r // 2, end=(k == KT - 1))

            mod_first(0)
            for s in range(LAST + 1):
                pre_norm(s)
                pe.wait_ge(x_ready, 2 * s) if s else pe.wait_ge(rel_row, 1)
                if s in (0, 2):
                    attention(s)
                elif s == 4:
                    conformer()
                else:
                    gated(s)
                if s % 2 == 0:
                    mod_rest(s // 2)
                elif s < LAST:
                    mod_first(s // 2 + 1)

        @block.scalar
        def _(act):
            def prep(u, n):
                act.wait_ge(ld[u], n * 16 + 16)
                need(act, used[u], n)
                act.activation(whi[:, u, :], raw[:, u, :], ACT.Copy).then_inc(hi[u], 1)

            def params(dst, src, s):
                act.dma_start(dst, src).then_inc(s, 16)

            def rows(src):
                return src.rearrange("a (r p) -> (a r) p", p=P)

            params(prow[0:8, 0, :], rows(c), c_loaded)
            params(prow[8:16, 0, :], rows(c_2), c_loaded)
            for t in range(TT):
                params(xt[:, t, :], x[0, t * P:(t + 1) * P, :], x_loaded)
            pre = [norm_g[0, 0:1], norm_g[0, 2:3], norm_g[1, 0:1], norm_g[1, 2:3], norm_pre_mix_2,
                   norm_pre_ffn_2, a_pw1_b_2, a_dw_b_2, a_ln_g_2, a_ln_b_2, diff_subln_g]
            at = 0
            for src in pre:
                r = src.shape[1] // P
                params(prow[at:at + r, 1, :], rows(src), par_loaded)
                at += r
            params(prow[0:4 * FT, 2, :], rows(f_dw_w_2[0, 0:2]), par_loaded)
            params(prow[0:2 * FT, 3, :], rows(f_dw_w_2[0, 2:3]), par_loaded)
            params(prow[2 * FT:4 * FT, 3, :], rows(f_dw_b_2), par_loaded)
            params(prow[0:16 * KT, 4, :], rows(a_dw_w_2[0, 0:16]), par_loaded)
            params(prow[0:15 * KT, 5, :], rows(a_dw_w_2[0, 16:CONV]), par_loaded)
            params(relt[:], rel_bias, rel_loaded)
            params(onehot, bucket_onehot, rel_loaded)
            params(relrow, causal_fill, rel_loaded)
            params(lam_in, bass.AP(diff_lambda.tensor, diff_lambda.offset, [[0, P], [1, 256]]), lam_loaded)

            act.wait_ge(par_T, 1)
            act.activation(csil[:], par_bank[0][:, 0:16], ACT.Silu).then_inc(csil_ready, 1)
            for u in range(4):
                prep(u, 0)
            act.wait_ge(rel_row, 1)
            act.dma_start(rel_rows, relrow.unsqueeze(1).broadcast_to([H, P, REL])).then_inc(rel_stored, 16)
            for u in range(4, 6):
                prep(u, 0)
            act.wait_ge(rel_stored, 16)
            for off, lo_c, hi_c in ((255, 0, P), (127, P, 3 * P)):
                src = bass.AP(rel_rows.tensor, rel_rows.offset + off, [[REL - 1, P], [P * REL, H], [1, hi_c - lo_c]])
                act.dma_start(head_bias[:, :, lo_c:hi_c], src).then_inc(bias_loaded, 16)

            def pre_norm(s):
                for t in range(TT):
                    if s == 0:
                        act.wait_ge(x_loaded, 32)
                        act.wait_ge(par_T, len(PAR_ROWS))
                    else:
                        act.wait_ge(x_ready, 2 * (s - 1) + t + 1)
                    act.activation(xs[:, t, :], xt[:, t, :], ACT.Square, scale=D ** -0.5,
                                   accum_out=ssx[:, t:t + 1]).then_inc(ssx_done, 1)
                act.wait_ge(rsx_done, 2 * s + 2)
                act.activation(xs[:, 1, :], xt[:, 1, :], ACT.Copy, scale=rsx[:, 1:2]).then_inc(xs1, 1)
                act.wait_ge(mod_cols_used, s + 1)
                def scaled(b):
                    act.wait_ge(hT, 4 * s + b + 1)
                    for k in (2 * b, 2 * b + 1):
                        bank = work[:, b, (k % 2) * S:(k % 2 + 1) * S]
                        a = act.activation(bank, bank, ACT.Identity, scale=colA[:, k:k + 1],
                                           bias=colB[:, k:k + 1])
                    a.then_inc(h32a, 1)
                def high(b):
                    act.wait_ge((h32v, h32a)[b % 2], 2 * s + b // 2 + 1)
                    act.activation(h_hi[:, 2 * b:2 * b + 2, :].rearrange("p k n -> p (k n)"), work[:, b, :],
                                   ACT.Copy).then_inc(hhi, 1)
                scaled(1)
                high(0)
                high(1)
                scaled(3)
                high(2)
                high(3)

            def post_norm(s, u, n):
                for t in range(TT):
                    if t == 0:
                        act.wait_ge(y0_done, s + 1)
                    else:
                        act.wait_ge(used[u], n + 1)
                    act.activation(xs[:, t, :], Y[:, 2 * t:2 * t + 2, :].rearrange("p a b -> p (a b)"),
                                   ACT.Square, scale=D ** -0.5,
                                   accum_out=ssy[:, t:t + 1]).then_inc(ssy_done, 1)

            def attention(s):
                hb, rb, nb, nb3 = HEADS[s], ROWS[s], USE[s][0], USE[s][3]
                ne = 2 if s == 0 else 4

                def probs_T(T):
                    act.wait_ge(pT_mm, T + 1)
                    need(act, pv_mm, T)
                    act.activation(pT, work[:, 3, 0:3 * P], ACT.Copy).then_inc(pT_ev, 1)

                def out_hi(i, j):
                    if s == 0:
                        act.wait_ge(pv_mm, i * 2 + (hb + j + 1))
                        src, by = work[:, 1, 0:S], 1.0
                    else:
                        act.wait_ge(oT_mm, i * 2 + (j + 1))
                        src, by = work[:, 2, 0:S], subg
                    need(act, used[6 + j], i + nb3)
                    act.activation(a_hi[:, j, :], src, ACT.Copy, scale=by).then_inc(ahi, 1)

                def squares(T):
                    act.wait_ge(ocp, T - hb + 1)
                    for t in range(TT):
                        need(act, oT_mm, T - hb)
                        act.activation(osc[:, t * P:(t + 1) * P], oraw[:, t * P:(t + 1) * P], ACT.Square,
                                       scale=0.125, accum_out=sso[:, t:t + 1]).then_inc(oss, 1)

                def step(i, j, more):
                    T = i * 2 + (hb + j)
                    start = isinstance(i, int) and i == 0
                    first = start and j == 0
                    if s == 2 and not start:
                        out_hi(i - 1, j)
                    act.wait_ge(used[2 + j], i + (nb + 1))
                    need(act, s_mm, T)
                    act.activation(qk, work[:, 0, :], ACT.Copy).then_inc(qk_ev, 1)
                    if not first:
                        probs_T(T - 1)
                    if more:
                        prep(j, i + (nb + 1))
                        prep(2 + j, i + (nb + 1))
                    prep(6 + j, i + nb3)
                    if not first:
                        if s == 2:
                            squares(T - 1)
                        elif j:
                            out_hi(i, 0)
                        else:
                            out_hi(i - 1, 1)
                    act.wait_ge(ng_done, T + 1)
                    for q, (a, b) in enumerate(((0, P), (P, 3 * P))):
                        for g in range(ne // 2):
                            m = q * (ne // 2) + g
                            act.activation(pr[:, g, a:b], pr[:, g, a:b], ACT.Exp, bias=mneg[:, m:m + 1],
                                           accum_out=msum[:, m:m + 1]).then_inc(ex_done, 1)
                    if j == 0:
                        act.wait_ge(used[5], i + (nb + 1))
                        need(act, pv_mm, T)
                        act.activation(mix[:, 512:1024], work[:, 1, :], ACT.Copy).then_inc(v_ev, 1)
                    if more:
                        prep(4 + j, i + (nb + 1))

                def both(i, more):
                    step(i, 0, more)
                    step(i, 1, more)

                if s == 2:
                    act.wait_ge(lam_seq, 2)
                    act.activation(lame, lamv, ACT.Exp).then_inc(lam_exp, 1)
                    act.wait_ge(lam_seq, 5)
                sweep(act, 1, NI_A, s, both)
                T = hb + H
                if s == 2:
                    out_hi(NI_A - 1, 0)
                probs_T(T - 1)
                if s == 2:
                    squares(T - 1)
                out_hi(NI_A - 1, 1)

            def gated(s):
                rb, fb, nb, nb2 = ROWS[s], STEPS[s], USE[s][0], USE[s][2]
                gate = gate_of[s]

                def step(i, j, more):
                    start = isinstance(i, int) and i == 0
                    F = i * 2 + (fb + j)
                    if not start:
                        prep(4 + j, i + nb2)
                    act.wait_ge(used[j], i + (nb + 1))
                    if not start:
                        act.wait_ge(act_done, F - 1)
                    if s == 5:
                        act.wait_ge(taps_ready, i * 2 + (3 * KT + j + 1))
                        act.activation(gate[:, j, :], work[:, 2 * j, 0:S], ACT.Identity, scale=taps[:, j, 4:5],
                                       bias=taps[:, j, 6:7]).then_inc(cv_g0, 1)
                        if more:
                            prep(j, i + (nb + 1))
                        act.wait_ge(cv_g, i * 2 + (j + 1))
                        act.activation(gate[:, j, :], gate[:, j, :], ACT.Silu).then_inc(gate_done, 1)
                    else:
                        act.activation(gate[:, j, :], work[:, 2 * j, 0:S], ACT.Silu).then_inc(gate_done, 1)
                        if more:
                            prep(j, i + (nb + 1))
                    if more:
                        prep(2 + j, i + (nb + 1))
                    act.wait_ge(act_done, F + 1)
                    need(act, used[4 + j], i + nb2)
                    act.activation(a_hi[:, j, :], act32[:, j, :], ACT.Copy).then_inc(ahi, 1)

                def both(i, more):
                    step(i, 0, more)
                    step(i, 1, more)

                sweep(act, 1, NI_F, s, both)

            def conformer():
                nb, fb = USE[4][0], STEPS[4]
                gate = gate_of[4]
                for j in range(2):
                    act.wait_ge(used[6 + j], USE[4][3])
                act.wait_ge(cols_ready, len(PAR_ROWS) - 1)
                act.activation(tap_hi.bitcast(F32R), cols[:, ADW:ADW + CONV * KT]
                               .rearrange("p (c t) -> p t c", t=KT), ACT.Copy).then_inc(thi, 1)

                def step(i, j, more):
                    start = isinstance(i, int) and i == 0
                    T = i * 2 + j
                    F = T + fb
                    if more:
                        prep(j, i + (nb + 1))
                    act.wait_ge(used[2 + j], i + (nb + 1))
                    act.wait_ge(taps_ready, i * 6 + (3 * j + 3))
                    if not start:
                        act.wait_ge(act_done, F - 1)
                    act.activation(gate[:, j, :], work[:, 2 * j + 1, 0:S], ACT.Sigmoid,
                                   bias=taps[:, j, 32:33]).then_inc(gate_done, 1)
                    if more:
                        prep(2 + j, i + (nb + 1))
                    act.wait_ge(act_done, F + 1)
                    need(act, diag_used, T * NP - NP)
                    act.activation(u_hi[:, j, :], upad[:, j, :], ACT.Copy).then_inc(uhi, 1)
                    for m in range(NP):
                        if not (start and j == 0):
                            act.wait_ge(diag_used, T * NP + (m + 1 - NP))
                        for w in range(2):
                            d = act.activation(diag[w][:, m, :], ident[:], ACT.Copy,
                                               scale=taps[:, j, 36 + w * NP + m:37 + w * NP + m])
                        d.then_inc(diag_done, 1)

                def both(i, more):
                    step(i, 0, more)
                    step(i, 1, more)

                sweep(act, 1, NI_C, 4, both)
                act.wait_ge(mean_mm, 1)
                act.activation(ln_mean, Y[:, 2, 0:S], ACT.Copy, scale=1.0 / D).then_inc(mean_done, 1)
                for h in range(2):
                    act.wait_ge(d_done, h + 1)
                    act.activation(xs[:, h, :].rearrange("p (k n) -> p k n", k=4), convT[:, 4 * h:4 * h + 4, :],
                                   ACT.Square).then_inc(sq_done, 1)
                act.wait_ge(diag_used, KT * NP)
                for j in range(2):
                    prep(6 + j, USE[4][3])
                act.wait_ge(var_mm, 1)
                act.activation(ln_ms, Y[:, 1::2, 0], ACT.Identity, scale=1.0 / D, bias=lneps).then_inc(lms_done, 1)
                for r in range(4):
                    act.wait_ge(z_done, r // 2 + 1)
                    for k in (2 * r, 2 * r + 1):
                        a = act.activation(convT[:, k, :], convT[:, k, :], ACT.Silu, scale=cols[:, LNG + k:LNG + k + 1],
                                           bias=cols[:, LNB + k:LNB + k + 1])
                    a.then_inc(ln_act, 1)
                    act.wait_ge(ln_act, r + 1)
                    act.activation(h_hi[:, 2 * r:2 * r + 2, :], convT[:, 2 * r:2 * r + 2, :], ACT.Copy).then_inc(p_hi, 1)
                for p in (2, 3):
                    for j in range(2):
                        prep(2 * p + j, USE[4][p] + 1)

            for s in range(LAST + 1):
                pre_norm(s)
                if s in (2, 4, 5):
                    for j in range(2):
                        prep(4 + j, USE[s][2])
                if s in (0, 2):
                    attention(s)
                    post_norm(s, 7, USE[s][3] + NI_A - 1)
                elif s == 4:
                    conformer()
                    post_norm(s, 7, USE[4][3] + 1)
                else:
                    gated(s)
                    post_norm(s, 5, USE[s][2] + NI_F - 1)

        @block.vector
        def _(dve):
            def prep(u, n):
                dve.wait_ge(hi[u], n + 1)
                dve.tensor_tensor(wlo[:, u, :], raw[:, u, :], whi[:, u, :].bitcast(F32),
                                  ALU.subtract).then_inc(lo[u], 1)

            def gemv_step(layer, b, q):
                k, m = q // 2, b + NBLK * layer
                if q % 2 == 0:
                    dve.wait_ge(ada_ld[k], m * 16 + 16)
                if q:
                    dve.wait_ge(gemv, m * 8 + q)
                at = acc[:, bass.ds(b * BLK, BLK)]
                ccol = (8 if layer == 2 else 0) + q
                dve.scalar_tensor_tensor(at, ada_raw[:, k, q % 2, :], csil[:, ccol:ccol + 1], at,
                                         ALU.mult, ALU.add).then_inc(gemv, 1)

            def gemv_start(layer):
                dve.wait_ge(acc_bias, 16 * (layer + 1))
                if layer == 0:
                    dve.wait_ge(csil_ready, 1)

            gemv_start(0)
            for b in range(4):
                for q in range(KT):
                    gemv_step(0, b, q)
                if b == 1:
                    at = 0
                    for g, rows in enumerate(PAR_ROWS):
                        if g:
                            dve.wait_ge(par_T, g + 1)
                            dve.tensor_copy(cols[:, at:at + rows],
                                            par_bank[g][:, 0:rows]).then_inc(cols_ready, 1)
                            at += rows
                    dve.wait_ge(rel_mm, 1)
                    dve.tensor_tensor(relrow, Y[0:H, 0, 0:REL], relrow, ALU.add).then_inc(rel_row, 1)
                if b > 1:
                    prep(2 * b - 4, 0)
                    prep(2 * b - 3, 0)
            prep(4, 0)
            prep(5, 0)

            def columns(s):
                dve.wait_ge(mod_cols, s + 1)
                dve.wait_ge(cols_ready, len(PAR_ROWS) - 1)
                dve.scalar_tensor_tensor(colA[:], work[:, 3, KT:2 * KT], 1.0,
                                         cols[:, NORM + KT * s:NORM + KT * (s + 1)], ALU.add, ALU.mult)
                dve.tensor_copy(colB[:], work[:, 3, 0:KT]).then_inc(mod_cols_used, 1)

            def pre_norm(s):
                dve.wait_ge(rsx_done, 2 * s + 1)
                if s == 0:
                    dve.wait_ge(rel_stored, 16)
                dve.tensor_scalar(xs[:, 0, :], xt[:, 0, :], rsx[:, 0:1], None, ALU.mult).then_inc(xs0, 1)
                dve.wait_ge(mod_cols_used, s + 1)
                for b in (0, 2):
                    dve.wait_ge(hT, 4 * s + b + 1)
                    for k in (2 * b, 2 * b + 1):
                        bank = work[:, b, (k % 2) * S:(k % 2 + 1) * S]
                        v = dve.tensor_scalar(bank, bank, colA[:, k:k + 1], colB[:, k:k + 1], ALU.mult, ALU.add)
                    v.then_inc(h32v, 1)
                for b in range(4):
                    dve.wait_ge(hhi, 4 * s + b + 1)
                    hs = slice(2 * b, 2 * b + 2)
                    dve.tensor_tensor(h_lo[:, hs, :].rearrange("p k n -> p (k n)"), work[:, b, :],
                                      h_hi[:, hs, :].rearrange("p k n -> p (k n)").bitcast(F32),
                                      ALU.subtract).then_inc(hlo, 1)

            def post_norm(s, u, n):
                L = s // 2
                G, G_used = (Ga, mod_ga_used) if s % 2 == 0 else (Gf, mod_gf_used)
                if s % 2 == 0:
                    dve.wait_ge(mod_ga, L + 1)
                    dve.wait_ge(gain_loaded, 32 * (L + 1))
                    dve.tensor_tensor(Ga[:], work[:, 0:2, :].rearrange("p a b -> p (a b)"), Ga[:],
                                      ALU.mult).then_inc(mod_ga_used, 1)
                    columns(s + 1)
                dve.wait_ge(G_used, L + 1)
                for t in range(TT):
                    yt = Y[:, 2 * t:2 * t + 2, :].rearrange("p a b -> p (a b)")
                    dve.wait_ge(rsy_done, 2 * s + t + 1)
                    dve.scalar_tensor_tensor(xs[:, t, :], yt, rsy[:, t:t + 1], G[:], ALU.mult,
                                             ALU.mult).then_inc(y_tmp, 1)
                    dve.wait_ge(y_tmp, 2 * s + t + 1)
                    if s == 0:
                        dve.wait_ge(x_loaded, 32)
                    dve.tensor_tensor(xt[:, t, :], xt[:, t, :], xs[:, t, :], ALU.add).then_inc(x_ready, 1)
                if s % 2 == 0:
                    dve.wait_ge(mod_gf, 2 * L + 2)
                    dve.tensor_tensor(Gf[:], work[:, 2:4, :].rearrange("p a b -> p (a b)"), Gf[:],
                                      ALU.mult).then_inc(mod_gf_used, 1)

            def attention(s):
                hb, rb, nb, nb3 = HEADS[s], ROWS[s], USE[s][0], USE[s][3]

                def out_lo(i, j):
                    R = i * 2 + (rb + j)
                    dve.wait_ge(ahi, R + 1)
                    high = a_hi[:, j, :].bitcast(F32)
                    if s == 0:
                        dve.tensor_tensor(a_lo[:, j, :], work[:, 1, 0:S], high, ALU.subtract).then_inc(alo, 1)
                    else:
                        dve.scalar_tensor_tensor(a_lo[:, j, :], work[:, 2, 0:S], subg, high, ALU.mult,
                                                 ALU.subtract).then_inc(alo, 1)

                def copy_out(T):
                    dve.wait_ge(pv_mm, T + 1)
                    dve.tensor_copy(oraw, work[:, 1, 0:S]).then_inc(ocp, 1)

                def norm_out(T):
                    for t in range(TT):
                        dve.wait_ge(ors, (T - hb) * 2 + (t + 1))
                        dve.wait_ge(ocp, T - hb + 1)
                        dve.tensor_scalar(osc[:, t * P:(t + 1) * P], oraw[:, t * P:(t + 1) * P],
                                          rso[:, t:t + 1], None, ALU.mult).then_inc(osn, 1)

                def softmax(T, h, between):
                    ng = 1 if s == 0 else 2
                    n1 = (T - hb) * ng + (0 if s == 0 else HEADS[2])
                    dve.wait_ge(s_mm, T + 1)
                    need(dve, pT_mm, T)
                    for g in range(ng):
                        dve.scalar_tensor_tensor(pr[:, g, :], work[:, 2 + g, 0:3 * P], scale_of[s],
                                                 head_bias[:, bass.ds(h, 1), :].rearrange("p a n -> p (a n)"),
                                                 ALU.mult, ALU.add).then_inc(sb_done, 1)
                    dve.wait_ge(sb_done, n1 + ng)
                    for q, (a, b) in enumerate(((0, P), (P, 3 * P))):
                        dve.tensor_reduce(mmax[:, q * ng:(q + 1) * ng], pr[:, 0:ng, a:b], AX.X,
                                          ALU.max).then_inc(mx_done, 1)
                    dve.wait_ge(mx_done, T * 2 + 2)
                    dve.tensor_scalar(mneg[:, 0:2 * ng], mmax[:, 0:2 * ng], -1.0, None,
                                      ALU.mult).then_inc(ng_done, 1)
                    between()
                    n2 = (T - hb) * (2 * ng) + (0 if s == 0 else 2 * HEADS[2])
                    dve.wait_ge(ex_done, n2 + 2 * ng)
                    dve.reciprocal(mrec[:, 0:2 * ng], msum[:, 0:2 * ng]).then_inc(rc_done, 1)
                    dve.wait_ge(rc_done, T + 1)
                    if s == 0:
                        for q, (a, b) in enumerate(((0, P), (P, 3 * P))):
                            dve.tensor_scalar(pr[:, 0, a:b], pr[:, 0, a:b], mrec[:, q:q + 1], None,
                                              ALU.mult).then_inc(p_done, 1)
                        return
                    n3 = (T - hb) * 3
                    dve.tensor_scalar(lrec, mrec.rearrange("p (q g) -> p q g", g=2)[:, :, 1], lamf[:, 0:1], None,
                                      ALU.mult).then_inc(dif_seq, 1)
                    dve.wait_ge(dif_seq, n3 + 1)
                    for q, (a, b) in enumerate(((0, P), (P, 3 * P))):
                        dve.tensor_scalar(pr[:, 1, a:b], pr[:, 1, a:b], lrec[:, q:q + 1], None,
                                          ALU.mult).then_inc(dif_seq, 1)
                    for q, (a, b) in enumerate(((0, P), (P, 3 * P))):
                        dve.wait_ge(dif_seq, n3 + 2 + q)
                        dve.scalar_tensor_tensor(pr[:, 0, a:b], pr[:, 0, a:b], mrec[:, 2 * q:2 * q + 1],
                                                 pr[:, 1, a:b], ALU.mult, ALU.subtract).then_inc(p_done, 1)

                def step(i, j, more):
                    T = i * 2 + (hb + j)
                    start = isinstance(i, int) and i == 0
                    first = start and j == 0

                    def sums(q0):
                        if s == 0:
                            for q in range(q0, q0 + 2):
                                gemv_step(0, i * 2 + (4 + j), q)

                    if s == 2 and not start:
                        out_lo(i - 1, j)
                    sums(0)
                    if more:
                        prep(j, i + (nb + 1))
                        prep(2 + j, i + (nb + 1))
                    sums(2)
                    prep(6 + j, i + nb3)
                    if not first:
                        if s == 2:
                            copy_out(T - 1)
                        elif j:
                            out_lo(i, 0)
                        else:
                            out_lo(i - 1, 1)
                    sums(4)

                    def between():
                        if s == 2 and not first:
                            norm_out(T - 1)
                        sums(6)

                    softmax(T, i * 2 + j, between)
                    if more:
                        prep(4 + j, i + (nb + 1))

                def both(i, more):
                    step(i, 0, more)
                    step(i, 1, more)

                sweep(dve, 1, NI_A, s, both)
                T = hb + H
                if s == 2:
                    out_lo(NI_A - 1, 0)
                    copy_out(T - 1)
                    norm_out(T - 1)
                out_lo(NI_A - 1, 1)

            def lam_and_gain():
                dve.wait_ge(lam_loaded, 16)
                lam = lam_in.rearrange("p (a b n) -> p a b n", a=2, b=2)
                dve.tensor_tensor(lam_pr.rearrange("p (a n) -> p a n", a=2), lam[:, :, 0, :], lam[:, :, 1, :],
                                  ALU.mult).then_inc(lam_seq, 1)
                dve.wait_ge(lam_seq, 1)
                dve.tensor_reduce(lamv, lam_pr.rearrange("p (a n) -> p a n", a=2), AX.X, ALU.add).then_inc(lam_seq, 1)
                dve.wait_ge(lam_exp, 1)
                dve.tensor_tensor(lamf[:, 1:2], lame[:, 0:1], lame[:, 1:2], ALU.subtract).then_inc(lam_seq, 1)
                dve.wait_ge(lam_seq, 3)
                dve.tensor_scalar(lamf[:, 0:1], lamf[:, 1:2], LAMBDA_INIT, None, ALU.add).then_inc(lam_seq, 1)
                dve.tensor_scalar(subg, cols[:, SUB:SUB + 1], (1.0 - LAMBDA_INIT) * 2 ** 0.5, None, ALU.mult).then_inc(lam_seq, 1)
                dve.wait_ge(lam_seq, 5)

            def gated(s):
                rb, fb, nb, nb2 = ROWS[s], STEPS[s], USE[s][0], USE[s][2]
                gate = gate_of[s]
                fdw = cols[:, FDW:FDW + 8 * FT].rearrange("p (a g t) -> p a g t", a=4, g=2)

                def step(i, j, more):
                    start = isinstance(i, int) and i == 0
                    t1 = i * 2 + (j + 1)
                    F = i * 2 + (fb + j)

                    def sums(q):
                        if s < 5:
                            gemv_step(s // 2 + 1, i, 4 * j + q)

                    if s == 5:
                        dve.tensor_scalar(taps[:, j, 0:8].rearrange("p (a g t) -> p a g t", a=4, g=2),
                                          fdw[:, :, :, bass.ds(i * 2 + j, 1)], 1.0, None,
                                          ALU.mult).then_inc(taps_ready, 1)
                    sums(0)
                    if not start:
                        prep(4 + j, i + nb2)
                    sums(1)
                    if s == 5:
                        g, u = work[:, 2 * j, :], work[:, 2 * j + 1, :]
                        gt, ut = gate[:, j, :], act32[:, j, :]
                        dve.wait_ge(taps_ready, t1 + 3 * KT)
                        dve.wait_ge(cv_g0, t1)
                        dve.scalar_tensor_tensor(gt[:, 1:S], g[:, 0:S - 1], taps[:, j, 2:3], gt[:, 1:S],
                                                 ALU.mult, ALU.add).then_inc(cv_seq, 1)
                        if more:
                            prep(j, i + (nb + 1))
                        n = i * 6 + 3 * j
                        dve.wait_ge(cv_seq, n + 1)
                        dve.scalar_tensor_tensor(gt[:, 2:S], g[:, 0:S - 2], taps[:, j, 0:1], gt[:, 2:S],
                                                 ALU.mult, ALU.add).then_inc(cv_g, 1)
                        dve.wait_ge(used[2 + j], i + (nb + 1))
                        dve.tensor_scalar(ut, u[:, 0:S], taps[:, j, 5:6], taps[:, j, 7:8], ALU.mult,
                                          ALU.add).then_inc(cv_seq, 1)
                        dve.wait_ge(cv_seq, n + 2)
                        dve.scalar_tensor_tensor(ut[:, 1:S], u[:, 0:S - 1], taps[:, j, 3:4], ut[:, 1:S],
                                                 ALU.mult, ALU.add).then_inc(cv_seq, 1)
                        dve.wait_ge(cv_seq, n + 3)
                        dve.scalar_tensor_tensor(ut[:, 2:S], u[:, 0:S - 2], taps[:, j, 1:2], ut[:, 2:S],
                                                 ALU.mult, ALU.add).then_inc(cv_u, 1)
                        dve.wait_ge(cv_u, t1)
                        dve.wait_ge(gate_done, F + 1)
                        dve.tensor_tensor(ut, ut, gt, ALU.mult).then_inc(act_done, 1)
                        if more:
                            prep(2 + j, i + (nb + 1))
                    else:
                        if more:
                            prep(j, i + (nb + 1))
                        sums(2)
                        dve.wait_ge(used[2 + j], i + (nb + 1))
                        dve.wait_ge(gate_done, F + 1)
                        dve.tensor_tensor(act32[:, j, :], work[:, 2 * j + 1, 0:S], gate[:, j, :],
                                          ALU.mult).then_inc(act_done, 1)
                        if more:
                            prep(2 + j, i + (nb + 1))
                        sums(3)
                    dve.wait_ge(ahi, i * 2 + (rb + j + 1))
                    dve.wait_ge(act_done, F + 1)
                    dve.tensor_tensor(a_lo[:, j, :], act32[:, j, :], a_hi[:, j, :].bitcast(F32),
                                      ALU.subtract).then_inc(alo, 1)

                def both(i, more):
                    step(i, 0, more)
                    step(i, 1, more)

                if s < 5:
                    gemv_start(s // 2 + 1)
                sweep(dve, 1, NI_F, s, both)

            def conformer():
                nb, fb = USE[4][0], STEPS[4]
                gate = gate_of[4]
                adw = cols[:, ADW:ADW + CONV * KT].rearrange("p (c t) -> p c t", t=KT)
                bias = cols[:, PW1B:PW1B + 3 * KT].rearrange("p (c t) -> p c t", t=KT)
                dve.wait_ge(thi, 1)
                dve.tensor_tensor(tap_lo, adw.rearrange("p c t -> p t c"), tap_hi, ALU.subtract).then_inc(tlo, 1)
                dve.memset(upad[:, :, 0:CONV - 1], 0.0).then_inc(pad_zero, 1)
                dve.wait_ge(tlo, 1)
                dve.wait_ge(pad_zero, 1)

                def combine(i, j):
                    T = i * 2 + j
                    dve.wait_ge(diag_used, T * NP + NP)
                    dve.wait_ge(part_done, T + 1)
                    dve.tensor_tensor(convT[:, bass.ds(T, 1), :].rearrange("p a n -> p (a n)"),
                                      Y[:, j, 0:S], part[:, j, :], ALU.add).then_inc(conv_done, 1)

                def step(i, j, more):
                    start = isinstance(i, int) and i == 0
                    T = i * 2 + j
                    F = T + fb
                    dve.tensor_scalar(taps[:, j, 0:CONV].rearrange("p (c t) -> p c t", t=1),
                                      adw[:, :, bass.ds(T, 1)], 1.0, None, ALU.mult).then_inc(taps_ready, 1)
                    dve.tensor_scalar(taps[:, j, CONV:CONV + 3].rearrange("p (c t) -> p c t", t=1),
                                      bias[:, :, bass.ds(T, 1)], 1.0, None, ALU.mult).then_inc(taps_ready, 1)
                    need(dve, diag_done, T * NP - NP)
                    dve.tensor_scalar(taps[:, j, 36:36 + 2 * NP].rearrange("p (t w c) -> p t w c", t=1, w=2),
                                      tap_parts[:, bass.ds(T, 1), :, :], 1.0, None, ALU.mult).then_inc(taps_ready, 1)
                    if more:
                        prep(j, i + (nb + 1))
                    dve.wait_ge(taps_ready, i * 6 + (3 * j + 3))
                    dve.wait_ge(gate_done, F + 1)
                    u = upad[:, j, :]
                    dve.scalar_tensor_tensor(u[:, CONV - 1:PADW], work[:, 2 * j, 0:S], taps[:, j, 31:32],
                                             gate[:, j, :], ALU.add, ALU.mult).then_inc(act_done, 1)
                    if more:
                        prep(2 + j, i + (nb + 1))
                    dve.wait_ge(act_done, F + 1)
                    dve.wait_ge(uhi, T + 1)
                    dve.tensor_tensor(u_lo[:, j, :], u, u_hi[:, j, :].bitcast(F32), ALU.subtract).then_inc(ulo, 1)
                    n = T * (CONV - NP)
                    for c, m in enumerate(range(NP, CONV)):
                        w = taps[:, j, m:m + 1]
                        sums = cacc[:, c % 2, :]
                        if c == 0:
                            v = dve.tensor_scalar(sums, u[:, m:m + S], w, taps[:, j, 33:34], ALU.mult, ALU.add)
                        elif c == 1:
                            v = dve.tensor_scalar(sums, u[:, m:m + S], w, None, ALU.mult)
                        else:
                            dve.wait_ge(tap_seq, n + (c - 1))
                            v = dve.scalar_tensor_tensor(sums, u[:, m:m + S], w, sums, ALU.mult, ALU.add)
                        v.then_inc(tap_seq, 1)
                    if j:
                        combine(i, 0)
                    elif not start:
                        combine(i - 1, 1)
                    dve.wait_ge(tap_seq, n + (CONV - NP))
                    dve.tensor_tensor(part[:, j, :], cacc[:, 0, :], cacc[:, 1, :], ALU.add).then_inc(part_done, 1)

                def both(i, more):
                    step(i, 0, more)
                    step(i, 1, more)

                sweep(dve, 1, NI_C, 4, both)
                combine(NI_C - 1, 1)
                dve.wait_ge(mean_done, 1)
                for h in range(2):
                    half = convT[:, 4 * h:4 * h + 4, :]
                    dve.tensor_tensor(half, half, ln_mean.unsqueeze(1).broadcast_to([P, 4, S]),
                                      ALU.subtract).then_inc(d_done, 1)
                for j in range(2):
                    prep(6 + j, USE[4][3])
                dve.wait_ge(lrs_done, 1)
                for t in range(TT):
                    d = dve.tensor_scalar(ln_diag[:, t, :], ident[:], ln_rs[:, t:t + 1], None, ALU.mult)
                    d.then_inc(ln_dg, 1)
                dve.wait_ge(lrs_mm, 1)
                dve.wait_ge(sq_done, 2)
                for h in range(2):
                    half = convT[:, 4 * h:4 * h + 4, :]
                    dve.tensor_tensor(half, half, work[:, 0, 0:S].unsqueeze(1).broadcast_to([P, 4, S]),
                                      ALU.mult).then_inc(z_done, 1)
                for r in range(4):
                    hs = slice(2 * r, 2 * r + 2)
                    dve.wait_ge(p_hi, r + 1)
                    dve.tensor_tensor(h_lo[:, hs, :], convT[:, hs, :], h_hi[:, hs, :].bitcast(F32),
                                      ALU.subtract).then_inc(p_lo, 1)
                for p in (2, 3):
                    for j in range(2):
                        prep(2 * p + j, USE[4][p] + 1)

            columns(0)
            for s in range(LAST + 1):
                if s and s % 2 == 0:
                    columns(s)
                pre_norm(s)
                if s in (2, 4, 5):
                    for j in range(2):
                        prep(4 + j, USE[s][2])
                if s in (2, 4):
                    for q in range(KT):
                        gemv_step(s // 2, NBLK - 1, q)
                if s in (0, 2):
                    if s == 0:
                        dve.wait_ge(bias_loaded, 32)
                    else:
                        lam_and_gain()
                    attention(s)
                    post_norm(s, 7, USE[s][3] + NI_A - 1)
                elif s == 4:
                    conformer()
                    post_norm(s, 7, USE[4][3] + 1)
                else:
                    gated(s)
                    post_norm(s, 5, USE[s][2] + NI_F - 1)


def relative_constants():
    import math

    import numpy as np

    buckets, exact, far = 32, 16, 2048
    rel = (S - 1) - np.arange(REL)
    n = np.maximum(rel, 0)
    nf = np.maximum(n, 1).astype(np.float32)
    large = exact + (np.log(nf / np.float32(exact)) / np.float32(math.log(far / exact))
                     * np.float32(buckets - exact)).astype(np.int32)
    bucket = np.where(n < exact, n, np.minimum(large, buckets - 1))
    onehot = ((np.arange(buckets)[:, None] == bucket[None, :]) & (rel >= 0)).astype(np.float32)
    fill = np.broadcast_to(np.where(rel >= 0, 0.0, -1e30).astype(np.float32), (H, REL))
    return np.ascontiguousarray(onehot), np.ascontiguousarray(fill)


_INS = ["x", "c", "rel_bias", "ada_w", "ada_b", "norm_g", "moba_w_qkv", "moba_w_o", "diff_w_qkv",
        "diff_w_o", "diff_lambda", "diff_subln_g", "ffn_w_in", "ffn_w_out", "c_2", "mod_w_2", "mod_b_2",
        "norm_pre_mix_2", "norm_post_mix_2", "norm_pre_ffn_2", "norm_post_ffn_2", "a_pw1_w_2",
        "a_pw1_b_2", "a_dw_w_2", "a_dw_b_2", "a_ln_g_2", "a_ln_b_2", "a_pw2_w_2", "a_pw2_b_2",
        "f_up_w_2", "f_dw_w_2", "f_dw_b_2", "f_down_w_2"]


def kernel(**inputs):
    import numpy as np
    import concourse.bacc as bacc
    from concourse.bass_utils import run_bass_kernel_spmd

    nc = bacc.Bacc("TRN2", target_bir_lowering=False, num_devices=1)
    arrays, args = {}, []
    given = {name: np.ascontiguousarray(inputs[name]) for name in _INS}
    given["bucket_onehot"], given["causal_fill"] = relative_constants()
    for name, a in given.items():
        arrays[f"in_{name}"] = a
        args.append(nc.dram_tensor(f"in_{name}", a.shape, mybir.dt.from_np(a.dtype), kind="ExternalInput").ap())
    out = nc.dram_tensor("out", (1, S, D), F32, kind="ExternalOutput").ap()
    build(nc, *args, out)
    r = run_bass_kernel_spmd(nc, [arrays], core_ids=[0])
    return r.results[0]["out"]
```

```python
from contextlib import ExitStack

import concourse.bass as bass
from concourse import mybir

F32 = mybir.dt.float32
F32R = mybir.dt.float32r
ALU = mybir.AluOpType
ACT = mybir.ActivationFunctionType
AX = mybir.AxisListType

P = 128
S = 256
D = 1024
H = 8
KT = D // P
TT = S // P
FT = 22
FF = FT * P
CONV = 31
NP = 13
EPS, LN_EPS = 1e-6, 1e-5
LAMBDA_INIT = 0.8 - 0.6 * 0.7408182206817179
REL = 384
BLK = 512
NBLK = 6 * D // BLK
FIRST = 2 * D // BLK
PADW = S + CONV - 1
LAST = 5

NORM, PW1B, DWB, LNG, LNB, SUB = 0, 48, 64, 72, 80, 88
FDW, ADW = 89, 89 + 8 * FT
COLS = ADW + CONV * KT
PAR_ROWS = (16, 89, 4 * FT, 4 * FT, 16 * KT, 15 * KT)

USE = {0: (0, 0, 0, 0), 1: (4, 4, 4, 4), 2: (15, 15, 15, 4), 3: (19, 19, 19, 8),
       4: (30, 30, 30, 8), 5: (34, 34, 32, 10)}
ROWS = {0: 0, 1: 8, 2: 30, 3: 38, 5: 60}
STEPS = {1: 0, 3: 22, 4: 44, 5: 52}
HEADS = {0: 0, 2: 8}
GATE_BANK = {0: 1, 1: 2, 2: 2, 3: 2, 4: 2, 5: 2}
NI_A, NI_F, NI_C = H // 2, FT // 2, KT // 2


def build(nc, x, c, rel_bias, ada_w, ada_b, norm_g, moba_w_qkv, moba_w_o, diff_w_qkv, diff_w_o,
          diff_lambda, diff_subln_g, ffn_w_in, ffn_w_out, c_2, mod_w_2, mod_b_2, norm_pre_mix_2,
          norm_post_mix_2, norm_pre_ffn_2, norm_post_ffn_2, a_pw1_w_2, a_pw1_b_2, a_dw_w_2, a_dw_b_2,
          a_ln_g_2, a_ln_b_2, a_pw2_w_2, a_pw2_b_2, f_up_w_2, f_dw_w_2, f_dw_b_2, f_down_w_2,
          bucket_onehot, causal_fill, out):
    with ExitStack() as ctx:
        def sb(name, shape, dt=F32):
            return ctx.enter_context(nc.sbuf_tensor(name, shape, dt))

        def sem(name):
            return ctx.enter_context(nc.semaphore(name))

        rel_rows = nc.dram_tensor("rel_rows", (H, P, REL), F32, kind="Internal").ap()

        raw = sb("raw", [P, 8, D])
        whi = sb("whi", [P, 8, D], F32R)
        wlo = sb("wlo", [P, 8, D], F32R)
        ada_raw = sb("ada_raw", [P, 4, 2, BLK])
        acc = sb("acc", [P, 6 * D])
        xt_eps = sb("xt", [P, TT, D + 1])
        xs_pad = sb("xs", [P, TT, D + 1])
        h_hi = sb("h_hi", [P, KT, S], F32R)
        h_lo = sb("h_lo", [P, KT, S], F32R)
        head_bias = sb("head_bias", [P, H, REL])
        Ga = sb("Ga", [P, D])
        Gf = sb("Gf", [P, D])
        ab_hi = sb("ab_hi", [P, 2, PADW], F32R)
        ab_lo = sb("ab_lo", [P, 2, PADW], F32R)
        mix = sb("mix", [P, 2688])
        cols = sb("cols", [P, COLS])
        first_scale = sb("first_scale", [P, KT])
        csil = sb("csil", [P, 16])
        colA = sb("colA", [P, KT])
        colB = sb("colB", [P, KT])
        taps = sb("taps", [P, 2, 72])
        ident = sb("ident", [P, P])
        ones = sb("ones", [P, P])
        small = sb("small", [P, 96])
        relt = sb("relt", [32, H])
        Y = ctx.enter_context(nc.psum_tensor("Y", [P, 4, 512], F32))
        work = ctx.enter_context(nc.psum_tensor("work", [P, 4, 512], F32))

        xt, xs = xt_eps[:, :, 0:D], xs_pad[:, :, 0:D]
        a_hi, a_lo = ab_hi[:, :, 0:S], ab_lo[:, :, 0:S]
        u_hi, u_lo = ab_hi, ab_lo
        qk = mix[:, 0:512]
        vv = mix[:, 512:1024].rearrange("p (t n) -> p t n", t=TT)
        pr = mix[:, 1024:1792].rearrange("p (c n) -> p c n", c=2)
        pT = mix[:, 1792:2176]
        oraw = mix[:, 2176:2432]
        osc = mix[:, 2432:2688]
        lam_in, lam_pr = oraw, osc[:, 0:128]
        yG = mix[:, 0:TT * D].rearrange("p (t n) -> p t n", t=TT)
        gate_of = {n: mix[:, at:at + 2 * S].rearrange("p (j n) -> p j n", j=2)
                   for n, at in ((1, 0), (3, 0), (5, 0), (4, 2176))}
        act32 = mix[:, 512:512 + 2 * S].rearrange("p (j n) -> p j n", j=2)
        upad = mix[:, 0:2 * PADW].rearrange("p (j n) -> p j n", j=2)
        cacc = mix[:, 576:576 + 2 * S].rearrange("p (j n) -> p j n", j=2)
        b2row = mix[0:1, 1152:1152 + D]
        ln_diag = mix[:, 576:576 + S].rearrange("p (t n) -> p t n", t=TT)
        convT = head_bias[:, :, 0:S]
        tap_hi = head_bias[:, :, S:S + CONV]
        tap_lo = head_bias[:, :, S + 32:S + 32 + CONV]
        tap_parts = head_bias[:, :, S:S + 64].rearrange("p t (w c) -> p t w c", w=2)[:, :, :, 0:NP]
        part = xs[:, :, 576:576 + S]
        diag = [w[:, 6:8, :].rearrange("p u (m n) -> p (u m) n", n=P) for w in (whi, wlo)]
        prow = mix[:, 0:6 * P].rearrange("p (g n) -> p g n", g=6)
        onehot = mix[0:32, 6 * P:6 * P + REL]
        relrow = mix[0:H, 6 * P + REL:6 * P + 2 * REL]
        par_bank = [Y[:, 3, 0:PAR_ROWS[0]]]
        for bank, g0, g1 in ((1, 1, 4), (2, 4, 6)):
            for g in range(g0, g1):
                at = sum(PAR_ROWS[g0:g])
                par_bank.append(Y[:, bank, at:at + PAR_ROWS[g]])
        mod_bank = {s: Y[:, 3, :] if s == 0 else work[:, 0, :] for s in range(6)}
        ssx, rsx = small[:, 0:2], small[:, 4:6]
        msy_half, msy, rsy = small[:, 6:8], small[:, 8:10], small[:, 10:12]
        mhalf, eps2 = small[:, 12:13], small[:, 13:14]
        mmax, mneg = small[:, 14:18], small[:, 18:22]
        msum, mrec = small[:, 22:26], small[:, 26:30]
        lrec = small[:, 30:32]
        sso, mso, rso = small[:, 32:34], small[:, 34:36], small[:, 36:38]
        subg = small[:, 38:39]
        lamv, lame, lamf = small[:, 40:42], small[:, 42:44], small[:, 44:46]
        lneps, ln_ms, ln_rs = small[:, 48:49], small[:, 50:52], small[:, 52:54]
        ssy = small[:, 56:56 + 2 * TT]

        ld = [sem(f"unit_loaded{u}") for u in range(8)]
        hi = [sem(f"unit_hi{u}") for u in range(8)]
        lo = [sem(f"unit_lo{u}") for u in range(8)]
        used = [sem(f"unit_multiplied{u}") for u in range(8)]
        ada_ld = [sem(f"ada_loaded{k}") for k in range(4)]
        odd_ld = [sem(f"first_odd_loaded{k}") for k in range(4)]
        gemv, first_mm, scale_done = sem("gemv_steps"), sem("first_quarters_multiplied"), sem("first_scale_done")
        acc_zero, acc_bias = sem("acc_zero"), [sem(f"acc_bias{n}") for n in range(1, 7)]
        c_loaded, par_loaded, x_loaded = sem("c_loaded"), sem("par_loaded"), sem("x_loaded")
        rel_loaded, rel_mm, rel_row = sem("rel_loaded"), sem("rel_mm"), sem("rel_row")
        rel_stored, bias_loaded = sem("rel_stored"), sem("bias_loaded")
        lam_loaded, lam_seq, lam_exp = sem("lam_loaded"), sem("lam_seq"), sem("lam_exp")
        b2_loaded, gain_loaded = sem("b2_loaded"), sem("gain_loaded")
        id_zero, consts = sem("id_zero"), sem("consts")
        par_T, cols_ready, csil_ready = sem("par_T"), sem("cols_ready"), sem("csil_ready")
        ssx_done, rsx_done = sem("ssx_done"), sem("rsx_done")
        ssy_done, msy_half_done = sem("ssy_done"), sem("msy_half_done")
        msy_done, rsy_done = sem("msy_done"), sem("rsy_done")
        xs_ready = sem("xs_ready")
        hT, h32v, h32a, hhi, hlo = sem("hT"), sem("h32v"), sem("h32a"), sem("h_hi_done"), sem("h_lo_done")
        x_ready, y0_done, y_tmp = sem("x_ready"), sem("y0_done"), sem("y_tmp")
        mod_cols, mod_cols_used = sem("mod_cols"), sem("mod_cols_used")
        mod_ga, mod_gf = sem("mod_ga"), sem("mod_gf")
        mod_ga_used, mod_gf_used = sem("mod_ga_used"), sem("mod_gf_used")
        gate_done, act_done = sem("gate_done"), sem("act_done")
        ahi, alo = sem("a_hi_done"), sem("a_lo_done")
        taps_ready = sem("taps_ready")
        cv_g0, cv_g, cv_u, cv_seq = sem("cv_g0"), sem("cv_g"), sem("cv_u"), sem("cv_seq")
        q_ev, k_ev, s_mm, sb_done, mx_done = sem("q_ev"), sem("k_ev"), sem("s_mm"), sem("sb_done"), sem("mx_done")
        ng_done, ex_done, rc_done = sem("ng_done"), sem("ex_done"), sem("rc_done")
        p_done, pT_mm, pT_ev = sem("p_done"), sem("pT_mm"), sem("pT_ev")
        pv_mm, v_ev = sem("pv_mm"), sem("v_ev")
        ocp, oss, oms, ors = sem("ocp"), sem("oss"), sem("oms"), sem("ors")
        osn, oT_mm, dif_seq = sem("osn"), sem("oT_mm"), sem("dif_seq")
        pad_zero, tap_seq, conv_done = sem("pad_zero"), sem("tap_seq"), sem("conv_done")
        thi, tlo = sem("taps_hi_done"), sem("taps_lo_done")
        uhi, ulo = sem("u_hi_done"), sem("u_lo_done")
        diag_done, diag_used, part_done = sem("diag_done"), sem("diag_multiplied"), sem("part_done")
        mean_mm, d_done = sem("mean_mm"), sem("d_done")
        sq_done, var_mm, lms_done, lrs_done = sem("sq_done"), sem("var_mm"), sem("lms_done"), sem("lrs_done")
        ln_dg, lrs_mm, fold_done = sem("ln_diag_done"), sem("lrs_mm"), sem("fold_done")
        z_done, ln_act, p_hi, p_lo = sem("z_done"), sem("ln_act"), sem("p_hi"), sem("p_lo")
        stored = sem("stored")

        block = ctx.enter_context(nc.Block())

        def need(eng, s, v):
            if not (isinstance(v, int) and v <= 0):
                eng.wait_ge(s, v)

        def sweep(eng, peel, n, s, body):
            for i in range(peel):
                body(i, True)
            end = n - 1 if s == LAST else n
            if end - peel > 1:
                with eng.Fori(peel, end) as i:
                    body(i, True)
            elif end > peel:
                body(peel, True)
            if s == LAST:
                body(n - 1, False)

        def first_raw(b, k):
            return ada_raw[:, k, :, :] if b % 2 == 0 else raw[:, 4 + k, :].rearrange("p (k n) -> p k n", k=2)

        def first_ld(b, k):
            return ada_ld[k] if b % 2 == 0 else odd_ld[k]

        qkv_w = {0: moba_w_qkv, 2: diff_w_qkv}
        o_w = {0: moba_w_o, 2: diff_w_o}
        in_w = {1: ffn_w_in[0], 3: ffn_w_in[1], 5: f_up_w_2[0]}
        out_w = {1: ffn_w_out[0], 3: ffn_w_out[1], 5: f_down_w_2[0]}
        ada = [ada_w[0], ada_w[1], mod_w_2[0]]
        scale_of = {0: P ** -0.5, 2: (P // 2) ** -0.5}

        @block.sync
        def _(sp):
            def load(u, n, src):
                need(sp, hi[u], n)
                need(sp, lo[u], n)
                dst = raw[:, u, :]
                if len(src.shape) == 3:
                    dst = dst.rearrange("p (k n) -> p k n", k=KT)
                sp.dma_start(dst, src).then_inc(ld[u], 16)

            def col_unit(w, at):
                return w[:, bass.ds(at, P)].rearrange("(k p) n -> p k n", p=P)

            def row_unit(w, at):
                return w[bass.ds(at, P), :]

            def unit(s, p, i, j):
                at = i * (2 * P) + j * P
                if s in (0, 2):
                    src = col_unit(qkv_w[s][0], at + p * D) if p < 3 else row_unit(o_w[s][0], at)
                elif s == 4:
                    src = col_unit(a_pw1_w_2[0], at + p * D)
                else:
                    src = col_unit(in_w[s], at + p * FF) if p < 2 else row_unit(out_w[s], at)
                load(2 * p + j, i + USE[s][p], src)

            def pw2_pair(r, p, n):
                for j in range(2):
                    load(2 * p + j, n, row_unit(a_pw2_w_2[0], (2 * r + j) * P))

            def ada_quarters(layer, b, ks):
                m8 = (b + NBLK * layer) * 8
                for k in ks:
                    need(sp, gemv, m8 + (2 * k - 6))
                    sp.dma_start(ada_raw[:, k, :, :],
                                 ada[layer][k * 2 * P:(k + 1) * 2 * P, bass.ds(b * BLK, BLK)]
                                 .rearrange("(k p) n -> p k n", p=P)).then_inc(ada_ld[k], 16)

            def first_block(b):
                for k in range(4):
                    if b > 1:
                        sp.wait_ge(gemv, 8 * (b - 2) + 2 * k + 2)
                    sp.dma_start(first_raw(b, k),
                                 ada[0][k * 2 * P:(k + 1) * 2 * P, b * BLK:(b + 1) * BLK]
                                 .rearrange("(k p) n -> p k n", p=P)).then_inc(first_ld(b, k), 16)

            def ada_block(layer, b):
                ada_quarters(layer, b, range(4))

            def units(s, slots, i, j):
                for p in slots:
                    unit(s, p, i, j)

            for b in range(FIRST):
                first_block(b)
            units(0, (0, 1), 0, 0)
            units(0, (0, 1), 0, 1)
            sp.wait_ge(first_mm, FIRST // 2)
            sp.wait_ge(gemv, 8 * FIRST)
            units(0, (2,), 0, 1)
            units(0, (2,), 0, 0)
            for s in range(LAST + 1):
                more = s < LAST
                if s in (0, 2):
                    def attention_loads(i, j):
                        if isinstance(i, int) and i == NI_A:
                            if more:
                                units(s + 1, (0, 1), 0, j)
                            unit(s, 3, i - 1, j)
                            if more:
                                unit(s + 1, 2, 0, j)
                        else:
                            units(s, (0, 1), i, j)
                            unit(s, 3, i - 1, j)
                            unit(s, 2, i, j)
                        if s == 0 and not (isinstance(i, int) and i == 1):
                            ada_block(0, i * 2 + j)

                    attention_loads(1, 0)
                    attention_loads(1, 1)
                    with sp.Fori(2, NI_A) as i:
                        attention_loads(i, 0)
                        attention_loads(i, 1)
                    attention_loads(NI_A, 0)
                    attention_loads(NI_A, 1)
                elif s == 4:
                    with sp.Fori(1, NI_C) as i:
                        units(4, (0, 1), i, 0)
                        units(4, (0, 1), i, 1)
                    if more:
                        units(5, (0, 1), 0, 0)
                        units(5, (0, 1), 0, 1)
                    pw2_pair(2, 2, USE[4][2] + 1)
                    pw2_pair(3, 3, USE[4][3] + 1)
                    if more:
                        units(5, (2,), 0, 0)
                        units(5, (2,), 0, 1)
                else:
                    def ffn_loads(i, j):
                        if s == 5:
                            if isinstance(i, int) and i <= 4:
                                ada_quarters(2, NBLK - 2 + (i - 1) // 2, ((i - 1) % 2 * 2 + j,))
                        elif isinstance(i, int) and i <= 2:
                            ada_quarters(s // 2, NBLK - 3 + i, (2 * j, 2 * j + 1))
                        else:
                            ada_quarters(s // 2 + 1, i - 3, (2 * j, 2 * j + 1))
                        if not (isinstance(i, int) and i == 1):
                            unit(s, 2, i - 1, j)
                        if not (isinstance(i, int) and i == NI_F):
                            units(s, (0, 1), i, j)
                        elif more:
                            units(s + 1, (0, 1), 0, j)

                    for i in range(1, 5):
                        ffn_loads(i, 0)
                        ffn_loads(i, 1)
                    with sp.Fori(5, NI_F) as i:
                        ffn_loads(i, 0)
                        ffn_loads(i, 1)
                    ffn_loads(NI_F, 0)
                    ffn_loads(NI_F, 1)
                    if more:
                        if s == 1:
                            units(2, (2,), 0, 0)
                            units(2, (2,), 0, 1)
                        else:
                            pw2_pair(0, 2, USE[4][2])
                            pw2_pair(1, 3, USE[4][3])
                        ada_block(s // 2 + 1, NBLK - 3)
            for t in range(TT):
                sp.wait_ge(x_ready, 2 * LAST + t + 1)
                sp.dma_start(out[0, t * P:(t + 1) * P, :], xt[:, t, :]).then_inc(stored, 16)
            sp.wait_ge(stored, 16 * TT)

        @block.gpsimd
        def _(pool):
            def row(src):
                return bass.AP(src.tensor, src.offset, [[0, P], [1, D]])

            def acc_init(n, layer, lo_c, hi_c):
                pool.memset(acc[:, lo_c:hi_c], 0.0).then_inc(acc_zero, 1)
                pool.wait_ge(acc_zero, n)
                bias = ada_b[layer:layer + 1, lo_c:hi_c] if layer < 2 else mod_b_2[0:1, lo_c:hi_c]
                pool.dma_start(acc[0:1, lo_c:hi_c], bias).then_inc(acc_bias[n - 1], 16)

            def gains(layer):
                need(pool, x_ready, 4 * layer)
                post = ((norm_g[layer, 1], norm_g[layer, 3]) if layer < 2
                        else (norm_post_mix_2[0], norm_post_ffn_2[0]))
                for g, src in zip((Ga, Gf), post):
                    pool.dma_start(g[:], row(src)).then_inc(gain_loaded, 16)
                if layer == 2:
                    pool.dma_start(b2row, a_pw2_b_2[0:1, :]).then_inc(b2_loaded, 16)

            def rstd_y(s, t):
                n, c = 2 * s + t, slice(t, t + 1)
                pool.wait_ge(ssy_done, 2 * n + 1)
                pool.tensor_scalar(msy_half[:, c], ssy[:, 2 * t:2 * t + 1], EPS, None, ALU.add).then_inc(msy_half_done, 1)
                pool.wait_ge(ssy_done, 2 * n + 2)
                pool.wait_ge(msy_half_done, n + 1)
                pool.tensor_tensor(msy[:, c], msy_half[:, c], ssy[:, 2 * t + 1:2 * t + 2], ALU.add).then_inc(msy_done, 1)
                pool.wait_ge(msy_done, n + 1)
                pool.tensor_tensor(rsy[:, c], msy[:, c], mhalf, ALU.pow).then_inc(rsy_done, 1)

            acc_init(1, 0, 0, 2 * D)
            pool.memset(ident[:], 0.0).then_inc(id_zero, 1)
            pool.wait_ge(id_zero, 1)
            pool.affine_select(out=ident[:], in_=ident[:], compare_op=ALU.not_equal, fill=1.0, base=0,
                               pattern=[[-1, P]], channel_multiplier=1).then_inc(consts, 1)
            pool.memset(ones[:], 1.0).then_inc(consts, 1)
            pool.memset(mhalf, -0.5).then_inc(consts, 1)
            pool.memset(eps2, 2 * EPS).then_inc(consts, 1)
            pool.memset(xt_eps[:, :, D:D + 1], (D * EPS) ** 0.5).then_inc(consts, 1)
            pool.memset(lneps, LN_EPS).then_inc(consts, 1)
            acc_init(2, 0, 2 * D, 6 * D)
            pool.wait_ge(consts, 6)
            for s in range(LAST + 1):
                for t in range(TT):
                    pool.wait_ge(ssx_done, 2 * s + t + 1)
                    pool.tensor_tensor(rsx[:, t:t + 1], ssx[:, t:t + 1], mhalf, ALU.pow).then_inc(rsx_done, 1)
                if s in (2, 4):
                    pool.wait_ge(mod_gf, s // 2)
                    acc_init(s + 2, s // 2, 5 * D, 6 * D)
                    gains(s // 2)
                elif s in (1, 3):
                    pool.wait_ge(mod_ga, s // 2 + 1)
                    pool.wait_ge(mod_cols, s + 1)
                    acc_init(s + 2, s // 2 + 1, 0, 5 * D)
                if s == 0:
                    pool.wait_ge(rel_row, 1)
                    pool.wait_ge(odd_ld[3], 2 * 16)
                    pool.dma_start(rel_rows, relrow.unsqueeze(1).broadcast_to([H, P, REL])).then_inc(rel_stored, 16)
                    pool.wait_ge(rel_stored, 16)
                    for off, lo_c, hi_c in ((255, 0, P), (127, P, 3 * P)):
                        src = bass.AP(rel_rows.tensor, rel_rows.offset + off,
                                      [[REL - 1, P], [P * REL, H], [1, hi_c - lo_c]])
                        pool.dma_start(head_bias[:, :, lo_c:hi_c], src).then_inc(bias_loaded, 16)
                    gains(0)
                if s == 2:
                    def head_rstd(i):
                        for at in range(2 * TT):
                            t = at % TT
                            pool.wait_ge(oss, i * 4 + at + 1)
                            pool.tensor_tensor(mso[:, t:t + 1], sso[:, t:t + 1], eps2, ALU.add).then_inc(oms, 1)
                            pool.wait_ge(oms, i * 4 + at + 1)
                            pool.tensor_tensor(rso[:, t:t + 1], mso[:, t:t + 1], mhalf, ALU.pow)\
                                .then_inc(ors, 1)
                    with pool.Fori(0, NI_A) as i:
                        head_rstd(i)
                if s == 4:
                    pool.wait_ge(lms_done, 1)
                    pool.tensor_tensor(ln_rs, ln_ms, mhalf.broadcast_to([P, TT]), ALU.pow).then_inc(lrs_done, 1)
                for t in range(TT):
                    rstd_y(s, t)

        @block.tensor
        def _(pe):
            def col_product(dst, u, n, early=None, before=None):
                pe.wait_ge(lo[u], n + 1)
                for k in range(KT):
                    if early is not None and k % 2 == 0:
                        pe.wait_ge(hlo, 4 * early + k // 2 + 1)
                    ws = slice(k * P, (k + 1) * P)
                    for m, (w, h) in enumerate(((whi, h_hi), (whi, h_lo), (wlo, h_hi))):
                        mm = pe.matmul(dst, w[:, u, ws], h[:, k, :], start=(k == 0 and m == 0),
                                       stop=(k == KT - 1 and m == 2))
                        if before is not None and k == 0 and m == 0:
                            mm.then_inc(before, 1)
                mm.then_inc(used[u], 1)

            def row_product(a_h, a_l, u, n, first=False, end=False, half_way=None):
                pe.wait_ge(lo[u], n + 1)
                for t in range(TT):
                    ts = slice(t * P, (t + 1) * P)
                    for m, (a, w) in enumerate(((a_h, whi), (a_h, wlo), (a_l, whi))):
                        for f in range(2):
                            mm = pe.matmul(Y[:, 2 * t + f, :], a[:, ts], w[:, u, f * 512:(f + 1) * 512],
                                           start=(first and m == 0), stop=(end and m == 2))
                    if t == 0 and end:
                        mm.then_inc(y0_done, 1)
                    if t == 0 and half_way:
                        half_way()
                mm.then_inc(used[u], 1)

            def mod_columns(s, layer, b0):
                for b in range(b0, b0 + 2 * D // BLK):
                    pe.wait_ge(gemv, 8 * (NBLK * layer + b + 1))
                    for n in range(BLK // P):
                        m, at = (b - b0) * (BLK // P) + n, b * BLK + n * P
                        mm = pe.matmul(mod_bank[s][:, m:m + 1], acc[:, at:at + P], ones[:, 0:1], start=True, stop=True)
                mm.then_inc(mod_cols, 1)

            def mod_first(layer):
                mod_columns(2 * layer, layer, 0)

            def mod_gate(base, bank, done):
                for f in range(2):
                    mm = pe.matmul(work[:, bank + f, :], ones[:], acc[:, base + f * BLK:base + (f + 1) * BLK],
                                   start=True, stop=True)
                mm.then_inc(done, 1)

            def mod_gate_a(layer):
                pe.wait_ge(gemv, 8 * (NBLK * layer + 6))
                mod_gate(2 * D, GATE_BANK[2 * layer], mod_ga)

            def mod_next(layer):
                mod_columns(2 * layer + 1, layer, 3 * D // BLK)

            def mod_gate_f(layer):
                pe.wait_ge(gemv, 8 * NBLK * (layer + 1))
                mod_gate(5 * D, GATE_BANK[2 * layer + 1], mod_gf)

            def pre_norm(s):
                if s:
                    pe.wait_ge(mod_cols_used, s + 1)
                if s % 2:
                    pe.wait_ge(mod_ga_used, s // 2 + 1)
                for t in range(TT):
                    pe.wait_ge(xs_ready, 2 * s + t + 1)
                    for k in range(KT):
                        at = (k % 2) * S + t * P
                        mm = pe.transpose(work[:, k // 2, at:at + P], xs[:, t, k * P:(k + 1) * P], ident[:])
                        if t == TT - 1 and k % 2:
                            mm.then_inc(hT, 1)

            def first_columns(b):
                pe.wait_ge(first_ld(b, 0), 16 * (b // 2 + 1))
                for n in range(BLK // P):
                    m = b * (BLK // P) + n
                    for q in range(2):
                        mm = pe.matmul(mod_bank[0][:, KT + m:KT + m + 1], first_raw(b, 0)[:, q, n * P:(n + 1) * P],
                                       csil[:, q:q + 1], start=(q == 0), stop=(q == 1))
                mm.then_inc(first_mm, 1)

            def first_sums(b):
                pe.wait_ge(gemv, 8 * (b + 1))
                for n in range(BLK // P):
                    m, at = b * (BLK // P) + n, b * BLK + n * P
                    mm = pe.matmul(mod_bank[0][:, m:m + 1], acc[:, at:at + P], ones[:, 0:1], start=True, stop=True)
                if b == FIRST - 1:
                    mm.then_inc(mod_cols, 1)

            def par_columns(g):
                rows = PAR_ROWS[g]
                pe.transpose(par_bank[g], prow[0:rows, g, :], ident[0:rows, 0:rows]).then_inc(par_T, 1)

            pe.wait_ge(consts, 6)
            pe.wait_ge(c_loaded, 32)
            par_columns(0)
            pe.wait_ge(csil_ready, 1)
            first_sums(0)
            pe.wait_ge(rel_loaded, 48)
            pe.matmul(Y[0:H, 0, 0:REL], relt[:], onehot, start=True, stop=True).then_inc(rel_mm, 1)
            first_columns(2)
            first_sums(1)
            pre_norm(0)
            first_columns(3)
            pe.wait_ge(par_loaded, 16 * 16)
            for g in range(1, len(PAR_ROWS)):
                par_columns(g)
            first_sums(2)
            first_sums(3)

            def attention(s):
                hb, rb, nb, nb3 = HEADS[s], ROWS[s], USE[s][0], USE[s][3]

                def head_out_T(T, n):
                    pe.wait_ge(osn, (T - hb) * 2 + 2)
                    pe.wait_ge(v_ev, n)
                    for t in range(TT):
                        mm = pe.transpose(work[:, 1, S + t * P:S + (t + 1) * P], osc[:, t * P:(t + 1) * P], ident[:])
                    mm.then_inc(oT_mm, 1)

                def probs_T(T, more=True):
                    pe.wait_ge(p_done, T * 2 + 2)
                    pe.wait_ge(q_ev, (T + 2 if more else T + 1))
                    for m in range(3):
                        mm = pe.transpose(work[:, 0, m * P:(m + 1) * P], pr[:, 0, m * P:(m + 1) * P], ident[:])
                    mm.then_inc(pT_mm, 1)

                def head_values(i, j):
                    pe.wait_ge(pT_ev, i * 2 + (hb + j + 1))
                    pe.wait_ge(v_ev, i + (hb // 2 + 1))
                    if s == 2:
                        need(pe, alo, i * 2 + (rb + j))
                    v0, v1 = (vv[:, t, j * P:(j + 1) * P] for t in range(TT))
                    if s == 0:
                        pe.matmul(work[:, 3, 0:P], v0, pT[:, 0:P], start=True, stop=True)
                        pe.matmul(work[:, 3, P:S], v0, pT[:, P:S], start=True, stop=False)
                        mm = pe.matmul(work[:, 3, P:S], v1, pT[:, S:3 * P], start=False, stop=True)
                    else:
                        pe.matmul(work[:, 1, 0:P], pT[:, 0:P], v0, start=True, stop=True)
                        pe.matmul(work[:, 1, P:S], pT[:, P:S], v0, start=True, stop=False)
                        mm = pe.matmul(work[:, 1, P:S], pT[:, S:3 * P], v1, start=False, stop=True)
                    mm.then_inc(pv_mm, 1)

                def scores(T):
                    pe.wait_ge(k_ev, T + 1)
                    if s == 0:
                        need(pe, sb_done, T)
                        pe.matmul(work[:, 2, 0:P], qk[:, 0:P], qk[:, S:S + P], start=True, stop=True)
                        mm = pe.matmul(work[:, 2, P:3 * P], qk[:, P:S], qk[:, S:2 * S], start=True, stop=True)
                    else:
                        need(pe, sb_done, (T - hb) * 2 + HEADS[2])
                        for g in range(2):
                            half = slice(g * 64, (g + 1) * 64)
                            pe.matmul(work[:, 2 + g, 0:P], qk[half, 0:P], qk[half, S:S + P],
                                      start=True, stop=True)
                            mm = pe.matmul(work[:, 2 + g, P:3 * P], qk[half, P:S], qk[half, S:2 * S],
                                           start=True, stop=True)
                    mm.then_inc(s_mm, 1)

                def values(T, n):
                    pe.wait_ge(lo[4], n + 1)
                    pe.wait_ge(lo[5], n + 1)
                    if s == 2:
                        need(pe, ocp, T - hb)
                    need(pe, v_ev, n - nb + hb // 2)
                    for t in range(TT):
                        ts = slice(t * P, (t + 1) * P)
                        for k in range(KT):
                            ws = slice(k * P, (k + 1) * P)
                            for m, (h, w) in enumerate(((h_hi, whi), (h_lo, whi), (h_hi, wlo))):
                                mm = pe.matmul(work[:, 1, t * S:(t + 1) * S], h[:, k, ts], w[:, 4:6, ws],
                                               start=(k == 0 and m == 0), stop=(k == KT - 1 and m == 2))
                    mm.then_inc(used[5], 1)

                def w_o(i, j, first=False, end=False, half_way=None):
                    pe.wait_ge(alo, i * 2 + (rb + j + 1))
                    row_product(a_hi[:, j, :], a_lo[:, j, :], 6 + j, i + nb3, first, end, half_way)

                def step(i, j):
                    T = i * 2 + (hb + j)
                    start = isinstance(i, int) and i == 0
                    need(pe, pT_ev, T - 1)
                    col_product(work[:, 0, 0:S], j, i + nb, s if start and j == 0 else None,
                                used[4] if j else None)
                    if s == 0:
                        need(pe, alo, T - 1)
                    else:
                        need(pe, sb_done, (T - hb) * 2 + HEADS[2])
                    col_product(work[:, 3, 0:S], 2 + j, i + nb)
                    if s == 2 and not start:
                        head_out_T(T - 2, i + (hb // 2 + j))
                    if not (start and j == 0):
                        probs_T(T - 1)
                    scores(T)
                    if j:
                        head_values(i, 0)
                    elif not start:
                        head_values(i - 1, 1)
                    if not start:
                        w_o(i - 1, j, first=isinstance(i, int) and i == 1 and j == 0)
                    if j == 0:
                        values(T, i + nb)

                for i in range(2):
                    step(i, 0)
                    step(i, 1)
                with pe.Fori(2, NI_A) as i:
                    step(i, 0)
                    step(i, 1)
                T = hb + H
                pe.wait_ge(sb_done, H if s == 0 else 2 * H + HEADS[2])
                if s == 0:
                    pe.wait_ge(v_ev, NI_A)
                mod_gate_a(s // 2)
                if s == 2:
                    head_out_T(T - 2, T // 2)
                probs_T(T - 1, more=False)
                head_values(NI_A - 1, 1)
                w_o(NI_A - 1, 0, half_way=(lambda: head_out_T(T - 1, T // 2)) if s == 2 else None)
                w_o(NI_A - 1, 1, end=True)
                pe.wait_ge(pT_ev, T)
                mod_next(s // 2)

            def gated(s):
                rb, fb, nb, nb2 = ROWS[s], STEPS[s], USE[s][0], USE[s][2]

                def down(i, j, first=False, end=False):
                    pe.wait_ge(alo, i * 2 + (rb + j + 1))
                    row_product(a_hi[:, j, :], a_lo[:, j, :], 4 + j, i + nb2, first, end)

                def step(i, j):
                    start = isinstance(i, int) and i == 0
                    before = i * 2 + j - 1
                    if not start:
                        if s == 5:
                            pe.wait_ge(cv_g, before)
                        else:
                            pe.wait_ge(gate_done, before + fb)
                    col_product(work[:, 2 * j, 0:S], j, i + nb, s if start and j == 0 else None)
                    if not start:
                        if s == 5:
                            pe.wait_ge(cv_u, before)
                        else:
                            pe.wait_ge(act_done, before + fb)
                    col_product(work[:, 2 * j + 1, 0:S], 2 + j, i + nb)
                    if j == 1:
                        down(i, 0, first=start)
                    elif not start:
                        down(i - 1, 1)

                def both(i, more):
                    step(i, 0)
                    step(i, 1)

                sweep(pe, 1, NI_F, s, both)
                pe.wait_ge(act_done, fb + FT)
                mod_gate_f(s // 2)
                down(NI_F - 1, 1, end=True)
                if s < LAST:
                    mod_first(s // 2 + 1)

            def conformer():
                nb, fb = USE[4][0], STEPS[4]

                def conv(i, j):
                    T = i * 2 + j
                    pe.wait_ge(ulo, T + 1)
                    need(pe, conv_done, T - 1)
                    for m in range(NP):
                        pe.wait_ge(diag_done, T * NP + (m + 1))
                        for n, (w, u) in enumerate(((0, u_hi), (0, u_lo), (1, u_hi))):
                            mm = pe.matmul(Y[:, j, 0:S], diag[w][:, m, :], u[:, j, m:m + S],
                                           start=(m == 0 and n == 0), stop=(m == NP - 1 and n == 2))
                        mm.then_inc(diag_used, 1)

                def mean_sum(t, first=False, end=False):
                    pe.wait_ge(conv_done, t + 1)
                    mm = pe.matmul(Y[:, 2, 0:S], ones[:], convT[:, bass.ds(t, 1), :].rearrange("p a n -> p (a n)"),
                                   start=first, stop=end)
                    if end:
                        mm.then_inc(mean_mm, 1)

                def step(i, j):
                    start = isinstance(i, int) and i == 0
                    before = i * 2 + (j - 1 + fb)
                    if not start:
                        pe.wait_ge(act_done, before)
                    col_product(work[:, 2 * j, 0:S], j, i + nb, 4 if start and j == 0 else None)
                    if not start:
                        pe.wait_ge(gate_done, before)
                    col_product(work[:, 2 * j + 1, 0:S], 2 + j, i + nb)
                    if j:
                        conv(i, 0)
                    elif not start:
                        conv(i - 1, 1)
                    if not start:
                        mean_sum(i * 2 + (j - 2), first=isinstance(i, int) and i == 1 and j == 0)

                def both(i, more):
                    step(i, 0)
                    step(i, 1)

                sweep(pe, 2, NI_C, 4, both)
                conv(NI_C - 1, 1)
                mean_sum(KT - 2)
                mean_sum(KT - 1, end=True)
                pe.wait_ge(b2_loaded, 16)
                for bank in (0, 1, 3, 2):
                    if bank == 2:
                        pe.wait_ge(d_done, 2)
                    f = bank % 2
                    pe.matmul(Y[:, bank, :], ones[0:1, :], b2row[:, f * 512:(f + 1) * 512],
                              start=True, stop=False)
                pe.wait_ge(fold_done, 2)
                for t in range(TT):
                    for k in range(2):
                        at = k * S + t * P
                        mm = pe.matmul(work[:, 0, t:t + 1], xs[:, 0, at:at + P], ones[:, 0:1],
                                       start=(k == 0), stop=(k == 1))
                mm.then_inc(var_mm, 1)
                pe.wait_ge(ln_dg, TT)
                for t in range(TT):
                    mm = pe.matmul(work[:, 1, t * P:(t + 1) * P], ones[:], ln_diag[:, t, :], start=True, stop=True)
                mm.then_inc(lrs_mm, 1)
                mod_gate_a(2)
                for k in range(KT):
                    r, j = k // 2, k % 2
                    pe.wait_ge(p_lo, r + 1)
                    row_product(h_hi[:, k, :], h_lo[:, k, :], 4 + 2 * (r % 2) + j,
                                USE[4][2 + r % 2] + r // 2, end=(k == KT - 1))
                pe.wait_ge(lms_done, 1)
                mod_next(2)

            for s in range(LAST + 1):
                if s:
                    pre_norm(s)
                    pe.wait_ge(x_ready, 2 * s)
                else:
                    pe.wait_ge(rel_row, 1)
                    pe.wait_ge(cols_ready, 2)
                if s in (0, 2):
                    attention(s)
                elif s == 4:
                    conformer()
                else:
                    gated(s)

        @block.scalar
        def _(act):
            def prep(u, n):
                act.wait_ge(ld[u], n * 16 + 16)
                need(act, used[u], n)
                act.activation(whi[:, u, :], raw[:, u, :], ACT.Copy).then_inc(hi[u], 1)

            def pre_stats(s):
                if s == 0:
                    act.wait_ge(consts, 6)
                for t in range(TT):
                    if s == 0:
                        act.wait_ge(x_loaded, 32)
                    else:
                        act.wait_ge(x_ready, 2 * (s - 1) + t + 1)
                    act.activation(xs_pad[:, t, :], xt_eps[:, t, :], ACT.Square, scale=D ** -0.5,
                                   accum_out=ssx[:, t:t + 1]).then_inc(ssx_done, 1)

            def params(dst, src, s):
                act.dma_start(dst, src).then_inc(s, 16)

            def rows(src):
                return src.rearrange("a (r p) -> (a r) p", p=P)

            params(prow[0:8, 0, :], rows(c), c_loaded)
            params(prow[8:16, 0, :], rows(c_2), c_loaded)
            for t in range(TT):
                params(xt[:, t, :], x[0, t * P:(t + 1) * P, :], x_loaded)
            params(relt[:], rel_bias, rel_loaded)
            params(onehot, bucket_onehot, rel_loaded)
            params(relrow, causal_fill, rel_loaded)
            act.wait_ge(par_T, 1)
            act.activation(csil[:], par_bank[0], ACT.Silu).then_inc(csil_ready, 1)
            pre = [norm_g[0, 0:1], norm_g[0, 2:3], norm_g[1, 0:1], norm_g[1, 2:3], norm_pre_mix_2,
                   norm_pre_ffn_2, a_pw1_b_2, a_dw_b_2, a_ln_g_2, a_ln_b_2, diff_subln_g]
            at = 0
            for src in pre:
                r = src.shape[1] // P
                params(prow[at:at + r, 1, :], rows(src), par_loaded)
                at += r
            params(prow[0:4 * FT, 2, :], rows(f_dw_w_2[0, 0:2]), par_loaded)
            params(prow[0:2 * FT, 3, :], rows(f_dw_w_2[0, 2:3]), par_loaded)
            params(prow[2 * FT:4 * FT, 3, :], rows(f_dw_b_2), par_loaded)
            params(prow[0:16 * KT, 4, :], rows(a_dw_w_2[0, 0:16]), par_loaded)
            params(prow[0:15 * KT, 5, :], rows(a_dw_w_2[0, 16:CONV]), par_loaded)
            params(lam_in, bass.AP(diff_lambda.tensor, diff_lambda.offset, [[0, P], [1, 256]]), lam_loaded)

            pre_stats(0)
            for t in range(TT):
                act.wait_ge(rsx_done, t + 1)
                act.activation(xs[:, t, :], xt[:, t, :], ACT.Copy, scale=rsx[:, t:t + 1]).then_inc(xs_ready, 1)
            at = 0
            for bank, g0, g1 in ((1, 1, 4), (2, 4, 6)):
                n = sum(PAR_ROWS[g0:g1])
                act.wait_ge(par_T, g1)
                act.activation(cols[:, at:at + n], Y[:, bank, 0:n], ACT.Copy).then_inc(cols_ready, 1)
                at += n
            for u in (0, 2):
                prep(u, 0)
            def pre_norm(s):
                if s:
                    pre_stats(s)
                act.wait_ge(mod_cols_used, s + 1)
                def scaled(b):
                    act.wait_ge(hT, 4 * s + b + 1)
                    for k in (2 * b, 2 * b + 1):
                        bank = work[:, b, (k % 2) * S:(k % 2 + 1) * S]
                        a = act.activation(bank, bank, ACT.Identity, scale=colA[:, k:k + 1],
                                           bias=colB[:, k:k + 1])
                    a.then_inc(h32a, 1)
                def high(b):
                    act.wait_ge((h32v, h32a)[b % 2], 2 * s + b // 2 + 1)
                    act.activation(h_hi[:, 2 * b:2 * b + 2, :].rearrange("p k n -> p (k n)"), work[:, b, :],
                                   ACT.Copy).then_inc(hhi, 1)
                scaled(1)
                high(0)
                high(1)
                scaled(3)
                high(2)
                high(3)

            def post_norm(s, u, n):
                for t in range(TT):
                    if t == 0:
                        act.wait_ge(y0_done, s + 1)
                    else:
                        act.wait_ge(used[u], n + 1)
                    for f in range(2):
                        b = 2 * t + f
                        if f:
                            act.wait_ge(y_tmp, 4 * s + b)
                        act.activation(xs[:, t, f * 512:(f + 1) * 512], Y[:, b, :], ACT.Square, scale=D ** -0.5,
                                       accum_out=ssy[:, b:b + 1]).then_inc(ssy_done, 1)

            def attention(s):
                hb, rb, nb, nb3 = HEADS[s], ROWS[s], USE[s][0], USE[s][3]
                ne = 2 if s == 0 else 4

                def probs_T(T):
                    act.wait_ge(pT_mm, T + 1)
                    need(act, pv_mm, T)
                    act.activation(pT, work[:, 0, 0:3 * P], ACT.Copy).then_inc(pT_ev, 1)

                def out_hi(i, j):
                    if s == 0:
                        act.wait_ge(pv_mm, i * 2 + (hb + j + 1))
                        src, by = work[:, 3, 0:S], 1.0
                    else:
                        act.wait_ge(oT_mm, i * 2 + (j + 1))
                        src, by = work[:, 1, S:2 * S], subg
                    need(act, used[6 + j], i + nb3)
                    act.activation(a_hi[:, j, :], src, ACT.Copy, scale=by).then_inc(ahi, 1)

                def squares(T):
                    act.wait_ge(ocp, T - hb + 1)
                    for t in range(TT):
                        need(act, oT_mm, T - hb)
                        act.activation(osc[:, t * P:(t + 1) * P], oraw[:, t * P:(t + 1) * P], ACT.Square,
                                       scale=0.125, accum_out=sso[:, t:t + 1]).then_inc(oss, 1)

                def step(i, j, more):
                    T = i * 2 + (hb + j)
                    start = isinstance(i, int) and i == 0
                    first = start and j == 0
                    act.wait_ge(used[j], i + (nb + 1))
                    need(act, s_mm, T)
                    act.activation(qk[:, 0:S], work[:, 0, 0:S], ACT.Copy).then_inc(q_ev, 1)
                    act.wait_ge(used[2 + j], i + (nb + 1))
                    act.activation(qk[:, S:2 * S], work[:, 3, 0:S], ACT.Copy).then_inc(k_ev, 1)
                    if s == 2 and not start:
                        out_hi(i - 1, j)
                    if not first:
                        probs_T(T - 1)
                    if more:
                        prep(j, i + (nb + 1))
                        prep(2 + j, i + (nb + 1))
                    if s == 0 and not first:
                        if j:
                            out_hi(i, 0)
                        else:
                            out_hi(i - 1, 1)
                    act.wait_ge(ng_done, T + 1)
                    for q, (a, b) in enumerate(((0, P), (P, 3 * P))):
                        for g in range(ne // 2):
                            m = q * (ne // 2) + g
                            act.activation(pr[:, g, a:b], pr[:, g, a:b], ACT.Exp, bias=mneg[:, m:m + 1],
                                           accum_out=msum[:, m:m + 1]).then_inc(ex_done, 1)
                    if s == 2 and not first:
                        squares(T - 1)
                    prep(6 + j, i + nb3)
                    if j == 0:
                        act.wait_ge(used[5], i + (nb + 1))
                        need(act, pv_mm, T)
                        act.activation(mix[:, 512:1024], work[:, 1, :], ACT.Copy).then_inc(v_ev, 1)
                    if more:
                        prep(4 + j, i + (nb + 1))

                def both(i, more):
                    step(i, 0, more)
                    step(i, 1, more)

                if s == 2:
                    act.wait_ge(lam_seq, 2)
                    act.activation(lame, lamv, ACT.Exp).then_inc(lam_exp, 1)
                    act.wait_ge(lam_seq, 5)
                sweep(act, 1, NI_A, s, both)
                T = hb + H
                if s == 2:
                    out_hi(NI_A - 1, 0)
                probs_T(T - 1)
                if s == 2:
                    squares(T - 1)
                out_hi(NI_A - 1, 1)

            def gated(s):
                rb, fb, nb, nb2 = ROWS[s], STEPS[s], USE[s][0], USE[s][2]
                gate = gate_of[s]

                def step(i, j, more):
                    start = isinstance(i, int) and i == 0
                    F = i * 2 + (fb + j)
                    if not start:
                        prep(4 + j, i + nb2)
                    act.wait_ge(used[j], i + (nb + 1))
                    if not start:
                        act.wait_ge(act_done, F - 1)
                    if s == 5:
                        act.wait_ge(taps_ready, i * 2 + (3 * KT + j + 1))
                        act.activation(gate[:, j, :], work[:, 2 * j, 0:S], ACT.Identity, scale=taps[:, j, 4:5],
                                       bias=taps[:, j, 6:7]).then_inc(cv_g0, 1)
                        if more:
                            prep(j, i + (nb + 1))
                        act.wait_ge(cv_g, i * 2 + (j + 1))
                        act.activation(gate[:, j, :], gate[:, j, :], ACT.Silu).then_inc(gate_done, 1)
                    else:
                        act.activation(gate[:, j, :], work[:, 2 * j, 0:S], ACT.Silu).then_inc(gate_done, 1)
                        if more:
                            prep(j, i + (nb + 1))
                    if more:
                        prep(2 + j, i + (nb + 1))
                    act.wait_ge(act_done, F + 1)
                    need(act, used[4 + j], i + nb2)
                    act.activation(a_hi[:, j, :], act32[:, j, :], ACT.Copy).then_inc(ahi, 1)

                def both(i, more):
                    step(i, 0, more)
                    step(i, 1, more)

                sweep(act, 1, NI_F, s, both)

            def conformer():
                nb, fb = USE[4][0], STEPS[4]
                gate = gate_of[4]
                for j in range(2):
                    act.wait_ge(used[6 + j], USE[4][3])
                act.wait_ge(cols_ready, 2)
                act.activation(tap_hi.bitcast(F32R), cols[:, ADW:ADW + CONV * KT]
                               .rearrange("p (c t) -> p t c", t=KT), ACT.Copy).then_inc(thi, 1)

                def step(i, j, more):
                    start = isinstance(i, int) and i == 0
                    T = i * 2 + j
                    F = T + fb
                    if more:
                        prep(j, i + (nb + 1))
                    act.wait_ge(used[2 + j], i + (nb + 1))
                    act.wait_ge(taps_ready, i * 6 + (3 * j + 3))
                    if not start:
                        act.wait_ge(act_done, F - 1)
                    act.activation(gate[:, j, :], work[:, 2 * j + 1, 0:S], ACT.Sigmoid,
                                   bias=taps[:, j, 32:33]).then_inc(gate_done, 1)
                    if more:
                        prep(2 + j, i + (nb + 1))
                    act.wait_ge(act_done, F + 1)
                    need(act, diag_used, T * NP - NP)
                    act.activation(u_hi[:, j, :], upad[:, j, :], ACT.Copy).then_inc(uhi, 1)
                    for m in range(NP):
                        if not (start and j == 0):
                            act.wait_ge(diag_used, T * NP + (m + 1 - NP))
                        for w in range(2):
                            d = act.activation(diag[w][:, m, :], ident[:], ACT.Copy,
                                               scale=taps[:, j, 36 + w * NP + m:37 + w * NP + m])
                        d.then_inc(diag_done, 1)

                def both(i, more):
                    step(i, 0, more)
                    step(i, 1, more)

                sweep(act, 1, NI_C, 4, both)
                for h in range(2):
                    act.wait_ge(d_done, h + 1)
                    act.activation(xs[:, h, :].rearrange("p (k n) -> p k n", k=4), convT[:, 4 * h:4 * h + 4, :],
                                   ACT.Square).then_inc(sq_done, 1)
                act.wait_ge(diag_used, KT * NP)
                for j in range(2):
                    prep(6 + j, USE[4][3])
                act.wait_ge(var_mm, 1)
                act.activation(ln_ms, work[:, 0, 0:TT], ACT.Identity, scale=1.0 / D, bias=lneps).then_inc(lms_done, 1)
                for r in range(4):
                    act.wait_ge(z_done, r + 1)
                    for k in (2 * r, 2 * r + 1):
                        a = act.activation(convT[:, k, :], convT[:, k, :], ACT.Silu, scale=cols[:, LNG + k:LNG + k + 1],
                                           bias=cols[:, LNB + k:LNB + k + 1])
                    a.then_inc(ln_act, 1)
                    act.wait_ge(ln_act, r + 1)
                    act.activation(h_hi[:, 2 * r:2 * r + 2, :], convT[:, 2 * r:2 * r + 2, :], ACT.Copy).then_inc(p_hi, 1)
                for p in (2, 3):
                    for j in range(2):
                        prep(2 * p + j, USE[4][p] + 1)

            for s in range(LAST + 1):
                pre_norm(s)
                if s == 0:
                    prep(1, 0)
                    prep(3, 0)
                if s in (0, 2, 4, 5):
                    for j in range(2):
                        prep(4 + j, USE[s][2])
                if s in (0, 2):
                    attention(s)
                    post_norm(s, 7, USE[s][3] + NI_A - 1)
                elif s == 4:
                    conformer()
                    post_norm(s, 7, USE[4][3] + 1)
                else:
                    gated(s)
                    post_norm(s, 5, USE[s][2] + NI_F - 1)

        @block.vector
        def _(dve):
            def prep(u, n):
                dve.wait_ge(hi[u], n + 1)
                dve.tensor_tensor(wlo[:, u, :], raw[:, u, :], whi[:, u, :].bitcast(F32),
                                  ALU.subtract).then_inc(lo[u], 1)

            def gemv_step(layer, b, q):
                k, m = q // 2, b + NBLK * layer
                if q % 2 == 0:
                    dve.wait_ge(ada_ld[k], (m - FIRST // 2) * 16 + 16)
                if q:
                    dve.wait_ge(gemv, m * 8 + q)
                at = acc[:, bass.ds(b * BLK, BLK)]
                ccol = (8 if layer == 2 else 0) + q
                dve.scalar_tensor_tensor(at, ada_raw[:, k, q % 2, :], csil[:, ccol:ccol + 1], at,
                                         ALU.mult, ALU.add).then_inc(gemv, 1)

            def first_step(b, q):
                q0 = 0 if b < FIRST // 2 else 2
                if q % 2 == 0:
                    dve.wait_ge(first_ld(b, q // 2), 16 * (b // 2 + 1))
                if q > q0:
                    dve.wait_ge(gemv, b * 8 + q)
                at = acc[:, b * BLK:(b + 1) * BLK]
                dve.scalar_tensor_tensor(at, first_raw(b, q // 2)[:, q % 2, :], csil[:, q:q + 1], at,
                                         ALU.mult, ALU.add).then_inc(gemv, 1 + q0 if q == q0 else 1)

            def gemv_start(n):
                dve.wait_ge(acc_bias[n - 1], 16)

            def columns(s):
                dve.wait_ge(mod_cols, s + 1)
                dve.wait_ge(cols_ready, 2)
                scale = mod_bank[s][:, KT:2 * KT]
                if s == 0:
                    dve.tensor_copy(first_scale[:], mod_bank[0][:, 2 * KT:3 * KT]).then_inc(scale_done, 1)
                    dve.wait_ge(scale_done, 1)
                    dve.tensor_tensor(first_scale[:], first_scale[:], scale, ALU.add).then_inc(scale_done, 1)
                    dve.wait_ge(scale_done, 2)
                    scale = first_scale[:]
                dve.scalar_tensor_tensor(colA[:], scale, 1.0,
                                         cols[:, NORM + KT * s:NORM + KT * (s + 1)], ALU.add, ALU.mult)
                dve.tensor_copy(colB[:], mod_bank[s][:, 0:KT]).then_inc(mod_cols_used, 1)

            def pre_norm(s):
                if s:
                    for t in range(TT):
                        dve.wait_ge(rsx_done, 2 * s + t + 1)
                        dve.tensor_scalar(xs[:, t, :], xt[:, t, :], rsx[:, t:t + 1], None,
                                          ALU.mult).then_inc(xs_ready, 1)
                dve.wait_ge(mod_cols_used, s + 1)
                for b in (0, 2):
                    dve.wait_ge(hT, 4 * s + b + 1)
                    for k in (2 * b, 2 * b + 1):
                        bank = work[:, b, (k % 2) * S:(k % 2 + 1) * S]
                        v = dve.tensor_scalar(bank, bank, colA[:, k:k + 1], colB[:, k:k + 1], ALU.mult, ALU.add)
                    v.then_inc(h32v, 1)
                for b in range(4):
                    dve.wait_ge(hhi, 4 * s + b + 1)
                    hs = slice(2 * b, 2 * b + 2)
                    dve.tensor_tensor(h_lo[:, hs, :].rearrange("p k n -> p (k n)"), work[:, b, :],
                                      h_hi[:, hs, :].rearrange("p k n -> p (k n)").bitcast(F32),
                                      ALU.subtract).then_inc(hlo, 1)

            gemv_start(1)
            dve.wait_ge(csil_ready, 1)
            for b in range(FIRST):
                for q in range(0 if b < FIRST // 2 else 2, KT):
                    first_step(b, q)
                if b == 1:
                    dve.wait_ge(rel_mm, 1)
                    dve.tensor_tensor(relrow, Y[0:H, 0, 0:REL], relrow, ALU.add).then_inc(rel_row, 1)
            prep(0, 0)

            def gate_a(s):
                dve.wait_ge(mod_ga, s // 2 + 1)
                dve.wait_ge(gain_loaded, 32 * (s // 2 + 1))
                b = GATE_BANK[s]
                dve.tensor_tensor(Ga[:], work[:, b:b + 2, :].rearrange("p a b -> p (a b)"), Ga[:],
                                  ALU.mult).then_inc(mod_ga_used, 1)

            def gate_f(s):
                dve.wait_ge(mod_gf, s // 2 + 1)
                b = GATE_BANK[s]
                dve.tensor_tensor(Gf[:], work[:, b:b + 2, :].rearrange("p a b -> p (a b)"), Gf[:],
                                  ALU.mult).then_inc(mod_gf_used, 1)

            def post_norm(s, u, n):
                G, G_used = (Ga, mod_ga_used) if s % 2 == 0 else (Gf, mod_gf_used)
                dve.wait_ge(G_used, s // 2 + 1)
                for t in range(TT):
                    if t == 0:
                        dve.wait_ge(y0_done, s + 1)
                    else:
                        dve.wait_ge(used[u], n + 1)
                    for f in (1, 0):
                        b, fs = 2 * t + f, slice(f * 512, (f + 1) * 512)
                        if f == 0:
                            dve.wait_ge(ssy_done, 4 * s + b + 1)
                        dve.tensor_tensor(yG[:, t, fs], Y[:, b, :], G[:, fs], ALU.mult).then_inc(y_tmp, 1)
                for t in range(TT):
                    dve.wait_ge(y_tmp, 4 * s + 2 * t + 2)
                    dve.wait_ge(rsy_done, 2 * s + t + 1)
                    if s == 0:
                        dve.wait_ge(x_loaded, 32)
                    dve.scalar_tensor_tensor(xt[:, t, :], yG[:, t, :], rsy[:, t:t + 1], xt[:, t, :], ALU.mult,
                                             ALU.add).then_inc(x_ready, 1)

            def attention(s):
                hb, rb, nb, nb3 = HEADS[s], ROWS[s], USE[s][0], USE[s][3]

                def out_lo(i, j):
                    R = i * 2 + (rb + j)
                    dve.wait_ge(ahi, R + 1)
                    high = a_hi[:, j, :].bitcast(F32)
                    if s == 0:
                        dve.tensor_tensor(a_lo[:, j, :], work[:, 3, 0:S], high, ALU.subtract).then_inc(alo, 1)
                    else:
                        dve.scalar_tensor_tensor(a_lo[:, j, :], work[:, 1, S:2 * S], subg, high, ALU.mult,
                                                 ALU.subtract).then_inc(alo, 1)

                def copy_out(T):
                    dve.wait_ge(pv_mm, T + 1)
                    dve.tensor_copy(oraw, work[:, 1, 0:S]).then_inc(ocp, 1)

                def norm_out(T):
                    for t in range(TT):
                        dve.wait_ge(ors, (T - hb) * 2 + (t + 1))
                        dve.wait_ge(ocp, T - hb + 1)
                        dve.tensor_scalar(osc[:, t * P:(t + 1) * P], oraw[:, t * P:(t + 1) * P],
                                          rso[:, t:t + 1], None, ALU.mult).then_inc(osn, 1)

                def softmax(T, h, between):
                    ng = 1 if s == 0 else 2
                    n1 = (T - hb) * ng + (0 if s == 0 else HEADS[2])
                    dve.wait_ge(s_mm, T + 1)
                    need(dve, pT_mm, T)
                    for g in range(ng):
                        dve.scalar_tensor_tensor(pr[:, g, :], work[:, 2 + g, 0:3 * P], scale_of[s],
                                                 head_bias[:, bass.ds(h, 1), :].rearrange("p a n -> p (a n)"),
                                                 ALU.mult, ALU.add).then_inc(sb_done, 1)
                    dve.wait_ge(sb_done, n1 + ng)
                    for q, (a, b) in enumerate(((0, P), (P, 3 * P))):
                        dve.tensor_reduce(mmax[:, q * ng:(q + 1) * ng], pr[:, 0:ng, a:b], AX.X,
                                          ALU.max).then_inc(mx_done, 1)
                    dve.wait_ge(mx_done, T * 2 + 2)
                    dve.tensor_scalar(mneg[:, 0:2 * ng], mmax[:, 0:2 * ng], -1.0, None,
                                      ALU.mult).then_inc(ng_done, 1)
                    between()
                    n2 = (T - hb) * (2 * ng) + (0 if s == 0 else 2 * HEADS[2])
                    dve.wait_ge(ex_done, n2 + 2 * ng)
                    dve.reciprocal(mrec[:, 0:2 * ng], msum[:, 0:2 * ng]).then_inc(rc_done, 1)
                    dve.wait_ge(rc_done, T + 1)
                    if s == 0:
                        for q, (a, b) in enumerate(((0, P), (P, 3 * P))):
                            dve.tensor_scalar(pr[:, 0, a:b], pr[:, 0, a:b], mrec[:, q:q + 1], None,
                                              ALU.mult).then_inc(p_done, 1)
                        return
                    n3 = (T - hb) * 3
                    dve.tensor_scalar(lrec, mrec.rearrange("p (q g) -> p q g", g=2)[:, :, 1], lamf[:, 0:1], None,
                                      ALU.mult).then_inc(dif_seq, 1)
                    dve.wait_ge(dif_seq, n3 + 1)
                    for q, (a, b) in enumerate(((0, P), (P, 3 * P))):
                        dve.tensor_scalar(pr[:, 1, a:b], pr[:, 1, a:b], lrec[:, q:q + 1], None,
                                          ALU.mult).then_inc(dif_seq, 1)
                    for q, (a, b) in enumerate(((0, P), (P, 3 * P))):
                        dve.wait_ge(dif_seq, n3 + 2 + q)
                        dve.scalar_tensor_tensor(pr[:, 0, a:b], pr[:, 0, a:b], mrec[:, 2 * q:2 * q + 1],
                                                 pr[:, 1, a:b], ALU.mult, ALU.subtract).then_inc(p_done, 1)

                def step(i, j, more):
                    T = i * 2 + (hb + j)
                    start = isinstance(i, int) and i == 0
                    first = start and j == 0

                    def sums(q0, q1):
                        if s == 0 and not start:
                            for q in range(q0, q1):
                                gemv_step(0, i * 2 + (2 + j), q)
                        elif s == 2 and first:
                            for q in range(q0, q1):
                                gemv_step(1, NBLK - 3, q)

                    if s == 0:
                        sums(0, 4)
                    if s == 2 and not start:
                        out_lo(i - 1, j)

                    def between():
                        if s == 2 and not first:
                            copy_out(T - 1)
                        elif s == 0 and j:
                            out_lo(i, 0)
                        elif s == 0 and not first:
                            out_lo(i - 1, 1)
                        if more:
                            prep(j, i + (nb + 1))
                            prep(2 + j, i + (nb + 1))

                    softmax(T, i * 2 + j, between)
                    if s == 2 and not first:
                        norm_out(T - 1)
                    prep(6 + j, i + nb3)
                    sums(4 if s == 0 else 0, 8)
                    if more:
                        prep(4 + j, i + (nb + 1))

                def both(i, more):
                    step(i, 0, more)
                    step(i, 1, more)

                sweep(dve, 1, NI_A, s, both)
                T = hb + H
                if s == 2:
                    out_lo(NI_A - 1, 0)
                gate_a(s)
                if s == 2:
                    copy_out(T - 1)
                    norm_out(T - 1)
                out_lo(NI_A - 1, 1)

            def lam_and_gain():
                dve.wait_ge(lam_loaded, 16)
                lam = lam_in.rearrange("p (a b n) -> p a b n", a=2, b=2)
                dve.tensor_tensor(lam_pr.rearrange("p (a n) -> p a n", a=2), lam[:, :, 0, :], lam[:, :, 1, :],
                                  ALU.mult).then_inc(lam_seq, 1)
                dve.wait_ge(lam_seq, 1)
                dve.tensor_reduce(lamv, lam_pr.rearrange("p (a n) -> p a n", a=2), AX.X, ALU.add).then_inc(lam_seq, 1)
                dve.wait_ge(lam_exp, 1)
                dve.tensor_tensor(lamf[:, 1:2], lame[:, 0:1], lame[:, 1:2], ALU.subtract).then_inc(lam_seq, 1)
                dve.wait_ge(lam_seq, 3)
                dve.tensor_scalar(lamf[:, 0:1], lamf[:, 1:2], LAMBDA_INIT, None, ALU.add).then_inc(lam_seq, 1)
                dve.tensor_scalar(subg, cols[:, SUB:SUB + 1], (1.0 - LAMBDA_INIT) * 2 ** 0.5, None, ALU.mult).then_inc(lam_seq, 1)
                dve.wait_ge(lam_seq, 5)

            def gated(s):
                rb, fb, nb, nb2 = ROWS[s], STEPS[s], USE[s][0], USE[s][2]
                gate = gate_of[s]
                fdw = cols[:, FDW:FDW + 8 * FT].rearrange("p (a g t) -> p a g t", a=4, g=2)

                def step(i, j, more):
                    start = isinstance(i, int) and i == 0
                    t1 = i * 2 + (j + 1)
                    F = i * 2 + (fb + j)

                    def sums(q):
                        if s == 5:
                            if isinstance(i, int) and i < 4 and q % 2 == 0:
                                gemv_step(2, NBLK - 2 + i // 2, i % 2 * 4 + 2 * j + q // 2)
                        elif isinstance(i, int) and i < 2:
                            gemv_step(s // 2, NBLK - 2 + i, 4 * j + q)
                        else:
                            gemv_step(s // 2 + 1, i - 2, 4 * j + q)

                    if s == 5:
                        dve.tensor_scalar(taps[:, j, 0:8].rearrange("p (a g t) -> p a g t", a=4, g=2),
                                          fdw[:, :, :, bass.ds(i * 2 + j, 1)], 1.0, None,
                                          ALU.mult).then_inc(taps_ready, 1)
                    sums(0)
                    if not start:
                        prep(4 + j, i + nb2)
                    sums(1)
                    if s == 5:
                        g, u = work[:, 2 * j, :], work[:, 2 * j + 1, :]
                        gt, ut = gate[:, j, :], act32[:, j, :]
                        dve.wait_ge(taps_ready, t1 + 3 * KT)
                        dve.wait_ge(cv_g0, t1)
                        dve.scalar_tensor_tensor(gt[:, 1:S], g[:, 0:S - 1], taps[:, j, 2:3], gt[:, 1:S],
                                                 ALU.mult, ALU.add).then_inc(cv_seq, 1)
                        if more:
                            prep(j, i + (nb + 1))
                        n = i * 6 + 3 * j
                        dve.wait_ge(cv_seq, n + 1)
                        dve.scalar_tensor_tensor(gt[:, 2:S], g[:, 0:S - 2], taps[:, j, 0:1], gt[:, 2:S],
                                                 ALU.mult, ALU.add).then_inc(cv_g, 1)
                        dve.wait_ge(used[2 + j], i + (nb + 1))
                        dve.tensor_scalar(ut, u[:, 0:S], taps[:, j, 5:6], taps[:, j, 7:8], ALU.mult,
                                          ALU.add).then_inc(cv_seq, 1)
                        dve.wait_ge(cv_seq, n + 2)
                        dve.scalar_tensor_tensor(ut[:, 1:S], u[:, 0:S - 1], taps[:, j, 3:4], ut[:, 1:S],
                                                 ALU.mult, ALU.add).then_inc(cv_seq, 1)
                        dve.wait_ge(cv_seq, n + 3)
                        dve.scalar_tensor_tensor(ut[:, 2:S], u[:, 0:S - 2], taps[:, j, 1:2], ut[:, 2:S],
                                                 ALU.mult, ALU.add).then_inc(cv_u, 1)
                        dve.wait_ge(cv_u, t1)
                        dve.wait_ge(gate_done, F + 1)
                        dve.tensor_tensor(ut, ut, gt, ALU.mult).then_inc(act_done, 1)
                        if more:
                            prep(2 + j, i + (nb + 1))
                        sums(2)
                        sums(3)
                    else:
                        if more:
                            prep(j, i + (nb + 1))
                        sums(2)
                        dve.wait_ge(used[2 + j], i + (nb + 1))
                        dve.wait_ge(gate_done, F + 1)
                        dve.tensor_tensor(act32[:, j, :], work[:, 2 * j + 1, 0:S], gate[:, j, :],
                                          ALU.mult).then_inc(act_done, 1)
                        if more:
                            prep(2 + j, i + (nb + 1))
                        sums(3)
                    dve.wait_ge(ahi, i * 2 + (rb + j + 1))
                    dve.wait_ge(act_done, F + 1)
                    dve.tensor_tensor(a_lo[:, j, :], act32[:, j, :], a_hi[:, j, :].bitcast(F32),
                                      ALU.subtract).then_inc(alo, 1)

                def both(i, more):
                    if isinstance(i, int) and i == 1 and s < 5:
                        gemv_start(s + 2)
                    step(i, 0, more)
                    step(i, 1, more)

                gemv_start(s + 1)
                sweep(dve, 4 if s == 5 else 2, NI_F, s, both)
                gate_f(s)

            def conformer():
                nb, fb = USE[4][0], STEPS[4]
                gate = gate_of[4]
                adw = cols[:, ADW:ADW + CONV * KT].rearrange("p (c t) -> p c t", t=KT)
                bias = cols[:, PW1B:PW1B + 3 * KT].rearrange("p (c t) -> p c t", t=KT)
                dve.wait_ge(thi, 1)
                dve.tensor_tensor(tap_lo, adw.rearrange("p c t -> p t c"), tap_hi, ALU.subtract).then_inc(tlo, 1)
                dve.memset(upad[:, :, 0:CONV - 1], 0.0).then_inc(pad_zero, 1)
                dve.wait_ge(tlo, 1)
                dve.wait_ge(pad_zero, 1)

                def combine(i, j):
                    T = i * 2 + j
                    dve.wait_ge(diag_used, T * NP + NP)
                    dve.wait_ge(part_done, T + 1)
                    dve.tensor_tensor(convT[:, bass.ds(T, 1), :].rearrange("p a n -> p (a n)"),
                                      Y[:, j, 0:S], part[:, j, :], ALU.add).then_inc(conv_done, 1)

                def step(i, j, more):
                    start = isinstance(i, int) and i == 0
                    T = i * 2 + j
                    F = T + fb
                    dve.tensor_scalar(taps[:, j, 0:CONV].rearrange("p (c t) -> p c t", t=1),
                                      adw[:, :, bass.ds(T, 1)], 1.0, None, ALU.mult).then_inc(taps_ready, 1)
                    dve.tensor_scalar(taps[:, j, CONV:CONV + 3].rearrange("p (c t) -> p c t", t=1),
                                      bias[:, :, bass.ds(T, 1)], 1.0, None, ALU.mult).then_inc(taps_ready, 1)
                    need(dve, diag_done, T * NP - NP)
                    dve.tensor_scalar(taps[:, j, 36:36 + 2 * NP].rearrange("p (t w c) -> p t w c", t=1, w=2),
                                      tap_parts[:, bass.ds(T, 1), :, :], 1.0, None, ALU.mult).then_inc(taps_ready, 1)
                    if more:
                        prep(j, i + (nb + 1))
                    dve.wait_ge(taps_ready, i * 6 + (3 * j + 3))
                    dve.wait_ge(gate_done, F + 1)
                    u = upad[:, j, :]
                    dve.scalar_tensor_tensor(u[:, CONV - 1:PADW], work[:, 2 * j, 0:S], taps[:, j, 31:32],
                                             gate[:, j, :], ALU.add, ALU.mult).then_inc(act_done, 1)
                    if more:
                        prep(2 + j, i + (nb + 1))
                    dve.wait_ge(act_done, F + 1)
                    dve.wait_ge(uhi, T + 1)
                    dve.tensor_tensor(u_lo[:, j, :], u, u_hi[:, j, :].bitcast(F32), ALU.subtract).then_inc(ulo, 1)
                    n = T * (CONV - NP)
                    for c, m in enumerate(range(NP, CONV)):
                        w = taps[:, j, m:m + 1]
                        sums = cacc[:, c % 2, :]
                        if c == 0:
                            v = dve.tensor_scalar(sums, u[:, m:m + S], w, taps[:, j, 33:34], ALU.mult, ALU.add)
                        elif c == 1:
                            v = dve.tensor_scalar(sums, u[:, m:m + S], w, None, ALU.mult)
                        else:
                            dve.wait_ge(tap_seq, n + (c - 1))
                            v = dve.scalar_tensor_tensor(sums, u[:, m:m + S], w, sums, ALU.mult, ALU.add)
                        v.then_inc(tap_seq, 1)
                    if j:
                        combine(i, 0)
                    elif not start:
                        combine(i - 1, 1)
                    dve.wait_ge(tap_seq, n + (CONV - NP))
                    dve.tensor_tensor(part[:, j, :], cacc[:, 0, :], cacc[:, 1, :], ALU.add).then_inc(part_done, 1)

                def both(i, more):
                    step(i, 0, more)
                    step(i, 1, more)

                sweep(dve, 1, NI_C, 4, both)
                combine(NI_C - 1, 1)
                dve.wait_ge(mean_mm, 1)
                for h in range(2):
                    half = convT[:, 4 * h:4 * h + 4, :]
                    dve.scalar_tensor_tensor(half, Y[:, 2, 0:S].unsqueeze(1).broadcast_to([P, 4, S]), -1.0 / D, half,
                                             ALU.mult, ALU.add).then_inc(d_done, 1)
                dve.wait_ge(sq_done, 2)
                dve.tensor_tensor(xs[:, 0, :], xs[:, 0, :], xs[:, 1, :], ALU.add).then_inc(fold_done, 1)
                dve.wait_ge(fold_done, 1)
                dve.tensor_tensor(xs[:, 0, 0:2 * S], xs[:, 0, 0:2 * S], xs[:, 0, 2 * S:4 * S],
                                  ALU.add).then_inc(fold_done, 1)
                dve.wait_ge(lrs_done, 1)
                for t in range(TT):
                    d = dve.tensor_scalar(ln_diag[:, t, :], ident[:], ln_rs[:, t:t + 1], None, ALU.mult)
                    d.then_inc(ln_dg, 1)
                dve.wait_ge(lrs_mm, 1)
                for r in range(4):
                    pair = convT[:, 2 * r:2 * r + 2, :]
                    dve.tensor_tensor(pair, pair, work[:, 1, 0:S].unsqueeze(1).broadcast_to([P, 2, S]),
                                      ALU.mult).then_inc(z_done, 1)
                for r in range(4):
                    hs = slice(2 * r, 2 * r + 2)
                    dve.wait_ge(p_hi, r + 1)
                    dve.tensor_tensor(h_lo[:, hs, :], convT[:, hs, :], h_hi[:, hs, :].bitcast(F32),
                                      ALU.subtract).then_inc(p_lo, 1)
                    if r < 2:
                        prep(6 + r, USE[4][3])
                gate_a(4)
                for p in (2, 3):
                    for j in range(2):
                        prep(2 * p + j, USE[4][p] + 1)
                for q in range(KT):
                    gemv_step(2, NBLK - 3, q)

            for s in range(LAST + 1):
                columns(s)
                pre_norm(s)
                if s == 0:
                    for u in (2, 1, 3):
                        prep(u, 0)
                if s in (0, 2, 4, 5):
                    for j in range(2):
                        prep(4 + j, USE[s][2])
                if s in (0, 2):
                    if s == 0:
                        dve.wait_ge(bias_loaded, 32)
                        gemv_start(2)
                    else:
                        lam_and_gain()
                    attention(s)
                    post_norm(s, 7, USE[s][3] + NI_A - 1)
                elif s == 4:
                    conformer()
                    post_norm(s, 7, USE[4][3] + 1)
                else:
                    gated(s)
                    post_norm(s, 5, USE[s][2] + NI_F - 1)


def relative_constants():
    import math

    import numpy as np

    buckets, exact, far = 32, 16, 2048
    rel = (S - 1) - np.arange(REL)
    n = np.maximum(rel, 0)
    nf = np.maximum(n, 1).astype(np.float32)
    large = exact + (np.log(nf / np.float32(exact)) / np.float32(math.log(far / exact))
                     * np.float32(buckets - exact)).astype(np.int32)
    bucket = np.where(n < exact, n, np.minimum(large, buckets - 1))
    onehot = ((np.arange(buckets)[:, None] == bucket[None, :]) & (rel >= 0)).astype(np.float32)
    fill = np.broadcast_to(np.where(rel >= 0, 0.0, -1e30).astype(np.float32), (H, REL))
    return np.ascontiguousarray(onehot), np.ascontiguousarray(fill)


_INS = ["x", "c", "rel_bias", "ada_w", "ada_b", "norm_g", "moba_w_qkv", "moba_w_o", "diff_w_qkv",
        "diff_w_o", "diff_lambda", "diff_subln_g", "ffn_w_in", "ffn_w_out", "c_2", "mod_w_2", "mod_b_2",
        "norm_pre_mix_2", "norm_post_mix_2", "norm_pre_ffn_2", "norm_post_ffn_2", "a_pw1_w_2",
        "a_pw1_b_2", "a_dw_w_2", "a_dw_b_2", "a_ln_g_2", "a_ln_b_2", "a_pw2_w_2", "a_pw2_b_2",
        "f_up_w_2", "f_dw_w_2", "f_dw_b_2", "f_down_w_2"]


def kernel(**inputs):
    import numpy as np
    import concourse.bacc as bacc
    from concourse.bass_utils import run_bass_kernel_spmd

    nc = bacc.Bacc("TRN2", target_bir_lowering=False, num_devices=1)
    arrays, args = {}, []
    given = {name: np.ascontiguousarray(inputs[name]) for name in _INS}
    given["bucket_onehot"], given["causal_fill"] = relative_constants()
    for name, a in given.items():
        arrays[f"in_{name}"] = a
        args.append(nc.dram_tensor(f"in_{name}", a.shape, mybir.dt.from_np(a.dtype), kind="ExternalInput").ap())
    out = nc.dram_tensor("out", (1, S, D), F32, kind="ExternalOutput").ap()
    build(nc, *args, out)
    r = run_bass_kernel_spmd(nc, [arrays], core_ids=[0])
    return r.results[0]["out"]
```
